# Optimizing a Trainium2 kernel written in Bass

```python
import jax, jax.numpy as jnp
from jax import lax
import numpy as np
import math

D_MODEL = 1024
BATCH = 1
SEQ = 256
DEPTH = 1

MIX_WIDTH = 256
CONV_K = 3
GMLP_GROUPS = 4
GMLP_CHUNK = 128
HEAD_DIM = 64
SB_HEADS = MIX_WIDTH // HEAD_DIM
FOX_HEADS = MIX_WIDTH // HEAD_DIM
Q_BLOCK = 128
N_BRANCH = 4
FFN_HIDDEN = -(-8 * D_MODEL // (3 * 256)) * 256
EPS = 1e-6
IN_SPLIT_SIZES = (MIX_WIDTH, MIX_WIDTH, MIX_WIDTH, 2 * MIX_WIDTH, MIX_WIDTH, MIX_WIDTH, MIX_WIDTH,
                  MIX_WIDTH, MIX_WIDTH, MIX_WIDTH, FOX_HEADS, N_BRANCH * D_MODEL)
N_IN = sum(IN_SPLIT_SIZES)


def _rms_norm(x, g):
    xf = x.astype(jnp.float32)
    y = xf * lax.rsqrt(jnp.mean(xf * xf, axis=-1, keepdims=True) + EPS)
    return (y * g.astype(jnp.float32)).astype(x.dtype)

def _layer_norm(x, g, b):
    xf = x.astype(jnp.float32)
    mu = jnp.mean(xf, axis=-1, keepdims=True)
    var = jnp.mean(jnp.square(xf - mu), axis=-1, keepdims=True)
    y = (xf - mu) * lax.rsqrt(var + EPS)
    return (y * g.astype(jnp.float32) + b.astype(jnp.float32)).astype(x.dtype)

def _split_heads(t, n_heads):
    b, s, _ = t.shape
    return t.reshape(b, s, n_heads, HEAD_DIM).transpose(0, 2, 1, 3)

def _merge_heads(t):
    b, h, s, d = t.shape
    return t.transpose(0, 2, 1, 3).reshape(b, s, h * d)

def _short_conv_mixer(b_gate, c_gate, xt, w_conv):
    xc = c_gate * xt
    y = lax.conv_general_dilated(
        xc, w_conv[:, None, :].astype(xc.dtype), window_strides=(1,),
        padding=[(CONV_K - 1, 0)], dimension_numbers=('NWC', 'WIO', 'NWC'),
        feature_group_count=MIX_WIDTH)
    return b_gate * y

def _spatial_gating_mixer(uv, w_s, b_s, ln_g, ln_b):
    u, v = jnp.split(jax.nn.gelu(uv), 2, axis=-1)
    v = _layer_norm(v, ln_g, ln_b)
    bsz, s, _ = v.shape
    v = v.reshape(bsz, s // GMLP_CHUNK, GMLP_CHUNK, GMLP_GROUPS, MIX_WIDTH // GMLP_GROUPS)
    w_causal = jnp.tril(w_s).astype(v.dtype)
    mixed = jnp.einsum('gts,bcsge->bctge', w_causal, v) + b_s.T[None, None, :, :, None].astype(v.dtype)
    return u * mixed.reshape(bsz, s, MIX_WIDTH)

def _stick_breaking_attention(q, k, v):
    seq = q.shape[2]
    scale = HEAD_DIM ** -0.5
    outs = []
    for i in range(seq // Q_BLOCK):
        start, end = i * Q_BLOCK, (i + 1) * Q_BLOCK
        z = jnp.einsum('bhqd,bhkd->bhqk', q[:, :, start:end], k[:, :, :end]).astype(jnp.float32) * scale
        q_pos = start + jnp.arange(Q_BLOCK)[:, None]
        k_pos = jnp.arange(end)[None, :]
        strict = k_pos < q_pos
        log_1m_beta = jnp.where(strict, jax.nn.log_sigmoid(-z), 0.0)
        later = lax.cumsum(log_1m_beta, axis=3, reverse=True) - log_1m_beta
        w = jnp.where(strict, jnp.exp(jax.nn.log_sigmoid(z) + later), 0.0)
        outs.append(jnp.einsum('bhqk,bhkd->bhqd', w.astype(v.dtype), v[:, :, :end]))
    return jnp.concatenate(outs, axis=2)

def _forgetting_attention(q, k, v, log_f_cum):
    seq = q.shape[2]
    scale = HEAD_DIM ** -0.5
    neg = jnp.finfo(jnp.float32).min
    outs = []
    for i in range(seq // Q_BLOCK):
        start, end = i * Q_BLOCK, (i + 1) * Q_BLOCK
        logits = jnp.einsum('bhqd,bhkd->bhqk', q[:, :, start:end], k[:, :, :end]).astype(jnp.float32) * scale
        logits = logits + log_f_cum[:, :, start:end, None] - log_f_cum[:, :, None, :end]
        causal = jnp.arange(end)[None, :] <= (start + jnp.arange(Q_BLOCK)[:, None])
        p = jax.nn.softmax(jnp.where(causal, logits, neg), axis=-1)
        outs.append(jnp.einsum('bhqk,bhkd->bhqd', p.astype(v.dtype), v[:, :, :end]))
    return jnp.concatenate(outs, axis=2)

def _mixer_block(xn, w_in, w_conv, w_s, b_s, ln_g, ln_b, q_norm_g, k_norm_g, b_f, w_branch, w_out):
    bsz, s, _ = xn.shape
    proj = xn @ w_in
    idx, acc = [], 0
    for size in IN_SPLIT_SIZES[:-1]:
        acc += size
        idx.append(acc)
    (cb, cc, cx, uv, sb_q, sb_k, sb_v, fx_q, fx_k, fx_v, f_raw, gate_raw) = jnp.split(proj, idx, axis=-1)

    y_a = _short_conv_mixer(cb, cc, cx, w_conv)
    y_b = _spatial_gating_mixer(uv, w_s, b_s, ln_g, ln_b)
    y_c = _merge_heads(_stick_breaking_attention(
        _split_heads(sb_q, SB_HEADS), _split_heads(sb_k, SB_HEADS), _split_heads(sb_v, SB_HEADS)))
    fq = _rms_norm(_split_heads(fx_q, FOX_HEADS), q_norm_g)
    fk = _rms_norm(_split_heads(fx_k, FOX_HEADS), k_norm_g)
    log_f = jax.nn.log_sigmoid((f_raw + b_f).astype(jnp.float32)).transpose(0, 2, 1)
    y_d = _merge_heads(_forgetting_attention(fq, fk, _split_heads(fx_v, FOX_HEADS), lax.cumsum(log_f, axis=2)))

    ys = jnp.stack([y_a, y_b, y_c, y_d], axis=2)
    branches = jnp.einsum('bsnc,ncd->bsnd', ys, w_branch)
    gates = jax.nn.sigmoid(gate_raw.reshape(bsz, s, N_BRANCH, D_MODEL).astype(jnp.float32)).astype(xn.dtype)
    merged = jnp.sum(gates * branches, axis=2)
    return merged @ w_out

def _swiglu(x, w_in, w_out):
    g, u = jnp.split(x @ w_in, 2, axis=-1)
    return (jax.nn.silu(g) * u) @ w_out

def first_inputs(seed: int = 0) -> dict:
    key = jax.random.key(seed)
    ks = jax.random.split(key, 16)
    f32 = jnp.float32
    nrm = lambda k, shape: jax.random.normal(k, shape, f32)
    return {
        'x': nrm(ks[0], (BATCH, SEQ, D_MODEL)),
        'norm_mix_g': 1.0 + 0.05 * nrm(ks[1], (DEPTH, D_MODEL)),
        'w_in': nrm(ks[2], (DEPTH, D_MODEL, N_IN)) * D_MODEL ** -0.5,
        'w_conv': nrm(ks[3], (DEPTH, CONV_K, MIX_WIDTH)) * CONV_K ** -0.5,
        'w_spatial': nrm(ks[4], (DEPTH, GMLP_GROUPS, GMLP_CHUNK, GMLP_CHUNK)) * GMLP_CHUNK ** -0.5,
        'b_spatial': 1.0 + 0.1 * nrm(ks[5], (DEPTH, GMLP_GROUPS, GMLP_CHUNK)),
        'gmlp_ln_g': 1.0 + 0.05 * nrm(ks[6], (DEPTH, MIX_WIDTH)),
        'gmlp_ln_b': 0.02 * nrm(ks[7], (DEPTH, MIX_WIDTH)),
        'fox_q_norm_g': 1.0 + 0.05 * nrm(ks[8], (DEPTH, HEAD_DIM)),
        'fox_k_norm_g': 1.0 + 0.05 * nrm(ks[9], (DEPTH, HEAD_DIM)),
        'fox_forget_b': 2.0 + 0.5 * nrm(ks[10], (DEPTH, FOX_HEADS)),
        'w_branch': nrm(ks[11], (DEPTH, N_BRANCH, MIX_WIDTH, D_MODEL)) * MIX_WIDTH ** -0.5,
        'w_out': nrm(ks[12], (DEPTH, D_MODEL, D_MODEL)) * D_MODEL ** -0.5,
        'norm_ffn_g': 1.0 + 0.05 * nrm(ks[13], (DEPTH, D_MODEL)),
        'w_ffn_in': nrm(ks[14], (DEPTH, D_MODEL, 2 * FFN_HIDDEN)) * D_MODEL ** -0.5,
        'w_ffn_out': nrm(ks[15], (DEPTH, FFN_HIDDEN, D_MODEL)) * FFN_HIDDEN ** -0.5,
    }

def first_block(x, norm_mix_g, w_in, w_conv, w_spatial, b_spatial, gmlp_ln_g, gmlp_ln_b,
              fox_q_norm_g, fox_k_norm_g, fox_forget_b, w_branch, w_out, norm_ffn_g,
              w_ffn_in, w_ffn_out):
    h = x
    for l in range(DEPTH):
        xn = _rms_norm(h, norm_mix_g[l])
        h = h + _mixer_block(xn, w_in[l], w_conv[l], w_spatial[l], b_spatial[l], gmlp_ln_g[l],
                             gmlp_ln_b[l], fox_q_norm_g[l], fox_k_norm_g[l], fox_forget_b[l],
                             w_branch[l], w_out[l])
        h = h + _swiglu(_rms_norm(h, norm_ffn_g[l]), w_ffn_in[l], w_ffn_out[l])
    return h


GRID_W = 64
CTX_LEN = 256
N_HEADS = 8
HEAD_DIM_2 = D_MODEL // 16
QK_W = N_HEADS * 2 * HEAD_DIM_2
V_W = N_HEADS * 2 * HEAD_DIM_2
ATTN_SCALE = HEAD_DIM_2 ** -0.5
ROT_FREQS = HEAD_DIM_2 // 4
ROPE_BASE = 10000.0
LAMBDA_STD = 0.1
F_GROUPS = 4
F_GROUP_DIM = D_MODEL // 8
F_W = F_GROUPS * F_GROUP_DIM
Q_OFF = 0
K_OFF = Q_OFF + QK_W
V_OFF = K_OFF + QK_W
F_OFF = V_OFF + V_W
GA_OFF = F_OFF + F_W
GF_OFF = GA_OFF + D_MODEL
PROJ_W = GF_OFF + D_MODEL
N_GROUPS = 4
EXPERTS_PER_GROUP = 4
N_EXPERTS = N_GROUPS * EXPERTS_PER_GROUP
TOP_K_IN_GROUP = 2
EXPERT_HIDDEN = D_MODEL // 2


def rmsnorm(x, g):
    x32 = x.astype(jnp.float32)
    y = x32 * lax.rsqrt(jnp.mean(x32 * x32, axis=-1, keepdims=True) + EPS)
    return (y * g.astype(jnp.float32)).astype(x.dtype)

def modulate(h, shift, scale):
    return h * (1 + scale) + shift

def axial_angles(rows):
    inv = 1.0 / (ROPE_BASE ** (jnp.arange(ROT_FREQS, dtype=jnp.float32) / ROT_FREQS))
    row = jnp.broadcast_to(jnp.arange(rows, dtype=jnp.float32)[:, None], (rows, GRID_W)).reshape(-1)
    col = jnp.broadcast_to(jnp.arange(GRID_W, dtype=jnp.float32)[None, :], (rows, GRID_W)).reshape(-1)
    return row[:, None] * inv[None, :], col[:, None] * inv[None, :]

def rotate(x, ang):
    cos = jnp.cos(ang)[:, None, None, :].astype(x.dtype)
    sin = jnp.sin(ang)[:, None, None, :].astype(x.dtype)
    x1, x2 = x[..., :ROT_FREQS], x[..., ROT_FREQS:]
    return jnp.concatenate([x1 * cos - x2 * sin, x2 * cos + x1 * sin], axis=-1)

def axial_rope(x, ang_row, ang_col):
    half = 2 * ROT_FREQS
    return jnp.concatenate([rotate(x[..., :half], ang_row), rotate(x[..., half:], ang_col)], axis=-1)

def split_proj(p):
    b, n = p.shape[:2]
    q = p[..., Q_OFF:K_OFF].reshape(b, n, N_HEADS, 2, HEAD_DIM_2)
    k = p[..., K_OFF:V_OFF].reshape(b, n, N_HEADS, 2, HEAD_DIM_2)
    v = p[..., V_OFF:F_OFF].reshape(b, n, N_HEADS, 2 * HEAD_DIM_2)
    f = p[..., F_OFF:GA_OFF]
    ga = p[..., GA_OFF:GF_OFF]
    gf = p[..., GF_OFF:PROJ_W]
    return q, k, v, f, ga, gf

def diff_attend(q, k, v, lam):
    s = jnp.einsum('bqhid,bkhid->bhiqk', q, k, preferred_element_type=jnp.float32) * ATTN_SCALE
    p = jax.nn.softmax(s, axis=-1)
    a = p[:, :, 0] - lam * p[:, :, 1]
    return jnp.einsum('bhqk,bkhe->bqhe', a.astype(v.dtype), v)

def blocked_latent_attention(q, k_all, v_all, lam):
    b, n = q.shape[:2]
    qb = q.reshape(b, n // Q_BLOCK, Q_BLOCK, N_HEADS, 2, HEAD_DIM_2).transpose(1, 0, 2, 3, 4, 5)
    out = lax.map(lambda qblk: diff_attend(qblk, k_all, v_all, lam), qb)
    return out.transpose(1, 0, 2, 3, 4).reshape(b, n, N_HEADS, 2 * HEAD_DIM_2)

def merge_branches(heads, f, ga, gf, subln_g, lam_init, w_ao, w_fo, w_o):
    b, n = heads.shape[:2]
    attn = (rmsnorm(heads, subln_g) * (1.0 - lam_init)).reshape(b, n, V_W)
    fg = f.reshape(b, n, F_GROUPS, F_GROUP_DIM).astype(jnp.float32)
    four = jnp.fft.fftn(fg, axes=(1, 3), norm='ortho').real.astype(f.dtype).reshape(b, n, F_W)
    y = jax.nn.sigmoid(ga) * (attn @ w_ao) + jax.nn.sigmoid(gf) * (four @ w_fo)
    return y @ w_o

def hier_moe(h, w_rg, b_rg, w_re, b_re, w1, w3, w2):
    b, n, d = h.shape
    t = h.reshape(-1, d)
    lg = (t @ w_rg + b_rg).astype(jnp.float32)
    g_sel = jnp.argmax(lg, axis=-1)
    w_grp = jnp.take_along_axis(jax.nn.softmax(lg, axis=-1), g_sel[:, None], axis=-1)
    le = (t @ w_re + b_re).astype(jnp.float32).reshape(-1, N_GROUPS, EXPERTS_PER_GROUP)
    le_g = jnp.take_along_axis(le, g_sel[:, None, None], axis=1)[:, 0]
    top_v, top_i = lax.top_k(le_g, TOP_K_IN_GROUP)
    w_top = jax.nn.softmax(top_v, axis=-1) * w_grp
    eid = g_sel[:, None] * EXPERTS_PER_GROUP + top_i
    gates = jnp.einsum('tk,tke->et', w_top, jax.nn.one_hot(eid, N_EXPERTS, dtype=jnp.float32)).astype(t.dtype)

    def expert_step(acc, xs):
        w1e, w3e, w2e, ge = xs
        y = (jax.nn.silu(t @ w1e) * (t @ w3e)) @ w2e
        return acc + ge[:, None] * y, None

    acc, _ = lax.scan(expert_step, jnp.zeros_like(t), (w1, w3, w2, gates))
    return acc.reshape(b, n, d)

def second_inputs(seed: int = 0) -> dict:
    key = jax.random.key(seed)
    ks = jax.random.split(key, 32)
    f32 = jnp.float32
    d = D_MODEL

    def nrm(k, shape, scale):
        return jax.random.normal(k, shape, f32) * scale

    return {
        'x': nrm(ks[0], (BATCH, SEQ, d), 1.0),
        'c': nrm(ks[1], (BATCH, d), 1.0),
        'ctx': nrm(ks[2], (BATCH, CTX_LEN, d), 1.0),
        'c_ctx': nrm(ks[3], (d,), 1.0),
        'w_mod': nrm(ks[4], (DEPTH, d, 6 * d), 0.5 * d ** -0.5),
        'b_mod': nrm(ks[5], (DEPTH, 6 * d), 0.02),
        'norm1_g': 1.0 + nrm(ks[6], (DEPTH, d), 0.02),
        'norm2_g': 1.0 + nrm(ks[7], (DEPTH, d), 0.02),
        'w_in': nrm(ks[8], (DEPTH, d, PROJ_W), d ** -0.5),
        'lam_q1': nrm(ks[9], (DEPTH, HEAD_DIM_2), LAMBDA_STD),
        'lam_k1': nrm(ks[10], (DEPTH, HEAD_DIM_2), LAMBDA_STD),
        'lam_q2': nrm(ks[11], (DEPTH, HEAD_DIM_2), LAMBDA_STD),
        'lam_k2': nrm(ks[12], (DEPTH, HEAD_DIM_2), LAMBDA_STD),
        'subln_g': 1.0 + nrm(ks[13], (DEPTH, 2 * HEAD_DIM_2), 0.02),
        'w_attn_out': nrm(ks[14], (DEPTH, V_W, d), V_W ** -0.5),
        'w_four_out': nrm(ks[15], (DEPTH, F_W, d), F_W ** -0.5),
        'w_out': nrm(ks[16], (DEPTH, d, d), d ** -0.5),
        'w_router_group': nrm(ks[17], (DEPTH, d, N_GROUPS), d ** -0.5),
        'b_router_group': nrm(ks[18], (DEPTH, N_GROUPS), 0.01),
        'w_router_expert': nrm(ks[19], (DEPTH, d, N_EXPERTS), d ** -0.5),
        'b_router_expert': nrm(ks[20], (DEPTH, N_EXPERTS), 0.01),
        'w_exp_gate': nrm(ks[21], (DEPTH, N_EXPERTS, d, EXPERT_HIDDEN), d ** -0.5),
        'w_exp_up': nrm(ks[22], (DEPTH, N_EXPERTS, d, EXPERT_HIDDEN), d ** -0.5),
        'w_exp_down': nrm(ks[23], (DEPTH, N_EXPERTS, EXPERT_HIDDEN, d), EXPERT_HIDDEN ** -0.5),
        'final_g': 1.0 + nrm(ks[24], (d,), 0.02),
    }

def second_block(x, c, ctx, c_ctx, w_mod, b_mod, norm1_g, norm2_g, w_in, lam_q1, lam_k1, lam_q2, lam_k2,
              subln_g, w_attn_out, w_four_out, w_out, w_router_group, b_router_group, w_router_expert,
              b_router_expert, w_exp_gate, w_exp_up, w_exp_down, final_g):
    n = x.shape[1]
    rows = n // GRID_W
    ang_row, ang_col = axial_angles(rows)
    x_lat, x_ctx = x, ctx
    for l in range(DEPTH):
        update_ctx = l < DEPTH - 1
        lam_init = 0.8 - 0.6 * math.exp(-0.3 * l)
        lam = (jnp.exp(jnp.sum(lam_q1[l].astype(jnp.float32) * lam_k1[l].astype(jnp.float32)))
               - jnp.exp(jnp.sum(lam_q2[l].astype(jnp.float32) * lam_k2[l].astype(jnp.float32)))
               + lam_init)
        sh1, sc1, g1, sh2, sc2, g2 = [m[:, None, :] for m in jnp.split(jax.nn.silu(c) @ w_mod[l] + b_mod[l], 6, axis=-1)]
        csh1, csc1, cg1, csh2, csc2, cg2 = jnp.split(jax.nn.silu(c_ctx) @ w_mod[l] + b_mod[l], 6, axis=-1)

        h_c = modulate(rmsnorm(x_ctx, norm1_g[l]), csh1, csc1)
        if update_ctx:
            q_c, k_c, v_c, f_c, ga_c, gf_c = split_proj(h_c @ w_in[l])
        else:
            kv_c = h_c @ w_in[l][:, K_OFF:F_OFF]
            k_c = kv_c[..., :QK_W].reshape(x_ctx.shape[0], x_ctx.shape[1], N_HEADS, 2, HEAD_DIM_2)
            v_c = kv_c[..., QK_W:].reshape(x_ctx.shape[0], x_ctx.shape[1], N_HEADS, 2 * HEAD_DIM_2)
        h_l = modulate(rmsnorm(x_lat, norm1_g[l]), sh1, sc1)
        q_l, k_l, v_l, f_l, ga_l, gf_l = split_proj(h_l @ w_in[l])
        q_l = axial_rope(q_l, ang_row, ang_col)
        k_l = axial_rope(k_l, ang_row, ang_col)
        k_all = jnp.concatenate([k_c, k_l], axis=1)
        v_all = jnp.concatenate([v_c, v_l], axis=1)
        heads_l = blocked_latent_attention(q_l, k_all, v_all, lam)
        mix_l = merge_branches(heads_l, f_l, ga_l, gf_l, subln_g[l], lam_init, w_attn_out[l], w_four_out[l], w_out[l])
        x_lat = x_lat + g1 * mix_l
        if update_ctx:
            heads_c = diff_attend(q_c, k_c, v_c, lam)
            mix_c = merge_branches(heads_c, f_c, ga_c, gf_c, subln_g[l], lam_init, w_attn_out[l], w_four_out[l], w_out[l])
            x_ctx = x_ctx + cg1 * mix_c

        h2_l = modulate(rmsnorm(x_lat, norm2_g[l]), sh2, sc2)
        x_lat = x_lat + g2 * hier_moe(h2_l, w_router_group[l], b_router_group[l], w_router_expert[l],
                                      b_router_expert[l], w_exp_gate[l], w_exp_up[l], w_exp_down[l])
        if update_ctx:
            h2_c = modulate(rmsnorm(x_ctx, norm2_g[l]), csh2, csc2)
            x_ctx = x_ctx + cg2 * hier_moe(h2_c, w_router_group[l], b_router_group[l], w_router_expert[l],
                                          b_router_expert[l], w_exp_gate[l], w_exp_up[l], w_exp_down[l])
    return rmsnorm(x_lat, final_g)


def setup_inputs(seed=0):
    out = dict(first_inputs(seed))
    for name, value in second_inputs(seed + 1).items():
        if name != "x":
            out[name + "_2"] = value
    return out


def reference(
    x, norm_mix_g, w_in, w_conv, w_spatial, b_spatial, gmlp_ln_g, gmlp_ln_b, fox_q_norm_g,
    fox_k_norm_g, fox_forget_b, w_branch, w_out, norm_ffn_g, w_ffn_in, w_ffn_out, c_2, ctx_2,
    c_ctx_2, w_mod_2, b_mod_2, norm1_g_2, norm2_g_2, w_in_2, lam_q1_2, lam_k1_2, lam_q2_2,
    lam_k2_2, subln_g_2, w_attn_out_2, w_four_out_2, w_out_2, w_router_group_2,
    b_router_group_2, w_router_expert_2, b_router_expert_2, w_exp_gate_2, w_exp_up_2,
    w_exp_down_2, final_g_2,
):
    x = first_block(
        x, norm_mix_g, w_in, w_conv, w_spatial, b_spatial, gmlp_ln_g, gmlp_ln_b, fox_q_norm_g,
        fox_k_norm_g, fox_forget_b, w_branch, w_out, norm_ffn_g, w_ffn_in, w_ffn_out,
    )
    return second_block(
        x, c_2, ctx_2, c_ctx_2, w_mod_2, b_mod_2, norm1_g_2, norm2_g_2, w_in_2, lam_q1_2,
        lam_k1_2, lam_q2_2, lam_k2_2, subln_g_2, w_attn_out_2, w_four_out_2, w_out_2,
        w_router_group_2, b_router_group_2, w_router_expert_2, b_router_expert_2, w_exp_gate_2,
        w_exp_up_2, w_exp_down_2, final_g_2,
    )


_drawn_inputs = setup_inputs


def setup_inputs(seed=0):
    import zlib

    import numpy as np

    out = dict(_drawn_inputs(seed))
    spreads = {}
    factors = {'gmlp_ln_g': 5.027,
     'gmlp_ln_b': 8.0,
     'fox_q_norm_g': 7.164,
     'fox_k_norm_g': 6.886,
     'b_mod_2': 3.91,
     'norm1_g_2': 8.0,
     'norm2_g_2': 7.775,
     'lam_q1_2': 64.0,
     'lam_k1_2': 64.0,
     'lam_q2_2': 6.037,
     'lam_k2_2': 5.57,
     'subln_g_2': 8.0,
     'b_router_group_2': 8.0,
     'b_router_expert_2': 8.0,
     'final_g_2': 8.15}
    for name, (base, spread) in spreads.items():
        noise = np.random.default_rng([zlib.crc32(name.encode()), seed]).standard_normal(out[name].shape)
        drawn = base * np.exp(spread * noise) if base else spread * noise
        out[name] = __import__('jax').numpy.asarray(drawn.astype(out[name].dtype))
    for name, factor in factors.items():
        out[name] = (out[name] * factor).astype(out[name].dtype)
    return out
```

```python
from contextlib import ExitStack

import numpy as np
import concourse.bass as bass
from concourse import mybir

F32 = mybir.dt.float32
ALU = mybir.AluOpType
ACT = mybir.ActivationFunctionType
AX = mybir.AxisListType

P = 128
D = 1024
SEQ = 256
KT = D // P
TT = SEQ // P
MIX = 256
FFN = 2816
FT_TILES = FFN // P
HEADS1 = 4
HD = 64
HEADS2 = 8
NEXP = 16
HID = 512
EPS = 1e-6
NEG = -1e30
COL = 512
SLOT = KT * COL
RING = 5

W_IN_STARTS = (0, 512, 1024, 1536, 2048, 2560)
F_RAW = 2816
GATE_RAW = 2820
Q_OFF, K_OFF, V_OFF, F_OFF, GA_OFF, GF_OFF = 0, 1024, 2048, 3072, 3584, 4608


def shape_tables():
    i = np.arange(P)
    parts = {}
    parts["ident"] = np.eye(P)
    parts["upto"] = (i[:, None] <= i[None, :]) * 1.0
    parts["ones"] = np.ones((P, P))
    parts["from"] = (i[:, None] >= i[None, :]) * 1.0
    strict = (i[:, None] < i[None, :]) * 1.0
    parts["strict"] = np.concatenate([strict, np.ones((P, P)), strict], 1)
    parts["strict_neg"] = np.where(parts["strict"] > 0, 0.0, NEG)
    parts["causal_neg"] = np.where(i[None, :] <= i[:, None], 0.0, NEG)
    turn = np.zeros((P, P))
    for b in range(0, P, 32):
        for j in range(16):
            turn[b + 16 + j, b + j] = -1.0
            turn[b + j, b + 16 + j] = 1.0
    parts["turn"] = turn
    inv = (1.0 / (np.float32(10000.0) ** (np.arange(16, dtype=np.float32) / np.float32(16)))).astype(np.float32)
    tok = np.arange(SEQ)
    row = (tok // 64).astype(np.float32)
    col = (tok % 64).astype(np.float32)
    d = i % 64
    angle = np.where((d < 32)[:, None], row[None, :] * inv[d % 16][:, None], col[None, :] * inv[d % 16][:, None])
    parts["cos"] = np.cos(angle.astype(np.float64))
    parts["sin"] = np.sin(angle.astype(np.float64))
    w = 2 * np.pi * np.outer(tok, tok) / SEQ
    dft = np.concatenate([np.cos(w), np.sin(w)], 1) / np.sqrt(SEQ)
    parts["dft_tok"] = dft.reshape(TT, P, 2 * SEQ).transpose(1, 0, 2).reshape(P, -1)
    w = 2 * np.pi * np.outer(i, i) / P
    parts["dft_cos"] = np.cos(w) / np.sqrt(P)
    parts["dft_nsin"] = -np.sin(w) / np.sqrt(P)
    parts["rev"] = np.tile(np.array([4.0, 3.0, 2.0, 1.0]), (P, 1))
    at, start = {}, 0
    for name, a in parts.items():
        at[name] = (start, a.shape[1])
        start += a.shape[1]
    return np.concatenate(list(parts.values()), 1).astype(np.float32), at


TABLES, TABLE_AT = shape_tables()

ROWS = {}
for _name, _n in (("norm_mix_g", 8), ("norm_ffn_g", 8), ("norm1_g_2", 8), ("norm2_g_2", 8), ("c_2", 8),
                  ("c_ctx_2", 8), ("b_mod_2", 48), ("w_conv", 6)):
    ROWS[_name] = (sum(n for _, n in ROWS.values()), _n)
N_ROWS = sum(n for _, n in ROWS.values())


def plan_chunks(a):
    def cols(w, start, n=COL):
        return w[:, start:start + n].rearrange("(k p) n -> p k n", p=P)

    w_in, w_ffn, w_in2, w_mod = a["w_in"][0], a["w_ffn_in"][0], a["w_in_2"][0], a["w_mod_2"][0]
    out = [("in", cols(w_in, s, min(COL, GATE_RAW - s))) for s in W_IN_STARTS]
    out += [("gate", cols(w_in, GATE_RAW + COL * i)) for i in range(8)]
    wb = a["w_branch"][0].rearrange("n c d -> (n c) d")
    out += [("branch", cols(wb, COL * h)) for h in range(2)]
    out += [("out1", cols(a["w_out"][0], COL * h)) for h in range(2)]
    for i in range(6):
        n = min(COL, FFN - COL * i)
        out += [("ffn_g", cols(w_ffn, COL * i, n)), ("ffn_u", cols(w_ffn, FFN + COL * i, n))]
    wo = a["w_ffn_out"][0]
    for i in range(6):
        k = min(4, FT_TILES - 4 * i)
        out.append(("ffn_o", wo[512 * i:512 * i + P * k, :].rearrange("(k p) n -> p k n", p=P)))
    out += [("mod_T", cols(w_mod, D * part + COL * h)) for part in (0, 1, 3, 4) for h in range(2)]
    for name, start, n in (("q", Q_OFF, 2), ("k", K_OFF, 2), ("v", V_OFF, 2), ("f", F_OFF, 1), ("g2", GA_OFF, 4)):
        out += [(name, cols(w_in2, start + COL * i)) for i in range(n)]
    out += [("mod_g1", cols(w_mod, 2 * D + COL * h)) for h in range(2)]
    out.append(("fo", a["w_four_out_2"][0].rearrange("(k p) n -> p k n", p=P)))
    out += [("ao", cols(a["w_attn_out_2"][0], COL * h)) for h in range(2)]
    out += [("out2", cols(a["w_out_2"][0], COL * h)) for h in range(2)]
    out += [("mod_g2", cols(w_mod, 5 * D + COL * h)) for h in range(2)]
    return out


def slot_of(i, first_expert):
    return i % RING if i < first_expert else (i - first_expert) % (RING + 1)


def block_pair_kernel(nc, a, out):
    chunks = plan_chunks(a)
    n_dense = len(chunks)
    n_chunks = n_dense + 3 * NEXP
    index = {}
    for i, (name, _) in enumerate(chunks):
        index.setdefault(name, i)
    use_of = {}
    prev = {}
    seen = {}
    for i in range(n_chunks):
        s = slot_of(i, n_dense)
        use_of[i] = len(seen.setdefault(s, []))
        prev[i] = seen[s][-1] if seen[s] else None
        seen[s].append(i)

    ctx = ExitStack()
    with ctx:
        def sb(name, shape):
            return ctx.enter_context(nc.sbuf_tensor(name, shape, F32))

        sems = {}

        def sem(name):
            if name not in sems:
                sems[name] = ctx.enter_context(nc.semaphore(name))
            return sems[name]

        ring = sb("ring", [P, RING * SLOT])
        tables = sb("tables_sb", [P, TABLES.shape[1]])
        x = sb("x_sb", [P, TT, D])
        hT = sb("hT", [P, KT, 2 * SEQ])
        arena = sb("arena", [P, 21272])
        feat_cols = sb("feat_cols", [P, N_ROWS])
        lnw = sb("lnw", [P, 2, MIX])
        qk_g = sb("qk_g", [P, 2, HD])
        subln = sb("subln", [P, P])
        bs = sb("bs", [P, 2, P])
        bf = sb("bf", [P, HEADS1])
        rb = sb("rb", [P, 20])
        modT = sb("modT", [P, 4, KT, 2])
        silu_c = sb("silu_c", [P, KT, 2])
        half_root = sb("half_root", [P, 16])
        st = sb("st", [P, 416])
        PG = ctx.enter_context(nc.psum_tensor("gemm_ps", [P, 4, 512], F32))
        PM = ctx.enter_context(nc.psum_tensor("mix_ps", [P, 4, 512], F32))

        def at(start, *dims):
            n = int(np.prod(dims))
            v = arena[:, start:start + n]
            if len(dims) == 1:
                return v
            names = "abcd"[:len(dims)]
            return v.rearrange(f"p ({' '.join(names)}) -> p {' '.join(names)}", **dict(zip(names, dims)))

        def tab(name, *dims):
            s, n = TABLE_AT[name]
            v = tables[:, s:s + n]
            if not dims:
                return v
            names = "abcd"[:len(dims)]
            return v.rearrange(f"p ({' '.join(names)}) -> p {' '.join(names)}", **dict(zip(names, dims)))

        def feat(name, j=0):
            s, _ = ROWS[name]
            return feat_cols[:, s + j:s + j + 1]

        def feats(name, j, n):
            s, _ = ROWS[name]
            return feat_cols[:, s + j:s + j + n]

        ident = tab("ident")
        ones = tab("ones")

        SG = at(0, TT, 4 * D)
        CB, CC = at(8192, 2, SEQ), at(8704, 2, SEQ)
        XC = at(9216, 2, SEQ + 2)
        U, V = at(9736, 2, SEQ), at(10248, TT, MIX)
        SQ, SK, SV = at(10760, 2, SEQ), at(11272, 2, SEQ), at(11784, TT, MIX)
        FQK = at(12296, TT, 512)
        FV = at(13320, TT, MIX)
        FR = at(13832, TT, HEADS1)
        T1, T2, T3 = at(13848, 4, 384), at(15384, 4, 384), at(16920, 4, 384)
        FT = at(18456, 4, SEQ)
        WS, WST = at(18456, 4, P), at(19480, 4, P)
        NLF = at(19992, 2, HEADS1, P)
        VROWS = at(19992, P)
        lamv = at(21016, 4, HD)
        XN = at(13848, TT, D)
        JUNK = at(16920, D)
        TMP = at(16920, TT, COL)
        AT = at(0, FT_TILES, SEQ)
        SILU = at(8192, 2, 4, SEQ)
        YT = hT[:, :, SEQ:2 * SEQ]
        hTa, hTb = hT[:, :, 0:SEQ], hT[:, :, SEQ:2 * SEQ]
        QT = at(0, KT, SEQ)
        KTT = at(2048, KT, 2 * SEQ)
        V2 = at(6144, 4, D)
        SG2 = at(10240, TT, 2 * D)
        FT2 = at(14336, 4, SEQ)
        O = at(15360, TT, D)
        FN = at(15360, TT, COL)
        DT = at(16384, 2, 512)
        PP = at(17408, 2, 2, 512)
        RAW = at(17408, 2, 2, SEQ)
        ROT = at(18432, 2, 2, SEQ)
        AA = at(19456, 2, 512)
        CTX = at(15360, TT, D)
        XN2, JUNK2 = at(17408, TT, D), at(19456, D)
        SB = at(0, KT, P)
        G1 = at(1024, D)
        Y = at(2048, TT, D)
        XN3 = at(4096, TT, D)
        G2 = at(6144, D)
        JUNK3 = at(7168, D)
        OT = at(8192, KT, SEQ)
        ACC = at(2048, TT, D)
        BM = at(17408, 2, D)
        FINAL = at(19456, D)
        wr = at(20480, KT, 20)
        SL = at(14336, 2, 4, SEQ)
        ET = at(16384, 2, 4, SEQ)
        SLOT5 = 10240

        ss = st[:, 0:16]
        rs = st[:, 16:32]
        gm = st[:, 32:64]
        fs = st[:, 64:160]
        ds = st[:, 160:208]
        ms = st[:, 208:416]

        def slot(i):
            s = slot_of(i, n_dense)
            if s == RING:
                return arena[:, SLOT5:SLOT5 + SLOT]
            return ring[:, s * SLOT:(s + 1) * SLOT]

        def wide(i, n=COL):
            return slot(i)[:, 0:KT * n].rearrange("p (k n) -> p k n", k=KT)

        def tall(i, k=4):
            return slot(i)[:, 0:k * D].rearrange("p (k n) -> p k n", k=k)

        landed = [sem(f"landed{s}") for s in range(RING + 1)]

        def chunk_wait(eng, i):
            eng.wait_ge(landed[slot_of(i, n_dense)], 16 * (use_of[i] + 1))

        step = {}
        n_steps = 0
        for name, n in (("in", 6), ("gate", 8), ("branch", 8), ("out1", 2), ("ffn", 12), ("ffn_o", 2),
                        ("mod_T", 8), ("q", 2), ("k", 4), ("v", 4), ("f", 1), ("g2", 4), ("mod_g1", 2),
                        ("y", 4), ("out2", 2), ("mod_g2", 2), ("exp", 2 * NEXP)):
            step[name] = n_steps
            n_steps += n
        made = [sem("pair0_made"), sem("pair1_made")]
        freed = [sem("pair0_freed"), sem("pair1_freed")]

        def pair_wait(eng, p, bank):
            eng.wait_ge(made[p % 2], 2 * (p // 2) + 1 + bank)

        def pair_free_wait(eng, p):
            if p >= 2:
                eng.wait_ge(freed[p % 2], 2 * (p // 2))

        def bank(p, b):
            return PG[:, 2 * (p % 2) + b, :]

        TURN = {"x1": 0, "merged": 1, "x2": 2, "ctx": 3, "x3": 4, "heads": 5, "y2": 6, "x4": 7}
        rows_ready, turned = sem("rows_ready"), sem("turned")
        cols_dve, cols_act = sem("cols_by_vector"), sem("cols_by_scalar")
        NORM = {"x1": 0, "x2": 1, "ctx": 2, "x3": 3, "x4": 4, "last": 5}
        squares = sem("squares")

        block = ctx.enter_context(nc.Block())

        def expert_chunks():
            order = [("eg", 0)]
            for e in range(NEXP):
                order.append(("eu", e))
                if e + 1 < NEXP:
                    order.append(("eg", e + 1))
                order.append(("ed", e))
            return order

        expert_at = {key: n_dense + j for j, key in enumerate(expert_chunks())}

        def last_product(i):
            def of_step(p):
                return made[p % 2], 2 * (p // 2) + 2
            if i >= n_dense:
                kind, e = next(key for key, j in expert_at.items() if j == i)
                return (sem("expert_made"), 4 * (e + 1)) if kind == "ed" else of_step(step["exp"] + 2 * e + (kind == "eu"))
            name = chunks[i][0]
            c = i - index[name]
            if name == "ffn_o":
                return (sem("ffn_o_used"), c + 1) if c < 5 else of_step(step["ffn_o"] + 1)
            if name in ("ffn_g", "ffn_u"):
                return of_step(step["ffn"] + i - index["ffn_g"])
            steps = {"branch": step["branch"] + 4 * c + 3, "k": step["k"] + 2 * c + 1, "v": step["v"] + 2 * c + 1,
                     "fo": step["y"] + 1, "ao": step["y"] + 2 + c}
            return of_step(steps[name] if name in steps else step[name] + c)

        def slot_free_wait(eng, i):
            eng.wait_ge(*last_product(prev[i]))

        @block.sync
        def _(sp):
            for i, (name, src) in enumerate(chunks):
                if prev[i] is not None:
                    slot_free_wait(sp, i)
                _, k, n = src.shape
                dst = slot(i)[:, 0:k * n].rearrange("p (k n) -> p k n", k=k)
                sp.dma_start(dst, src).then_inc(landed[slot_of(i, n_dense)], 16)
            for (kind, e), i in expert_at.items():
                if prev[i] is not None:
                    slot_free_wait(sp, i)
                else:
                    sp.wait_ge(sem("y_ready"), TT)
                if kind == "ed":
                    src = a["w_exp_down_2"][0, e].rearrange("(k p) n -> p k n", p=P)
                    dst = tall(i)
                else:
                    w = a["w_exp_gate_2" if kind == "eg" else "w_exp_up_2"]
                    src = w[0, e].rearrange("(k p) n -> p k n", p=P)
                    dst = wide(i)
                sp.dma_start(dst, src).then_inc(landed[slot_of(i, n_dense)], 16)
            for t in range(TT):
                sp.wait_ge(sem("out_ready"), t + 1)
                sp.dma_start(out[0, t * P:(t + 1) * P, :], XN3[:, t, :]).then_inc(sem("out_sent"), 16)
            sp.wait_ge(sem("out_sent"), 16 * TT)

        @block.gpsimd
        def _(pool):
            def load(dst, src, name, n=16):
                pool.dma_start(dst, src).then_inc(sem(name), n)

            pool.memset(half_root[:, :], -0.5).then_inc(sem("exponent"), 1)
            pool.memset(XC[:, :, 0:2], 0.0).then_inc(sem("pad_ready"), 1)
            for n, (first, count) in ROWS.items():
                v = a[n]
                if n == "w_conv":
                    v = v[0].rearrange("k (j p) -> (k j) p", p=P)
                elif len(v.shape) == 1:
                    v = v.rearrange("(j p) -> j p", p=P)
                else:
                    v = v[0].rearrange("(j p) -> j p", p=P)
                load(VROWS[first:first + count, :], v, "vec_rows")
            load(WS, a["w_spatial"][0].rearrange("g t s -> t g s"), "ws_in")
            load(lnw[:, 0, :], a["gmlp_ln_g"].partition_broadcast(P), "small")
            load(lnw[:, 1, :], a["gmlp_ln_b"].partition_broadcast(P), "small")
            load(qk_g[:, 0, :], a["fox_q_norm_g"].partition_broadcast(P), "small")
            load(qk_g[:, 1, :], a["fox_k_norm_g"].partition_broadcast(P), "small")
            for g in range(4):
                h = 64 * (g % 2)
                load(bs[h:h + 64, g // 2, :], a["b_spatial"][0, g:g + 1, :].partition_broadcast(64), "small")
            load(bf[:, :], a["fox_forget_b"].partition_broadcast(P), "small")
            load(subln[:, :], a["subln_g_2"].partition_broadcast(P), "small2")
            for j, n in enumerate(("lam_q1_2", "lam_k1_2", "lam_q2_2", "lam_k2_2")):
                load(lamv[:, j, :], a[n].partition_broadcast(P), "small2")
            load(rb[:, 0:4], a["b_router_group_2"].partition_broadcast(P), "small2")
            load(rb[:, 4:20], a["b_router_expert_2"].partition_broadcast(P), "small2")
            pool.wait_ge(sem("exponent"), 1)
            roots = [0]

            def root(v):
                roots[0] += 1
                pool.wait_ge(sem("var_ready"), roots[0])
                nc.gpsimd.tensor_tensor(v, v, half_root[:, 0:v.shape[1]], ALU.pow).then_inc(sem("root_ready"), 1)

            def norm_roots(name):
                for t in range(TT):
                    j = 2 * NORM[name] + t
                    root(rs[:, j:j + 1])

            norm_roots("x1")
            root(gm[:, 2:4])
            root(fs[:, 40:56])
            norm_roots("x2")
            pool.wait_ge(sem("silu_used"), 6)
            load(CTX, a["ctx_2"][0].rearrange("(t p) d -> p t d", p=P), "ctx_in")
            norm_roots("ctx")
            norm_roots("x3")
            pool.wait_ge(sem("heads_rows"), HEADS2 * TT)
            load(BM[0:1, 0, :], a["b_mod_2"][:, 2 * D:3 * D], "late_in")
            load(BM[0:1, 1, :], a["b_mod_2"][:, 5 * D:6 * D], "late_in")
            load(FINAL, a["final_g_2"].rearrange("(o n) -> o n", o=1).partition_broadcast(P), "late_in")
            load(wr[:, :, 0:4], a["w_router_group_2"][0].rearrange("(k p) n -> p k n", p=P), "late_in")
            load(wr[:, :, 4:20], a["w_router_expert_2"][0].rearrange("(k p) n -> p k n", p=P), "late_in")

            root(ds[:, 32:48])
            norm_roots("x4")
            norm_roots("last")

        @block.tensor
        def _(pe):
            mm = nc.tensor.matmul

            def bank_of(j, k):
                return PM[:, k // 2, (k % 2) * SEQ:(k % 2 + 1) * SEQ]

            def turn(name, src):
                j = TURN[name]
                pe.wait_ge(rows_ready, TT * (j + 1))
                for b in range(4):
                    for k in (2 * b, 2 * b + 1):
                        for t in range(TT):
                            last = nc.tensor.transpose(bank_of(j, k)[:, t * P:(t + 1) * P], src[:, t, k * P:(k + 1) * P], ident)
                    last.then_inc(turned, 1)

            def cols_ready(name):
                j = TURN[name]
                pe.wait_ge(cols_dve, 4 * (j + 1))
                pe.wait_ge(cols_act, 4 * (j + 1))

            def rows_gemm(i, p, lhs, w, n=COL, t_tiles=(0, 1)):
                pair_free_wait(pe, p)
                chunk_wait(pe, i)
                ks = w.shape[1]
                for b, t in enumerate(t_tiles):
                    for k in range(ks):
                        last = mm(bank(p, b)[:, 0:n], lhs[:, k, t * P:(t + 1) * P], w[:, k, :], start=(k == 0), stop=(k == ks - 1))
                    last.then_inc(made[p % 2], 1)

            def cols_gemm(p, rhs, w, tiles, n=SEQ, first=0):
                ks = w.shape[1]
                per = 512 // n
                for m in tiles:
                    o = bank(p, (m - first) // per)[:, ((m - first) % per) * n:((m - first) % per + 1) * n]
                    for k in range(ks):
                        last = mm(o, w[:, k, m * P:(m + 1) * P], rhs(k), start=(k == 0), stop=(k == ks - 1))
                    if m == tiles[-1]:
                        last.then_inc(made[p % 2], 2 - (m - first) // per)
                    elif (m - first) % per == per - 1:
                        last.then_inc(made[p % 2], 1)
                return last

            pe.wait_ge(sem("tables_in"), 16)
            pe.wait_ge(sem("vec_rows"), 16 * len(ROWS))
            nc.tensor.transpose(PM[:, 0, 0:N_ROWS], VROWS[0:N_ROWS, :], ident[0:N_ROWS, 0:N_ROWS]).then_inc(sem("consts_turned"), 1)
            pe.wait_ge(sem("ws_in"), 16)
            for g in range(4):
                last = nc.tensor.transpose(PM[:, 1, g * P:(g + 1) * P], WS[:, g, :], ident)
            last.then_inc(sem("consts_turned"), 1)
            pe.wait_ge(sem("consts_read"), 2)
            turn("x1", XN)
            cols_ready("x1")

            h = hTa
            i = index["in"]
            for c in range(2):
                p = step["in"] + c
                pair_free_wait(pe, p)
                chunk_wait(pe, i + c)
                last = cols_gemm(p, lambda k: h[:, k, :], wide(i + c), (0, 1, 2, 3))
            p = step["in"] + 2
            pair_free_wait(pe, p)
            chunk_wait(pe, i + 2)
            w = wide(i + 2)
            for t in range(TT):
                for k in range(KT):
                    last = mm(bank(p, 0)[:, t * MIX:(t + 1) * MIX], h[:, k, t * P:(t + 1) * P], w[:, k, 0:MIX], start=(k == 0), stop=(k == KT - 1))
            last.then_inc(made[p % 2], 1)
            for m in range(2):
                for k in range(KT):
                    last = mm(bank(p, 1)[:, m * SEQ:(m + 1) * SEQ], w[:, k, MIX + m * P:MIX + (m + 1) * P], h[:, k, :], start=(k == 0), stop=(k == KT - 1))
            last.then_inc(made[p % 2], 1)
            p = step["in"] + 3
            pair_free_wait(pe, p)
            chunk_wait(pe, i + 3)
            w = wide(i + 3)
            for m in range(2):
                for k in range(KT):
                    last = mm(bank(p, 0)[:, m * SEQ:(m + 1) * SEQ], w[:, k, m * P:(m + 1) * P], h[:, k, :], start=(k == 0), stop=(k == KT - 1))
            last.then_inc(made[p % 2], 1)
            for t in range(TT):
                for k in range(KT):
                    last = mm(bank(p, 1)[:, t * MIX:(t + 1) * MIX], h[:, k, t * P:(t + 1) * P], w[:, k, MIX:2 * MIX], start=(k == 0), stop=(k == KT - 1))
            last.then_inc(made[p % 2], 1)
            rows_gemm(i + 4, step["in"] + 4, h, wide(i + 4))
            n5 = GATE_RAW - W_IN_STARTS[5]
            rows_gemm(i + 5, step["in"] + 5, h, wide(i + 5, n5), n=n5)

            def stick_scores():
                pe.wait_ge(sem("stick_qk"), 2)
                for hd in range(HEADS1):
                    r, j = HD * (hd % 2), hd // 2
                    mm(PM[:, hd, 0:SEQ], SK[r:r + HD, j, 0:P], SQ[r:r + HD, j, :], start=True, stop=True)
                    last = mm(PM[:, hd, SEQ:384], SK[r:r + HD, j, P:SEQ], SQ[r:r + HD, j, P:SEQ], start=True, stop=True)
                last.then_inc(sem("stick_z"), 1)

            def fox_turn():
                pe.wait_ge(sem("fox_qk"), 1)
                pe.wait_ge(sem("stick_z_read"), 1)
                for j in range(4):
                    for t in range(TT):
                        last = nc.tensor.transpose(PM[:, j // 2, (j % 2) * SEQ + t * P:(j % 2) * SEQ + (t + 1) * P],
                                                   FQK[:, t, j * P:(j + 1) * P], ident)
                last.then_inc(sem("fox_turned"), 1)

            def stick_sums():
                pe.wait_ge(sem("stick_l"), 1)
                pe.wait_ge(sem("fox_T"), 1)
                for hd in range(HEADS1):
                    mm(PM[:, hd, 0:384], tab("from"), T3[:, hd, :], start=True, stop=False)
                    last = mm(PM[:, hd, P:SEQ], ones, T3[:, hd, SEQ:384], start=False, stop=True)
                last.then_inc(sem("stick_c"), 1)

            def weigh(w, v, o, name):
                for hd in range(HEADS1):
                    r, j = HD * (hd % 2), hd // 2
                    dst = o[r:r + HD, j * SEQ:(j + 1) * SEQ]
                    mm(dst, v[:, 0, hd * HD:(hd + 1) * HD], w[:, hd, 0:SEQ], start=True, stop=False)
                    last = mm(dst[:, P:SEQ], v[:, 1, hd * HD:(hd + 1) * HD], w[:, hd, SEQ:384], start=False, stop=True)
                last.then_inc(sem(name), 1)

            def stick_out_and_spatial():
                pe.wait_ge(sem("stick_w"), 1)
                pe.wait_ge(sem("stick_v"), 1)
                weigh(T1, SV, PM[:, 0, :], "stick_o")
                pe.wait_ge(sem("spatial_v"), 1)
                for g in range(4):
                    r, j = HD * (g % 2), g // 2
                    for t in range(TT):
                        last = mm(PM[r:r + HD, 1, j * SEQ + t * P:j * SEQ + (t + 1) * P],
                                  V[:, t, g * HD:(g + 1) * HD], WST[:, g, :], start=True, stop=True)
                last.then_inc(sem("spatial_mix"), 1)

            def fox_scores():
                pe.wait_ge(sem("fox_f"), 1)
                pe.wait_ge(sem("stick_o_read"), 1)
                pe.wait_ge(sem("spatial_read"), 1)
                upto = tab("upto")
                s0, _ = TABLE_AT["upto"]
                upto_ones = tables[:, s0:s0 + 2 * P]
                for hd in range(HEADS1):
                    r, j = HD * (hd % 2), hd // 2
                    q = FT[r:r + HD, j, :]
                    k = FT[r:r + HD, 2 + j, :]
                    s = PM[:, hd, :]
                    mm(s[:, 0:P], q[:, 0:P], k[:, 0:P], start=True, stop=False)
                    mm(s[:, 0:P], NLF[:, 0, hd, :], upto, start=False, stop=False)
                    mm(s[:, 0:P], ident, tab("causal_neg"), start=False, stop=True)
                    mm(s[:, P:384], q[:, P:SEQ], k, start=True, stop=False)
                    mm(s[:, P:384], NLF[:, 0, hd, :], upto_ones, start=False, stop=False)
                    mm(s[:, SEQ:384], NLF[:, 1, hd, :], upto, start=False, stop=False)
                    mm(s[:, SEQ:384], ident, tab("causal_neg"), start=False, stop=True)
                f = PM[:, 0, 384:392]
                mm(f[:, 0:4], upto, NLF[:, 0, :, 0], start=True, stop=True)
                mm(f[:, 4:8], ones, NLF[:, 0, :, 0], start=True, stop=False)
                mm(f[:, 4:8], upto, NLF[:, 1, :, 0], start=False, stop=True).then_inc(sem("fox_s"), 1)

            def fox_probs_turn():
                pe.wait_ge(sem("fox_p"), 1)
                for hd in range(HEADS1):
                    for b in range(3):
                        last = nc.tensor.transpose(PM[:, hd, b * P:(b + 1) * P], T2[:, hd, b * P:(b + 1) * P], ident)
                last.then_inc(sem("fox_p_turned"), 1)

            def fox_out():
                pe.wait_ge(sem("fox_pT"), 1)
                weigh(T3, FV, PM[:, 0, :], "fox_o")

            between = {0: stick_scores, 1: fox_turn, 2: stick_sums, 3: stick_out_and_spatial,
                       4: fox_scores, 5: fox_probs_turn, 6: fox_out}
            for c in range(8):
                rows_gemm(index["gate"] + c, step["gate"] + c, h, wide(index["gate"] + c))
                if c in between:
                    between[c]()
            pe.wait_ge(sem("branch_T"), 4)
            for half in range(2):
                i = index["branch"] + half
                chunk_wait(pe, i)
                w = wide(i)
                for n in range(4):
                    p = step["branch"] + 4 * half + n
                    pair_free_wait(pe, p)
                    for t in range(TT):
                        for k in range(2):
                            last = mm(bank(p, t), YT[:, 2 * n + k, t * P:(t + 1) * P], w[:, 2 * n + k, :], start=(k == 0), stop=(k == 1))
                        last.then_inc(made[p % 2], 1)
            pe.wait_ge(sem("fox_o_read"), 1)
            turn("merged", XN)
            cols_ready("merged")
            for half in range(2):
                rows_gemm(index["out1"] + half, step["out1"] + half, hTa, wide(index["out1"] + half))
            turn("x2", XN)
            cols_ready("x2")
            for c in range(6):
                tiles = tuple(range(4 if c < 5 else 2))
                for j in range(2):
                    i = index["ffn_g"] + 2 * c + j
                    p = step["ffn"] + 2 * c + j
                    pair_free_wait(pe, p)
                    chunk_wait(pe, i)
                    cols_gemm(p, lambda k: hTb[:, k, :], wide(i, len(tiles) * P), tiles)
            p = step["ffn_o"]
            pair_free_wait(pe, p)
            pair_free_wait(pe, p + 1)
            for c in range(6):
                i = index["ffn_o"] + c
                ks = min(4, FT_TILES - 4 * c)
                chunk_wait(pe, i)
                pe.wait_ge(sem("ffn_hidden"), c + 1)
                w = tall(i, ks)
                for t in range(TT):
                    for half in range(2):
                        for k in range(ks):
                            kk = 4 * c + k
                            last = mm(bank(p + t, half), AT[:, kk, t * P:(t + 1) * P], w[:, k, half * COL:(half + 1) * COL],
                                      start=(kk == 0), stop=(kk == FT_TILES - 1))
                        if c == 5:
                            last.then_inc(made[(p + t) % 2], 1)
                        elif (t, half) == (1, 1):
                            last.then_inc(sem("ffn_o_used"), 1)
            pe.wait_ge(sem("silu_c"), 1)
            for c in range(8):
                p = step["mod_T"] + c
                i = index["mod_T"] + c
                pair_free_wait(pe, p)
                chunk_wait(pe, i)
                w = wide(i)
                for m in range(4):
                    for k in range(KT):
                        last = mm(bank(p, 0)[:, 2 * m:2 * m + 2], w[:, k, m * P:(m + 1) * P], silu_c[:, k, :], start=(k == 0), stop=(k == KT - 1))
                last.then_inc(made[p % 2], 2)
            turn("ctx", XN2)
            cols_ready("ctx")
            turn("x3", XN2)
            cols_ready("x3")
            for c in range(2):
                p, i = step["q"] + c, index["q"] + c
                pair_free_wait(pe, p)
                chunk_wait(pe, i)
                cols_gemm(p, lambda k: hT[:, k, SEQ:2 * SEQ], wide(i), (0, 1, 2, 3))

            def rope_products(j):
                pe.wait_ge(sem("rope_raw"), j + 1)
                if j >= 2:
                    pe.wait_ge(sem("rope_done"), j - 1)
                mm(PM[:, j % 2, :], tab("turn"), RAW[:, j % 2, :, :], start=True, stop=True).then_inc(sem("rope_rot"), 1)

            for j in range(2):
                rope_products(j)
            for c in range(2):
                i = index["k"] + c
                chunk_wait(pe, i)
                for half in range(2):
                    p = step["k"] + 2 * c + half
                    pair_free_wait(pe, p)
                    cols_gemm(p, lambda k: hT[:, k, :], wide(i), (2 * half, 2 * half + 1), n=512, first=2 * half)
                    rope_products(2 + 2 * c + half)
            for c in range(2):
                i = index["v"] + c
                for half in range(2):
                    rows_gemm(i, step["v"] + 2 * c + half, hT, wide(i), t_tiles=(2 * half, 2 * half + 1))
                    if 2 * c + half < 2:
                        rope_products(6 + 2 * c + half)
            rows_gemm(index["f"], step["f"], hTb, wide(index["f"]))
            pe.wait_ge(sem("four_rows"), 2)
            pe.wait_ge(sem("rope_done"), 8)
            dft = tab("dft_tok", TT, 512)
            for g in range(4):
                if g >= 2:
                    pe.wait_ge(sem("four_A"), g - 1)
                for t in range(TT):
                    last = mm(PM[:, g % 2, :], FN[:, t, g * P:(g + 1) * P], dft[:, t, :], start=(t == 0), stop=(t == 1))
                last.then_inc(sem("four_1"), 1)
                pe.wait_ge(sem("four_A"), g + 1)
                if g >= 2:
                    pe.wait_ge(sem("four_B"), g - 1)
                mm(PM[:, 2 + g % 2, 0:SEQ], tab("dft_cos"), DT[:, g % 2, 0:SEQ], start=True, stop=False)
                mm(PM[:, 2 + g % 2, 0:SEQ], tab("dft_nsin"), DT[:, g % 2, SEQ:512], start=False, stop=True).then_inc(sem("four_2"), 1)

            def scores(n):
                hd, t = n // TT, n % TT
                if n >= 1:
                    pe.wait_ge(sem("probs"), 2 * n)
                for c in range(2):
                    last = mm(PM[:, c, :], QT[c * HD:(c + 1) * HD, hd, t * P:(t + 1) * P], KTT[c * HD:(c + 1) * HD, hd, :], start=True, stop=True)
                last.then_inc(sem("scores"), 1)

            def probs_turn(n):
                pe.wait_ge(sem("diff"), n + 1)
                if n >= 1:
                    pe.wait_ge(sem("diff_T"), n)
                for k in range(4):
                    last = nc.tensor.transpose(PM[:, 2, k * P:(k + 1) * P], PP[:, n % 2, 0, k * P:(k + 1) * P], ident)
                last.then_inc(sem("diff_turned"), 1)

            def heads_out(n):
                hd, t = n // TT, n % TT
                pe.wait_ge(sem("diff_T"), n + 1)
                if n >= 1:
                    pe.wait_ge(sem("heads_rows"), n)
                for k in range(4):
                    last = mm(PM[:, 3, 0:P], AA[:, n % 2, k * P:(k + 1) * P], V2[:, k, hd * P:(hd + 1) * P], start=(k == 0), stop=(k == 3))
                last.then_inc(sem("heads_made"), 1)

            pe.wait_ge(sem("four_B"), 4)
            pe.wait_ge(sem("kv_ready"), 8)
            N = HEADS2 * TT
            for n in range(N + 2):
                if n < N:
                    c, q = n // 4, n % 4
                    i, p = index["g2"] + c, step["g2"] + c
                    if q == 0:
                        pair_free_wait(pe, p)
                        chunk_wait(pe, i)
                    w = wide(i)
                    t = q // 2
                    for k in range(4 * (q % 2), 4 * (q % 2) + 4):
                        last = mm(bank(p, t), hTb[:, k, t * P:(t + 1) * P], w[:, k, :], start=(k == 0), stop=(k == KT - 1))
                    if q % 2 == 1:
                        last.then_inc(made[p % 2], 1)
                    scores(n)
                if 1 <= n <= N:
                    probs_turn(n - 1)
                if n >= 2:
                    heads_out(n - 2)

            def mod_rows(name, which):
                for c in range(2):
                    i, p = index[name] + c, step[name] + c
                    pair_free_wait(pe, p)
                    chunk_wait(pe, i)
                    w = wide(i)
                    for k in range(KT):
                        mm(bank(p, 0), SB[:, k, :], w[:, k, :], start=(k == 0), stop=False)
                    pe.wait_ge(sem("late_in"), 80)
                    mm(bank(p, 0), ones[0:1, :], BM[0:1, which, c * COL:(c + 1) * COL], start=False, stop=True).then_inc(made[p % 2], 2)

            pe.wait_ge(sem("sb_ready"), 1)
            mod_rows("mod_g1", 0)
            turn("heads", O)
            i = index["fo"]
            for half in range(2):
                p = step["y"] + half
                pair_free_wait(pe, p)
                chunk_wait(pe, i)
                w = tall(i)
                for t in range(TT):
                    for k in range(4):
                        last = mm(bank(p, t), FT2[:, k, t * P:(t + 1) * P], w[:, k, half * COL:(half + 1) * COL], start=(k == 0), stop=(k == 3))
                    last.then_inc(made[p % 2], 1)
            cols_ready("heads")
            for half in range(2):
                rows_gemm(index["ao"] + half, step["y"] + 2 + half, OT, wide(index["ao"] + half))
            turn("y2", Y)
            cols_ready("y2")
            for half in range(2):
                rows_gemm(index["out2"] + half, step["out2"] + half, hTa, wide(index["out2"] + half))
            mod_rows("mod_g2", 1)
            turn("x4", XN3)
            cols_ready("x4")
            for t in range(TT):
                for k in range(KT):
                    last = mm(PM[:, 0, t * 20:(t + 1) * 20], hTb[:, k, t * P:(t + 1) * P], wr[:, k, :], start=(k == 0), stop=(k == KT - 1))
            last.then_inc(sem("logits"), 1)
            def expert_up(kind, e):
                i, p = expert_at[(kind, e)], step["exp"] + 2 * e + (kind == "eu")
                pair_free_wait(pe, p)
                chunk_wait(pe, i)
                cols_gemm(p, lambda k: hTb[:, k, :], wide(i), (0, 1, 2, 3))

            def expert_down(e):
                i = expert_at[("ed", e)]
                chunk_wait(pe, i)
                pe.wait_ge(sem("hidden"), 2 * (e + 1))
                if e == 0:
                    pe.wait_ge(sem("logits_read"), 1)
                w = tall(i)
                for t in range(TT):
                    for half in range(2):
                        if e >= 1:
                            pe.wait_ge(sem("added"), 4 * (e - 1) + 2 * t + half + 1)
                        for k in range(4):
                            last = mm(PM[:, 2 * t + half, :], ET[:, e % 2, k, t * P:(t + 1) * P], w[:, k, half * COL:(half + 1) * COL],
                                      start=(k == 0), stop=(k == 3))
                        last.then_inc(sem("expert_made"), 1)

            expert_up("eg", 0)
            for e in range(NEXP):
                expert_up("eu", e)
                if e + 1 < NEXP:
                    expert_up("eg", e + 1)
                expert_down(e)

        @block.scalar
        def _(act):
            A = nc.scalar.activation
            chain = [0]

            def link(ins):
                chain[0] += 1
                ins.then_inc(sem("act_chain"), 1)
                act.wait_ge(sem("act_chain"), chain[0])

            def take(p, b, out, fn=ACT.Copy, src=None, **kw):
                pair_wait(act, p, b)
                A(out, bank(p, b) if src is None else src, fn, **kw).then_inc(freed[p % 2], 1)

            def norm_squares(name, src, junk):
                j = NORM[name]
                for t in range(TT):
                    A(junk, src[:, t, :], ACT.Square, accum_out=ss[:, 2 * j + t:2 * j + t + 1]).then_inc(squares, 1)
                    act.wait_ge(squares, 2 * j + t + 1)

            def cols(name, dst, scale=None, shift=None):
                j = TURN[name]
                for k in range(4, KT):
                    if k % 2 == 0:
                        act.wait_ge(turned, 4 * j + k // 2 + 1)
                    src = PM[:, k // 2, (k % 2) * SEQ:(k % 2 + 1) * SEQ]
                    kw = {}
                    fn = ACT.Copy
                    if scale is not None:
                        kw["scale"] = scale(k)
                    if shift is not None:
                        kw["bias"] = shift(k)
                        fn = ACT.Identity
                    A(dst[:, k, :], src, fn, **kw).then_inc(cols_act, 1)

            act.dma_start(x[:, :, :], a["x"][0].rearrange("(t p) d -> p t d", p=P)).then_inc(sem("x_in"), 16)
            act.dma_start(tables[:, :], a["tables"]).then_inc(sem("tables_in"), 16)
            act.wait_ge(sem("x_in"), 16)
            norm_squares("x1", x, JUNK)
            act.wait_ge(sem("consts_read"), 2)
            cols("x1", hTa, scale=lambda k: feat("norm_mix_g", k))

            p = step["in"]
            take(p, 0, CB)
            take(p, 1, CC)
            pair_wait(act, p + 1, 1)
            A(U, bank(p + 1, 1), ACT.Gelu_apprx_tanh).then_inc(freed[(p + 1) % 2], 1)
            pair_wait(act, p + 2, 0)
            A(V, bank(p + 2, 0), ACT.Gelu_apprx_tanh).then_inc(sem("v_gelu"), 1)
            act.wait_ge(sem("v_gelu"), 1)
            act.nop().then_inc(freed[(p + 2) % 2], 1)
            pair_wait(act, p + 2, 1)
            A(SQ, bank(p + 2, 1), ACT.Copy).then_inc(sem("stick_qk"), 1)
            act.wait_ge(sem("stick_qk"), 1)
            act.nop().then_inc(freed[(p + 2) % 2], 1)
            pair_wait(act, p + 3, 0)
            A(SK, bank(p + 3, 0), ACT.Copy).then_inc(sem("stick_qk"), 1)
            act.wait_ge(sem("stick_qk"), 2)
            act.nop().then_inc(freed[(p + 3) % 2], 1)
            pair_wait(act, p + 3, 1)
            A(SV, bank(p + 3, 1), ACT.Copy).then_inc(sem("stick_v"), 1)
            act.wait_ge(sem("stick_v"), 1)
            act.nop().then_inc(freed[(p + 3) % 2], 1)
            for t in range(TT):
                take(p + 4, t, FQK[:, t, :])
            for t in range(TT):
                pair_wait(act, p + 5, t)
                link(A(FV[:, t, :], bank(p + 5, t)[:, 0:MIX], ACT.Copy))
                A(FR[:, t, :], bank(p + 5, t)[:, MIX:MIX + 4], ACT.Copy).then_inc(freed[(p + 5) % 2], 1)

            def stick_softplus():
                act.wait_ge(sem("stick_z_read"), 1)
                link(A(T2, T1, ACT.Abs))
                link(A(T2, T2, ACT.Exp, scale=-1.0))
                A(T2, T2, ACT.Ln, bias=1.0).then_inc(sem("stick_ln"), 1)

            def fox_T():
                act.wait_ge(sem("fox_turned"), 1)
                link(A(FT[:, 0:2, :], PM[:, 0, :], ACT.Copy))
                A(FT[:, 2:4, :], PM[:, 1, :], ACT.Copy).then_inc(sem("fox_T"), 1)

            def fox_log():
                act.wait_ge(sem("fox_abs"), 1)
                f = fs[:, 0:8]
                link(A(f, FR.rearrange("p t h -> p (t h)"), ACT.Abs))
                link(A(f, f, ACT.Exp, scale=-1.0))
                A(f, f, ACT.Ln, bias=1.0).then_inc(sem("fox_ln"), 1)

            def stick_exp():
                act.wait_ge(sem("stick_logw"), 1)
                A(T1, T1, ACT.Exp).then_inc(sem("stick_w"), 1)

            def stick_read():
                act.wait_ge(sem("stick_o"), 1)
                A(YT[:, 4:6, :], PM[:, 0, :].rearrange("p (j q) -> p j q", j=2), ACT.Copy).then_inc(sem("stick_o_read"), 1)
                act.wait_ge(sem("stick_o_read"), 1)
                act.nop().then_inc(sem("branch_T"), 1)

            def fox_exp():
                act.wait_ge(sem("fox_max"), 1)
                for hd in range(HEADS1):
                    for t in range(TT):
                        s = PM[:, hd, 0:P] if t == 0 else PM[:, hd, P:384]
                        d = T2[:, hd, 0:P] if t == 0 else T2[:, hd, P:384]
                        last = A(d, s, ACT.Exp, bias=fs[:, 24 + 4 * t + hd:25 + 4 * t + hd], accum_out=fs[:, 32 + 4 * t + hd:33 + 4 * t + hd])
                        last.then_inc(sem("fox_e"), 1)

            def fox_read():
                act.wait_ge(sem("fox_o"), 1)
                A(YT[:, 6:8, :], PM[:, 0, :].rearrange("p (j q) -> p j q", j=2), ACT.Copy).then_inc(sem("fox_o_read"), 1)
                act.wait_ge(sem("fox_o_read"), 1)
                act.nop().then_inc(sem("branch_T"), 1)

            between = {0: (stick_softplus, fox_log), 1: (fox_T,), 2: (stick_exp,), 3: (stick_read,), 4: (fox_exp,), 6: (fox_read,)}
            for c in range(8):
                for t in range(TT):
                    take(step["gate"] + c, t, SG[:, t, c * COL:(c + 1) * COL], ACT.Sigmoid)
                for f in between.get(c, ()):
                    f()
            act.nop().then_inc(sem("gates_sig"), 1)
            cols("merged", hTa)
            act.wait_ge(sem("x_1"), 4)
            norm_squares("x2", x, JUNK)
            cols("x2", hTb, scale=lambda k: feat("norm_ffn_g", k))
            for c in range(6):
                p = step["ffn"] + 2 * c
                if c >= 2:
                    act.wait_ge(sem("silu_used"), c - 1)
                if c < 5:
                    for b in range(2):
                        pair_wait(act, p, b)
                        ins = A(SILU[:, c % 2, 2 * b:2 * b + 2, :], bank(p, b), ACT.Silu)
                        ins.then_inc(sem("silu_done"), 1)
                        act.wait_ge(sem("silu_done"), 2 * c + b + 1)
                        act.nop().then_inc(freed[p % 2], 1)
                else:
                    pair_wait(act, p, 0)
                    A(SILU[:, c % 2, 0:2, :], bank(p, 0), ACT.Silu).then_inc(sem("silu_done"), 2)
                    act.wait_ge(sem("silu_done"), 2 * c + 2)
                    act.nop().then_inc(freed[p % 2], 2)
            A(silu_c[:, :, 0], feats("c_2", 0, 8), ACT.Silu)
            A(silu_c[:, :, 1], feats("c_ctx_2", 0, 8), ACT.Silu).then_inc(sem("silu_c"), 1)
            act.wait_ge(sem("lam_sums"), 2)
            A(ds[:, 2:4], ds[:, 0:2], ACT.Exp).then_inc(sem("lam_exp"), 1)
            act.wait_ge(sem("ctx_in"), 16)
            norm_squares("ctx", CTX, JUNK2)
            act.wait_ge(sem("mod_cols"), 1)
            cols("ctx", hTa, scale=lambda k: modT[:, 1, k, 1:2], shift=lambda k: modT[:, 0, k, 1:2])
            act.wait_ge(sem("x_2"), 4)
            norm_squares("x3", x, JUNK2)
            cols("x3", hTb, scale=lambda k: modT[:, 1, k, 0:1], shift=lambda k: modT[:, 0, k, 0:1])

            for j in range(4):
                p = step["q"] + j // 2
                if j >= 2:
                    act.wait_ge(sem("rope_done"), j - 1)
                pair_wait(act, p, j % 2)
                A(RAW[:, j % 2, :, :], bank(p, j % 2), ACT.Copy).then_inc(sem("rope_raw"), 1)
                act.wait_ge(sem("rope_raw"), j + 1)
                act.nop().then_inc(freed[p % 2], 1)
            for j in range(4):
                p = step["k"] + j
                act.wait_ge(sem("rope_done"), 3 + j)
                for b in range(2):
                    pair_wait(act, p, b)
                    link(A(KTT[:, 2 * j + b, 0:SEQ], bank(p, b)[:, 0:SEQ], ACT.Copy))
                    ins = A(RAW[:, j % 2, b, :], bank(p, b)[:, SEQ:512], ACT.Copy)
                    if b == 0:
                        link(ins)
                    else:
                        ins.then_inc(sem("rope_raw"), 1)
                        act.wait_ge(sem("rope_raw"), 5 + j)
                    act.nop().then_inc(freed[p % 2], 1)
            for j in range(4):
                p = step["v"] + j
                for b in range(2):
                    pair_wait(act, p, b)
                    c = j // 2
                    A(V2[:, 2 * (j % 2) + b, c * COL:(c + 1) * COL], bank(p, b), ACT.Copy).then_inc(sem("v_copied"), 1)
                    act.wait_ge(sem("v_copied"), 2 * j + b + 1)
                    act.nop().then_inc(freed[p % 2], 1)
            act.nop().then_inc(sem("kv_ready"), 4)
            p = step["f"]
            for t in range(TT):
                pair_wait(act, p, t)
                A(FN[:, t, :], bank(p, t), ACT.Copy).then_inc(sem("four_rows"), 1)
                act.wait_ge(sem("four_rows"), t + 1)
                act.nop().then_inc(freed[p % 2], 1)
            for g in range(4):
                act.wait_ge(sem("four_1"), g + 1)
                if g >= 2:
                    act.wait_ge(sem("four_2"), g - 1)
                A(DT[:, g % 2, :], PM[:, g % 2, :], ACT.Copy).then_inc(sem("four_A"), 1)

            N = HEADS2 * TT
            for n in range(N):
                act.wait_ge(sem("nmax"), n + 1)
                if n >= 2:
                    act.wait_ge(sem("diff_turned"), n - 1)
                for c in range(2):
                    A(PP[:, n % 2, c, :], PM[:, c, :], ACT.Exp, scale=HD ** -0.5, bias=ds[:, 16 + 2 * (n % 2) + c:17 + 2 * (n % 2) + c],
                      accum_out=ds[:, 20 + 2 * (n % 2) + c:21 + 2 * (n % 2) + c]).then_inc(sem("probs"), 1)
                if n % 2 == 1:
                    c, t = n // 4, (n % 4) // 2
                    take(step["g2"] + c, t, SG2[:, t, c * COL:(c + 1) * COL], ACT.Sigmoid)
                if n >= 1:
                    act.wait_ge(sem("heads_made"), n)
                    m = n - 1
                    A(O[:, m % TT, (m // TT) * P:(m // TT + 1) * P], PM[:, 3, 0:P], ACT.Copy).then_inc(sem("heads_rows"), 1)
            act.wait_ge(sem("heads_made"), N)
            m = N - 1
            A(O[:, m % TT, (m // TT) * P:(m // TT + 1) * P], PM[:, 3, 0:P], ACT.Copy).then_inc(sem("heads_rows"), 1)
            act.wait_ge(sem("heads_rows"), N)
            for c in range(2):
                p = step["mod_g1"] + c
                pair_wait(act, p, 1)
                A(G1[:, c * COL:(c + 1) * COL], bank(p, 0), ACT.Copy).then_inc(sem("g1_rows"), 1)
                act.wait_ge(sem("g1_rows"), c + 1)
                act.nop().then_inc(freed[p % 2], 2)
            cols("heads", OT)
            cols("y2", hTa)
            for c in range(2):
                p = step["mod_g2"] + c
                pair_wait(act, p, 1)
                A(G2[:, c * COL:(c + 1) * COL], bank(p, 0), ACT.Copy).then_inc(sem("g2_rows"), 1)
                act.wait_ge(sem("g2_rows"), c + 1)
                act.nop().then_inc(freed[p % 2], 2)
            act.wait_ge(sem("x_3"), 4)
            norm_squares("x4", x, JUNK3)
            cols("x4", hTb, scale=lambda k: modT[:, 3, k, 0:1], shift=lambda k: modT[:, 2, k, 0:1])
            act.wait_ge(sem("route_d"), 1)
            A(ms[:, 80:88], ms[:, 72:80], ACT.Exp).then_inc(sem("route_e"), 1)
            act.wait_ge(sem("route_r"), 1)
            A(ms[:, 130:132], ms[:, 128:130], ACT.Exp).then_inc(sem("route_e"), 1)
            for e in range(NEXP):
                p = step["exp"] + 2 * e
                if e >= 2:
                    act.wait_ge(sem("hidden"), 2 * (e - 1))
                for b in range(2):
                    pair_wait(act, p, b)
                    A(SL[:, e % 2, 2 * b:2 * b + 2, :], bank(p, b), ACT.Silu).then_inc(sem("exp_silu"), 1)
                    act.wait_ge(sem("exp_silu"), 2 * e + b + 1)
                    act.nop().then_inc(freed[p % 2], 1)
            act.wait_ge(sem("x_4"), 2)
            norm_squares("last", x, JUNK3)

        @block.vector
        def _(dve):
            V_ = nc.vector
            chain = [0]

            def link(ins):
                chain[0] += 1
                ins.then_inc(sem("vec_chain"), 1)
                dve.wait_ge(sem("vec_chain"), chain[0])

            roots = [0]

            def inv_sqrt(ins):
                roots[0] += 1
                ins.then_inc(sem("var_ready"), 1)
                dve.wait_ge(sem("root_ready"), roots[0])

            def norm_rows(name, src, dst, g_turn, turn_free=None):
                j = NORM[name]
                for t in range(TT):
                    s, r = ss[:, 2 * j + t:2 * j + t + 1], rs[:, 2 * j + t:2 * j + t + 1]
                    dve.wait_ge(squares, 2 * j + t + 1)
                    inv_sqrt(V_.tensor_scalar(r, s, 1.0 / D, EPS, ALU.mult, ALU.add))
                    ins = V_.tensor_scalar(dst[:, t, :], src[:, t, :], r, None, ALU.mult)
                    if g_turn:
                        ins.then_inc(rows_ready, 1)
                    else:
                        link(ins)

            def cols(name, dst, scale=None, shift=None):
                j = TURN[name]
                for k in range(4):
                    if k % 2 == 0:
                        dve.wait_ge(turned, 4 * j + k // 2 + 1)
                    src = PM[:, k // 2, (k % 2) * SEQ:(k % 2 + 1) * SEQ]
                    if scale is None:
                        ins = V_.tensor_copy(dst[:, k, :], src)
                    elif shift is None:
                        ins = V_.tensor_scalar(dst[:, k, :], src, scale(k), None, ALU.mult)
                    else:
                        ins = V_.tensor_scalar(dst[:, k, :], src, scale(k), shift(k), ALU.mult, ALU.add)
                    ins.then_inc(cols_dve, 1)

            dve.wait_ge(sem("consts_turned"), 1)
            V_.tensor_copy(feat_cols[:, :], PM[:, 0, 0:N_ROWS]).then_inc(sem("consts_read"), 1)
            dve.wait_ge(sem("consts_turned"), 2)
            dve.wait_ge(sem("tables_in"), 16)
            V_.tensor_tensor(WST, PM[:, 1, :].rearrange("p (g t) -> p g t", g=4), tab("upto").unsqueeze(1).to_broadcast([P, 4, P]),
                             ALU.mult).then_inc(sem("consts_read"), 1)
            dve.wait_ge(sem("x_in"), 16)
            norm_rows("x1", x, XN, True)
            dve.wait_ge(sem("consts_read"), 2)
            cols("x1", hTa, scale=lambda k: feat("norm_mix_g", k))

            p = step["in"]
            pair_wait(dve, p + 1, 0)
            dve.wait_ge(sem("pad_ready"), 1)
            dve.wait_ge(freed[p % 2], 2)
            V_.tensor_tensor(XC[:, :, 2:SEQ + 2], CC, bank(p + 1, 0).rearrange("p (j q) -> p j q", j=2), ALU.mult).then_inc(freed[(p + 1) % 2], 1)
            dve.wait_ge(freed[(p + 1) % 2], 2)
            for j in range(2):
                y = YT[:, j, :]
                link(V_.tensor_scalar(y, XC[:, j, 0:SEQ], feat("w_conv", j), None, ALU.mult))
                link(V_.scalar_tensor_tensor(y, XC[:, j, 1:SEQ + 1], feat("w_conv", 2 + j), y, ALU.mult, ALU.add))
                link(V_.scalar_tensor_tensor(y, XC[:, j, 2:SEQ + 2], feat("w_conv", 4 + j), y, ALU.mult, ALU.add))
            V_.tensor_tensor(YT[:, 0:2, :], YT[:, 0:2, :], CB, ALU.mult).then_inc(sem("branch_T"), 1)

            dve.wait_ge(sem("v_gelu"), 1)
            dve.wait_ge(sem("small"), 16 * 9)
            sq = T3[:, :, 0:P].rearrange("p a b -> p a b")
            mean, var = gm[:, 0:2], gm[:, 2:4]
            link(V_.tensor_reduce(mean, V, AX.X, ALU.add))
            link(V_.tensor_scalar(mean, mean, 1.0 / MIX, None, ALU.mult))
            for t in range(TT):
                link(V_.tensor_scalar(V[:, t, :], V[:, t, :], mean[:, t:t + 1], None, ALU.subtract))
            sq = TMP[:, :, 0:MIX]
            link(V_.tensor_tensor(sq, V, V, ALU.mult))
            link(V_.tensor_reduce(var, sq, AX.X, ALU.add))
            inv_sqrt(V_.tensor_scalar(var, var, 1.0 / MIX, EPS, ALU.mult, ALU.add))
            for t in range(TT):
                link(V_.scalar_tensor_tensor(V[:, t, :], V[:, t, :], var[:, t:t + 1], lnw[:, 0, :], ALU.mult, ALU.mult))
            V_.tensor_tensor(V, V, lnw[:, 1, :].unsqueeze(1).to_broadcast([P, TT, MIX]), ALU.add).then_inc(sem("spatial_v"), 1)

            dve.wait_ge(freed[(p + 4) % 2], 2 * ((p + 4) // 2 + 1))
            nh = 2 * HEADS1
            heads = FQK.rearrange("p t (h d) -> p t h d", d=HD)
            sq4 = TMP
            r = fs[:, 40:40 + 2 * nh].rearrange("p (t h) -> p t h", t=TT)
            link(V_.tensor_tensor(sq4, FQK, FQK, ALU.mult))
            link(V_.tensor_reduce(r, sq4.rearrange("p t (h d) -> p t h d", d=HD), AX.X, ALU.add))
            inv_sqrt(V_.tensor_scalar(r, r, 1.0 / HD, EPS, ALU.mult, ALU.add))
            link(V_.tensor_scalar(r[:, :, 0:HEADS1], r[:, :, 0:HEADS1], HD ** -0.5, None, ALU.mult))
            link(V_.tensor_tensor(heads, heads, r.unsqueeze(3).to_broadcast([P, TT, nh, HD]), ALU.mult))
            for n in range(2):
                hv = heads[:, :, n * HEADS1:(n + 1) * HEADS1, :]
                for t in range(TT):
                    ins = V_.tensor_tensor(hv[:, t], hv[:, t], qk_g[:, n, :].unsqueeze(1).to_broadcast([P, HEADS1, HD]), ALU.mult)
                    if (n, t) == (1, TT - 1):
                        ins.then_inc(sem("fox_qk"), 1)
                    else:
                        link(ins)
            dve.wait_ge(freed[(p + 5) % 2], 2 * ((p + 5) // 2 + 1))
            V_.tensor_tensor(FR, FR, bf[:, :].unsqueeze(1).to_broadcast([P, TT, HEADS1]), ALU.add).then_inc(sem("fox_abs"), 1)
            dve.wait_ge(sem("fox_abs"), 1)
            fflat = FR.rearrange("p t h -> p (t h)")
            link(V_.tensor_scalar(fs[:, 8:16], fflat, 0.0, None, ALU.min))

            dve.wait_ge(sem("stick_z"), 1)
            V_.tensor_scalar(T1, PM[:, :, 0:384], HD ** -0.5, None, ALU.mult).then_inc(sem("stick_z_read"), 1)
            dve.wait_ge(sem("stick_z_read"), 1)
            link(V_.tensor_scalar(T3, T1, 0.0, None, ALU.max))
            dve.wait_ge(sem("stick_ln"), 1)
            link(V_.tensor_tensor(T3, T3, T2, ALU.add))
            V_.tensor_tensor(T3, T3, tab("strict").unsqueeze(1).to_broadcast([P, 4, 384]), ALU.mult).then_inc(sem("stick_l"), 1)
            link(V_.tensor_tensor(T1, T1, tab("strict_neg").unsqueeze(1).to_broadcast([P, 4, 384]), ALU.add))
            dve.wait_ge(sem("fox_ln"), 1)
            link(V_.tensor_tensor(fs[:, 0:8], fs[:, 0:8], fs[:, 8:16], ALU.subtract))
            V_.tensor_copy(NLF.rearrange("p t h n -> p (t h) n"), fs[:, 0:8].unsqueeze(2).to_broadcast([P, 8, P])).then_inc(sem("fox_f"), 1)
            dve.wait_ge(sem("stick_c"), 1)
            V_.tensor_tensor(T1, T1, PM[:, :, 0:384], ALU.subtract).then_inc(sem("stick_logw"), 1)

            dve.wait_ge(sem("spatial_mix"), 1)
            dve.wait_ge(freed[(p + 1) % 2], 2)
            m4 = PM[:, 1, :].rearrange("p (j t n) -> p j t n", j=2, t=TT)
            y4 = YT[:, 2:4, :].rearrange("p j (t n) -> p j t n", t=TT)
            for j in range(2):
                ins = V_.tensor_tensor(y4[:, j], m4[:, j], bs[:, j, :].unsqueeze(1).to_broadcast([P, TT, P]), ALU.add)
                if j == 0:
                    link(ins)
                else:
                    ins.then_inc(sem("spatial_read"), 1)
            dve.wait_ge(sem("spatial_read"), 1)
            V_.tensor_tensor(YT[:, 2:4, :], YT[:, 2:4, :], U, ALU.mult).then_inc(sem("branch_T"), 1)

            dve.wait_ge(sem("fox_s"), 1)
            mx = fs[:, 16:24]
            link(V_.tensor_reduce(mx[:, 0:4], PM[:, :, 0:P], AX.X, ALU.max))
            link(V_.tensor_reduce(mx[:, 4:8], PM[:, :, P:384], AX.X, ALU.max))
            nF = fs[:, 60:68]
            link(V_.tensor_copy(nF, PM[:, 0, 384:392]))
            link(V_.tensor_tensor(mx, mx, nF, ALU.subtract))
            link(V_.tensor_tensor(fs[:, 24:32], mx, nF, ALU.add))
            V_.tensor_scalar(fs[:, 24:32], fs[:, 24:32], -1.0, None, ALU.mult).then_inc(sem("fox_max"), 1)
            dve.wait_ge(sem("fox_e"), 8)
            link(V_.reciprocal(fs[:, 32:40], fs[:, 32:40]))
            link(V_.tensor_tensor(T2[:, :, 0:P], T2[:, :, 0:P], fs[:, 32:36].unsqueeze(2).to_broadcast([P, 4, P]), ALU.mult))
            V_.tensor_tensor(T2[:, :, P:384], T2[:, :, P:384], fs[:, 36:40].unsqueeze(2).to_broadcast([P, 4, 2 * P]), ALU.mult).then_inc(sem("fox_p"), 1)
            dve.wait_ge(sem("fox_p_turned"), 1)
            V_.tensor_copy(T3, PM[:, :, 0:384]).then_inc(sem("fox_pT"), 1)

            for half in range(2):
                for n in range(4):
                    p = step["branch"] + 4 * half + n
                    for t in range(TT):
                        pair_wait(dve, p, t)
                        if (half, n, t) == (0, 0, 0):
                            dve.wait_ge(sem("gates_sig"), 1)
                            dve.wait_ge(freed[(step["gate"] + 7) % 2], 2 * ((step["gate"] + 7) // 2 + 1))
                            dve.wait_ge(freed[(step["gate"] + 6) % 2], 2 * ((step["gate"] + 6) // 2 + 1))
                            dve.wait_ge(sem("fox_o"), 1)
                        g = SG[:, t, n * D + half * COL:n * D + (half + 1) * COL]
                        m = XN[:, t, half * COL:(half + 1) * COL]
                        if n == 0:
                            V_.tensor_tensor(m, g, bank(p, t), ALU.mult).then_inc(freed[p % 2], 1)
                        else:
                            tmp = TMP[:, t, :]
                            V_.tensor_tensor(tmp, g, bank(p, t), ALU.mult).then_inc(freed[p % 2], 1)
                            dve.wait_ge(freed[p % 2], 2 * (p // 2) + t + 1)
                            ins = V_.tensor_tensor(m, m, tmp, ALU.add)
                            if half == 1 and n == 3:
                                ins.then_inc(rows_ready, 1)
                            else:
                                link(ins)
            cols("merged", hTa)
            for half in range(2):
                p = step["out1"] + half
                for t in range(TT):
                    pair_wait(dve, p, t)
                    xs = x[:, t, half * COL:(half + 1) * COL]
                    V_.tensor_tensor(xs, xs, bank(p, t), ALU.add).then_inc(sem("x_1"), 1)
                    dve.wait_ge(sem("x_1"), 2 * half + t + 1)
                    V_.nop().then_inc(freed[p % 2], 1)
            norm_rows("x2", x, XN, True)
            cols("x2", hTb, scale=lambda k: feat("norm_ffn_g", k))
            for c in range(6):
                p = step["ffn"] + 2 * c + 1
                dve.wait_ge(sem("silu_done"), 2 * c + 2)
                if c < 5:
                    for b in range(2):
                        pair_wait(dve, p, b)
                        m = 4 * c + 2 * b
                        ins = V_.tensor_tensor(AT[:, m:m + 2, :], SILU[:, c % 2, 2 * b:2 * b + 2, :],
                                               bank(p, b).rearrange("p (j q) -> p j q", j=2), ALU.mult)
                        ins.then_inc(freed[p % 2], 1)
                else:
                    pair_wait(dve, p, 0)
                    V_.tensor_tensor(AT[:, 20:22, :], SILU[:, c % 2, 0:2, :], bank(p, 0).rearrange("p (j q) -> p j q", j=2),
                                     ALU.mult).then_inc(freed[p % 2], 2)
                dve.wait_ge(freed[p % 2], 2 * (p // 2 + 1))
                V_.nop().then_inc(sem("ffn_hidden"), 1)
                V_.nop().then_inc(sem("silu_used"), 1)
            dve.wait_ge(sem("small2"), 16 * 7)
            for j in range(2):
                link(V_.tensor_tensor(lamv[:, 2 * j, :], lamv[:, 2 * j, :], lamv[:, 2 * j + 1, :], ALU.mult))
                V_.tensor_reduce(ds[:, j:j + 1], lamv[:, 2 * j, :], AX.X, ALU.add).then_inc(sem("lam_sums"), 1)
            dve.wait_ge(sem("lam_exp"), 1)
            link(V_.tensor_tensor(ds[:, 4:5], ds[:, 2:3], ds[:, 3:4], ALU.subtract))
            lam = ds[:, 5:6]
            link(V_.tensor_scalar(lam, ds[:, 4:5], 0.2, None, ALU.add))
            link(V_.tensor_scalar(subln[:, :], subln[:, :], 0.8, None, ALU.mult))
            p = step["ffn_o"]
            for t in range(TT):
                for half in range(2):
                    pair_wait(dve, p + t, half)
                    xs = x[:, t, half * COL:(half + 1) * COL]
                    V_.tensor_tensor(xs, xs, bank(p + t, half), ALU.add).then_inc(sem("x_2"), 1)
                    dve.wait_ge(sem("x_2"), 2 * t + half + 1)
                    V_.nop().then_inc(freed[(p + t) % 2], 1)
            for c in range(8):
                p = step["mod_T"] + c
                part, half = c // 2, c % 2
                pair_wait(dve, p, 1)
                b0 = (0, 1, 3, 4)[part] * 8 + 4 * half
                dst = modT[:, part, 4 * half:4 * half + 4, :]
                V_.tensor_tensor(dst, bank(p, 0)[:, 0:8].rearrange("p (m c) -> p m c", c=2),
                                 feats("b_mod_2", b0, 4).unsqueeze(2).to_broadcast([P, 4, 2]), ALU.add).then_inc(freed[p % 2], 2)
                dve.wait_ge(freed[p % 2], 2 * (p // 2 + 1))
            for part, g in ((1, "norm1_g_2"), (3, "norm2_g_2")):
                ins = V_.scalar_tensor_tensor(modT[:, part, :, :], modT[:, part, :, :], 1.0,
                                              feats(g, 0, 8).unsqueeze(2).to_broadcast([P, KT, 2]), ALU.add, ALU.mult)
                if part == 3:
                    ins.then_inc(sem("mod_cols"), 1)
                else:
                    link(ins)
            norm_rows("ctx", CTX, XN2, True)
            dve.wait_ge(sem("mod_cols"), 1)
            cols("ctx", hTa, scale=lambda k: modT[:, 1, k, 1:2], shift=lambda k: modT[:, 0, k, 1:2])
            norm_rows("x3", x, XN2, True)
            cols("x3", hTb, scale=lambda k: modT[:, 1, k, 0:1], shift=lambda k: modT[:, 0, k, 0:1])

            for j in range(8):
                dst = QT[:, 2 * j:2 * j + 2, :] if j < 4 else KTT[:, 2 * (j - 4):2 * (j - 4) + 2, SEQ:2 * SEQ]
                raw, rot = RAW[:, j % 2, :, :], ROT[:, j % 2, :, :]
                dve.wait_ge(sem("rope_raw"), j + 1)
                dve.wait_ge(sem("rope_rot"), j + 1)
                link(V_.tensor_tensor(rot, PM[:, j % 2, :].rearrange("p (a q) -> p a q", a=2),
                                      tab("sin").unsqueeze(1).to_broadcast([P, 2, SEQ]), ALU.mult))
                link(V_.tensor_tensor(dst, raw, tab("cos").unsqueeze(1).to_broadcast([P, 2, SEQ]), ALU.mult))
                V_.tensor_tensor(dst, dst, rot, ALU.add).then_inc(sem("rope_done"), 1)
                dve.wait_ge(sem("rope_done"), j + 1)
            V_.nop().then_inc(sem("kv_ready"), 4)
            for g in range(4):
                dve.wait_ge(sem("four_2"), g + 1)
                V_.tensor_copy(FT2[:, g, :], PM[:, 2 + g % 2, 0:SEQ]).then_inc(sem("four_B"), 1)

            N = HEADS2 * TT
            for n in range(N):
                nm = ds[:, 16 + 2 * (n % 2):18 + 2 * (n % 2)]
                sums = ds[:, 20 + 2 * (n % 2):22 + 2 * (n % 2)]
                dve.wait_ge(sem("scores"), n + 1)
                link(V_.tensor_reduce(ds[:, 8:10], PM[:, 0:2, :], AX.X, ALU.max))
                V_.tensor_scalar(nm, ds[:, 8:10], -HD ** -0.5, None, ALU.mult).then_inc(sem("nmax"), 1)
                if n >= 1:
                    dve.wait_ge(sem("diff_turned"), n)
                    if n >= 3:
                        dve.wait_ge(sem("heads_made"), n - 2)
                    V_.tensor_copy(AA[:, (n - 1) % 2, :], PM[:, 2, :]).then_inc(sem("diff_T"), 1)
                dve.wait_ge(sem("probs"), 2 * n + 2)
                link(V_.reciprocal(ds[:, 12:14], sums))
                link(V_.tensor_tensor(ds[:, 14:15], ds[:, 13:14], lam, ALU.mult))
                link(V_.tensor_scalar(PP[:, n % 2, 1, :], PP[:, n % 2, 1, :], ds[:, 14:15], None, ALU.mult))
                V_.scalar_tensor_tensor(PP[:, n % 2, 0, :], PP[:, n % 2, 0, :], ds[:, 12:13], PP[:, n % 2, 1, :],
                                        ALU.mult, ALU.subtract).then_inc(sem("diff"), 1)
            dve.wait_ge(sem("diff_turned"), N)
            V_.tensor_copy(AA[:, (N - 1) % 2, :], PM[:, 2, :]).then_inc(sem("diff_T"), 1)
            V_.tensor_copy(SB, silu_c[:, :, 0:1].to_broadcast([P, KT, P])).then_inc(sem("sb_ready"), 1)
            dve.wait_ge(sem("heads_rows"), N)
            hv = O.rearrange("p t (h d) -> p (t h) d", d=P)
            sq = XN3.rearrange("p t (h d) -> p (t h) d", d=P)
            r = ds[:, 32:48]
            link(V_.tensor_tensor(sq, hv, hv, ALU.mult))
            link(V_.tensor_reduce(r, sq, AX.X, ALU.add))
            inv_sqrt(V_.tensor_scalar(r, r, 1.0 / P, EPS, ALU.mult, ALU.add))
            link(V_.tensor_tensor(hv, hv, r.unsqueeze(2).to_broadcast([P, 16, P]), ALU.mult))
            for t in range(TT):
                ht = O[:, t, :].rearrange("p (h d) -> p h d", d=P)
                V_.tensor_tensor(ht, ht, subln[:, :].unsqueeze(1).to_broadcast([P, HEADS2, P]), ALU.mult).then_inc(rows_ready, 1)
            cols("heads", OT)
            for half in range(2):
                p = step["y"] + half
                for t in range(TT):
                    pair_wait(dve, p, t)
                    g = SG2[:, t, D + half * COL:D + (half + 1) * COL]
                    V_.tensor_tensor(Y[:, t, half * COL:(half + 1) * COL], g, bank(p, t), ALU.mult).then_inc(freed[p % 2], 1)
            for half in range(2):
                p = step["y"] + 2 + half
                for t in range(TT):
                    pair_wait(dve, p, t)
                    g = SG2[:, t, half * COL:(half + 1) * COL]
                    tmp = XN3[:, t, 0:COL]
                    ys = Y[:, t, half * COL:(half + 1) * COL]
                    V_.tensor_tensor(tmp, g, bank(p, t), ALU.mult).then_inc(freed[p % 2], 1)
                    dve.wait_ge(freed[p % 2], 2 * (p // 2) + t + 1)
                    ins = V_.tensor_tensor(ys, ys, tmp, ALU.add)
                    if half == 1:
                        ins.then_inc(rows_ready, 1)
                        dve.wait_ge(rows_ready, TT * TURN["y2"] + t + 1)
                        V_.nop().then_inc(sem("y_ready"), 1)
                    else:
                        link(ins)
            cols("y2", hTa)
            dve.wait_ge(sem("g1_rows"), 2)
            for half in range(2):
                p = step["out2"] + half
                for t in range(TT):
                    pair_wait(dve, p, t)
                    xs = x[:, t, half * COL:(half + 1) * COL]
                    tmp = XN3[:, t, half * COL:(half + 1) * COL]
                    V_.tensor_tensor(tmp, G1[:, half * COL:(half + 1) * COL], bank(p, t), ALU.mult).then_inc(freed[p % 2], 1)
                    dve.wait_ge(freed[p % 2], 2 * (p // 2) + t + 1)
                    V_.tensor_tensor(xs, xs, tmp, ALU.add).then_inc(sem("x_3"), 1)
                    dve.wait_ge(sem("x_3"), 2 * half + t + 1)
            norm_rows("x4", x, XN3, True)
            cols("x4", hTb, scale=lambda k: modT[:, 3, k, 0:1], shift=lambda k: modT[:, 2, k, 0:1])

            dve.wait_ge(sem("logits"), 1)
            L = ms[:, 0:40].rearrange("p (t n) -> p t n", t=TT)
            V_.tensor_tensor(L, PM[:, 0, 0:40].rearrange("p (t n) -> p t n", t=TT), rb[:, :].unsqueeze(1).to_broadcast([P, TT, 20]),
                             ALU.add).then_inc(sem("logits_read"), 1)
            dve.wait_ge(sem("logits_read"), 1)
            lg, le = L[:, :, 0:4], L[:, :, 4:20]
            rev = tab("rev").unsqueeze(1).to_broadcast([P, TT, 4])

            def small(s, n):
                return ms[:, s:s + TT * n].rearrange("p (t n) -> p t n", t=TT) if n > 1 else ms[:, s:s + TT]

            def spread(v, n=4):
                return v.unsqueeze(2).to_broadcast([P, TT, n])

            def first_max(src, top, hot, tmp):
                link(V_.tensor_reduce(top, src, AX.X, ALU.max))
                link(V_.tensor_tensor(hot, src, spread(top), ALU.is_equal))
                link(V_.tensor_tensor(hot, hot, rev, ALU.mult))
                link(V_.tensor_reduce(tmp, hot, AX.X, ALU.max))
                link(V_.tensor_tensor(hot, hot, spread(tmp), ALU.is_equal))

            gmax, ghot, t1 = small(40, 1), small(44, 4), small(42, 1)
            first_max(lg, gmax, ghot, t1)
            V_.tensor_tensor(small(72, 4), lg, spread(gmax), ALU.subtract).then_inc(sem("route_d"), 1)
            prod = ms[:, 144:176].rearrange("p (t g e) -> p t g e", t=TT, g=4)
            for t in range(TT):
                link(V_.tensor_tensor(prod[:, t], le[:, t, :].rearrange("p (g e) -> p g e", g=4),
                                      ghot[:, t, :].unsqueeze(2).to_broadcast([P, 4, 4]), ALU.mult))
            leg = small(52, 4)
            for t in range(TT):
                link(V_.tensor_reduce(leg[:, t, :], prod[:, t].rearrange("p g e -> p e g"), AX.X, ALU.add))
            v1, h1, v2, h2 = small(60, 1), small(92, 4), small(62, 1), small(100, 4)
            first_max(leg, v1, h1, t1)
            rest = small(108, 4)
            link(V_.scalar_tensor_tensor(rest, h1, NEG, leg, ALU.mult, ALU.add))
            first_max(rest, v2, h2, t1)
            V_.tensor_tensor(small(128, 1), v2, v1, ALU.subtract).then_inc(sem("route_r"), 1)
            dve.wait_ge(sem("route_e"), 1)
            wg = small(64, 1)
            link(V_.tensor_reduce(wg, small(80, 4), AX.X, ALU.add))
            dve.wait_ge(sem("route_e"), 2)
            r = small(130, 1)
            den, w1, w2 = small(66, 1), small(68, 1), small(70, 1)
            link(V_.tensor_scalar(den, r, 1.0, None, ALU.add))
            link(V_.tensor_tensor(den, den, wg, ALU.mult))
            link(V_.reciprocal(w1, den))
            link(V_.tensor_tensor(w2, w1, r, ALU.mult))
            link(V_.tensor_tensor(h1, h1, spread(w1), ALU.mult))
            link(V_.tensor_tensor(h2, h2, spread(w2), ALU.mult))
            link(V_.tensor_tensor(h1, h1, h2, ALU.add))
            gates = ms[:, 176:208].rearrange("p (t g e) -> p t g e", t=TT, g=4)
            for t in range(TT):
                link(V_.tensor_tensor(gates[:, t], ghot[:, t, :].unsqueeze(2).to_broadcast([P, 4, 4]),
                                      h1[:, t, :].unsqueeze(1).to_broadcast([P, 4, 4]), ALU.mult))

            def add_expert(e):
                for t in range(TT):
                    g = ms[:, 176 + t * NEXP + e:177 + t * NEXP + e]
                    for half in range(2):
                        n = 4 * e + 2 * t + half
                        dve.wait_ge(sem("expert_made"), n + 1)
                        acc = ACC[:, t, half * COL:(half + 1) * COL]
                        if e >= 1:
                            dve.wait_ge(sem("added"), n - 3)
                        if e == 0:
                            V_.tensor_scalar(acc, PM[:, 2 * t + half, :], g, None, ALU.mult).then_inc(sem("added"), 1)
                        else:
                            V_.scalar_tensor_tensor(acc, PM[:, 2 * t + half, :], g, acc, ALU.mult, ALU.add).then_inc(sem("added"), 1)

            for e in range(NEXP):
                p = step["exp"] + 2 * e + 1
                dve.wait_ge(sem("exp_silu"), 2 * e + 2)
                if e >= 2:
                    dve.wait_ge(sem("expert_made"), 4 * (e - 1))
                for b in range(2):
                    pair_wait(dve, p, b)
                    V_.tensor_tensor(ET[:, e % 2, 2 * b:2 * b + 2, :], SL[:, e % 2, 2 * b:2 * b + 2, :],
                                     bank(p, b).rearrange("p (j q) -> p j q", j=2), ALU.mult).then_inc(sem("hidden"), 1)
                    dve.wait_ge(sem("hidden"), 2 * e + b + 1)
                    V_.nop().then_inc(freed[p % 2], 1)
                add_expert(e)
            dve.wait_ge(sem("added"), 4 * NEXP)
            dve.wait_ge(sem("g2_rows"), 2)
            for t in range(TT):
                link(V_.tensor_tensor(ACC[:, t, :], ACC[:, t, :], G2, ALU.mult))
                V_.tensor_tensor(x[:, t, :], x[:, t, :], ACC[:, t, :], ALU.add).then_inc(sem("x_4"), 1)
            norm_rows("last", x, XN3, False)
            dve.wait_ge(sem("late_in"), 80)
            for t in range(TT):
                V_.tensor_tensor(XN3[:, t, :], XN3[:, t, :], FINAL, ALU.mult).then_inc(sem("out_ready"), 1)


_INS = ["x", "norm_mix_g", "w_in", "w_conv", "w_spatial", "b_spatial", "gmlp_ln_g", "gmlp_ln_b", "fox_q_norm_g",
        "fox_k_norm_g", "fox_forget_b", "w_branch", "w_out", "norm_ffn_g", "w_ffn_in", "w_ffn_out", "c_2", "ctx_2",
        "c_ctx_2", "w_mod_2", "b_mod_2", "norm1_g_2", "norm2_g_2", "w_in_2", "lam_q1_2", "lam_k1_2", "lam_q2_2",
        "lam_k2_2", "subln_g_2", "w_attn_out_2", "w_four_out_2", "w_out_2", "w_router_group_2", "b_router_group_2",
        "w_router_expert_2", "b_router_expert_2", "w_exp_gate_2", "w_exp_up_2", "w_exp_down_2", "final_g_2"]


def kernel(**inputs):
    import numpy as _np
    import concourse.bacc as _bacc
    from concourse.bass_utils import run_bass_kernel_spmd as _run

    nc = _bacc.Bacc("TRN2", target_bir_lowering=False, num_devices=1)
    arrays = {f"in_{n}_dram": _np.ascontiguousarray(inputs[n]) for n in _INS}
    arrays["in_tables_dram"] = TABLES
    a = {n: nc.dram_tensor(f"in_{n}_dram", arrays[f"in_{n}_dram"].shape, F32, kind="ExternalInput").ap()
         for n in [*_INS, "tables"]}
    out = nc.dram_tensor("out_0_dram", (1, SEQ, D), F32, kind="ExternalOutput").ap()
    block_pair_kernel(nc, a, out)
    r = _run(nc, [arrays], core_ids=[0])
    return r.results[0]["out_0_dram"]
```

```python
from contextlib import ExitStack

import numpy as np
import concourse.bass as bass
from concourse import mybir

F32 = mybir.dt.float32
F32R = mybir.dt.float32r
ALU = mybir.AluOpType
ACT = mybir.ActivationFunctionType
AX = mybir.AxisListType

P = 128
D = 1024
SEQ = 256
KT = D // P
TT = SEQ // P
MIX = 256
FFN = 2816
FT_TILES = FFN // P
FFN_GROUPS = -(-FFN // 512)
HEADS1 = 4
HD = 64
HEADS2 = 8
NEXP = 16
HID = 512
EPS = 1e-6
NEG = -1e30
COL = 512
SLOT = 4 * COL
RING = 4
UNIT = 2 * COL
UNITS = 4

W_IN_STARTS = (0, 512, 1024, 1536, 2048, 2560)
F_RAW = 2816
GATE_RAW = 2820
Q_OFF, K_OFF, V_OFF, F_OFF, GA_OFF, GF_OFF = 0, 1024, 2048, 3072, 3584, 4608


def shape_tables():
    i = np.arange(P)
    parts = {}
    parts["ident"] = np.eye(P)
    parts["upto"] = (i[:, None] <= i[None, :]) * 1.0
    parts["ones"] = np.ones((P, P))
    parts["from"] = (i[:, None] >= i[None, :]) * 1.0
    strict = (i[:, None] < i[None, :]) * 1.0
    parts["strict"] = np.concatenate([strict, np.ones((P, P)), strict], 1)
    parts["strict_neg"] = np.where(parts["strict"] > 0, 0.0, NEG)
    parts["causal_neg"] = np.where(i[None, :] <= i[:, None], 0.0, NEG)
    turn = np.zeros((P, P))
    for b in range(0, P, 32):
        for j in range(16):
            turn[b + 16 + j, b + j] = -1.0
            turn[b + j, b + 16 + j] = 1.0
    parts["turn"] = turn
    inv = (1.0 / (np.float32(10000.0) ** (np.arange(16, dtype=np.float32) / np.float32(16)))).astype(np.float32)
    tok = np.arange(SEQ)
    row = (tok // 64).astype(np.float32)
    col = (tok % 64).astype(np.float32)
    d = i % 64
    angle = np.where((d < 32)[:, None], row[None, :] * inv[d % 16][:, None], col[None, :] * inv[d % 16][:, None])
    parts["cos"] = np.cos(angle.astype(np.float64))
    parts["sin"] = np.sin(angle.astype(np.float64))
    w = 2 * np.pi * np.outer(tok, tok) / SEQ
    dft = np.concatenate([np.cos(w), np.sin(w)], 1) / np.sqrt(SEQ)
    parts["dft_tok"] = dft.reshape(TT, P, 2 * SEQ).transpose(1, 0, 2).reshape(P, -1)
    w = 2 * np.pi * np.outer(i, i) / P
    parts["dft_cos"] = np.cos(w) / np.sqrt(P)
    parts["dft_nsin"] = -np.sin(w) / np.sqrt(P)
    parts["rev"] = np.tile(np.array([4.0, 3.0, 2.0, 1.0]), (P, 1))
    at, start = {}, 0
    for name, a in parts.items():
        at[name] = (start, a.shape[1])
        start += a.shape[1]
    return np.concatenate(list(parts.values()), 1).astype(np.float32), at


TABLES, TABLE_AT = shape_tables()

ROWS = {}
for _name, _n in (("norm_mix_g", 8), ("norm_ffn_g", 8), ("norm1_g_2", 8), ("norm2_g_2", 8), ("c_2", 8),
                  ("c_ctx_2", 8), ("b_mod_2", 48), ("w_conv", 6)):
    ROWS[_name] = (sum(n for _, n in ROWS.values()), _n)
N_ROWS = sum(n for _, n in ROWS.values())


def plan_chunks(a):
    def cols(w, start, n=COL):
        return w[:, start:start + n].rearrange("(k p) n -> p k n", p=P)

    w_in, w_ffn, w_in2, w_mod = a["w_in"][0], a["w_ffn_in"][0], a["w_in_2"][0], a["w_mod_2"][0]
    out = [("in", cols(w_in, s, min(COL, GATE_RAW - s))) for s in W_IN_STARTS]
    out += [("gate", cols(w_in, GATE_RAW + COL * i)) for i in range(8)]
    wb = a["w_branch"][0].rearrange("n c d -> (n c) d")
    out += [("branch", cols(wb, COL * h)) for h in range(2)]
    out += [("out1", cols(a["w_out"][0], COL * h)) for h in range(2)]
    wo = a["w_ffn_out"][0]

    def ffn(kind, i):
        n = min(COL, FFN - COL * i)
        if kind == "ffn_o":
            return kind, wo[COL * i:COL * i + n, :].rearrange("(k p) n -> p k n", p=P)
        return kind, cols(w_ffn, COL * i + (FFN if kind == "ffn_u" else 0), n)

    out.append(ffn("ffn_g", 0))
    for i in range(FFN_GROUPS):
        out.append(ffn("ffn_u", i))
        if i + 1 < FFN_GROUPS:
            out.append(ffn("ffn_g", i + 1))
        out.append(ffn("ffn_o", i))
    out += [("mod_T", cols(w_mod, D * part + COL * h)) for part in (0, 1, 3, 4) for h in range(2)]
    for name, start, n in (("q", Q_OFF, 2), ("k", K_OFF, 2), ("v", V_OFF, 2), ("f", F_OFF, 1), ("g2", GA_OFF, 4)):
        out += [(name, cols(w_in2, start + COL * i)) for i in range(n)]
    out += [("mod_g1", cols(w_mod, 2 * D + COL * h)) for h in range(2)]
    out.append(("fo", a["w_four_out_2"][0].rearrange("(k p) n -> p k n", p=P)))
    out += [("ao", cols(a["w_attn_out_2"][0], COL * h)) for h in range(2)]
    out += [("out2", cols(a["w_out_2"][0], COL * h)) for h in range(2)]
    out += [("mod_g2", cols(w_mod, 5 * D + COL * h)) for h in range(2)]
    gate, up, down = (a[f"w_exp_{n}_2"][0] for n in ("gate", "up", "down"))
    out.append(("eg", cols(gate[0], 0)))
    for e in range(NEXP):
        out.append(("eu", cols(up[e], 0)))
        if e + 1 < NEXP:
            out.append(("eg", cols(gate[e + 1], 0)))
        out.append(("ed", down[e].rearrange("(k p) n -> p k n", p=P)))
    return out


def plan_units(chunks):
    pieces, units, of_chunk = [], [], []
    for c, (name, src) in enumerate(chunks):
        _, ks, n = src.shape
        split = not name.startswith("mod")
        per_piece = 4 if n <= COL else 2
        per_unit = per_piece // 2 if split else per_piece
        maker = None if not split else "dve" if name in ("ffn_g", "ffn_u", "ffn_o", "eg", "eu", "ed") else "pool"
        of_chunk.append([])
        for k0 in range(0, ks, per_piece):
            kn = min(per_piece, ks - k0)
            pieces.append(dict(chunk=c, k0=k0, ks=kn, n=n, units=[]))
            for k in range(k0, k0 + kn, per_unit):
                pieces[-1]["units"].append(len(units))
                of_chunk[c].append(len(units))
                units.append(dict(piece=len(pieces) - 1, chunk=c, k0=k, ks=min(per_unit, k0 + kn - k), n=n, maker=maker))
    counts = dict(split=0, dve=0, pool=0, used=0)
    for u, unit in enumerate(units):
        if unit["maker"]:
            unit["split"] = counts["split"]
            unit["lo"] = counts[unit["maker"]]
            counts["split"] += 1
            counts[unit["maker"]] += 1
            if u != of_chunk[unit["chunk"]][-1] and chunks[unit["chunk"]][0] != "branch":
                unit["used"] = counts["used"]
                counts["used"] += 1
    return pieces, units, of_chunk


def block_pair_kernel(nc, a, out):
    chunks = plan_chunks(a)
    pieces, units, units_of = plan_units(chunks)
    index = {}
    for i, (name, _) in enumerate(chunks):
        index.setdefault(name, []).append(i)
    split_units = [u for u, unit in enumerate(units) if unit["maker"]]

    ctx = ExitStack()
    with ctx:
        def sb(name, shape, dt=F32):
            return ctx.enter_context(nc.sbuf_tensor(name, shape, dt))

        sems = {}

        def sem(name):
            if name not in sems:
                sems[name] = ctx.enter_context(nc.semaphore(name))
            return sems[name]

        ring = sb("ring", [P, RING * SLOT])
        tables = sb("tables_sb", [P, TABLES.shape[1]])
        x = sb("x_sb", [P, TT, D])
        w_hi = sb("w_hi", [P, UNITS * UNIT], F32R)
        w_lo = sb("w_lo", [P, UNITS * UNIT], F32R)
        acts = sb("acts", [P, 10240], F32R)
        arena = sb("arena", [P, 19456])
        feat_cols = sb("feat_cols", [P, N_ROWS])
        lnw = sb("lnw", [P, 2, MIX])
        qk_g = sb("qk_g", [P, 2, HD])
        subln = sb("subln", [P, P])
        bs = sb("bs", [P, 2, P])
        bf = sb("bf", [P, HEADS1])
        rb = sb("rb", [P, 20])
        modT = sb("modT", [P, 4, KT, 2])
        silu_c = sb("silu_c", [P, KT, 2])
        half_root = sb("half_root", [P, 16])
        st = sb("st", [P, 416])
        PG = ctx.enter_context(nc.psum_tensor("gemm_ps", [P, 4, 512], F32))
        PM = ctx.enter_context(nc.psum_tensor("mix_ps", [P, 4, 512], F32))

        def at(start, *dims):
            n = int(np.prod(dims))
            v = arena[:, start:start + n]
            if len(dims) == 1:
                return v
            names = "abcd"[:len(dims)]
            return v.rearrange(f"p ({' '.join(names)}) -> p {' '.join(names)}", **dict(zip(names, dims)))

        def tab(name, *dims):
            s, n = TABLE_AT[name]
            v = tables[:, s:s + n]
            if not dims:
                return v
            names = "abcd"[:len(dims)]
            return v.rearrange(f"p ({' '.join(names)}) -> p {' '.join(names)}", **dict(zip(names, dims)))

        def feat(name, j=0):
            s, _ = ROWS[name]
            return feat_cols[:, s + j:s + j + 1]

        def feats(name, j, n):
            s, _ = ROWS[name]
            return feat_cols[:, s + j:s + j + n]

        ident = tab("ident")
        ones = tab("ones")

        CB, CC = at(6144, 2, SEQ), at(6656, 2, SEQ)
        XC = at(7168, 2, SEQ + 2)
        U, V = at(7688, 2, SEQ), at(8200, TT, MIX)
        SQ, SK, SV = at(8712, 2, SEQ), at(9224, 2, SEQ), at(9736, TT, MIX)
        FQK = at(10248, TT, 512)
        FV = at(11272, TT, MIX)
        FR = at(11784, TT, HEADS1)
        T1, T2, T3 = at(11800, 4, 384), at(13336, 4, 384), at(14872, 4, 384)
        FT = at(16408, 4, SEQ)
        WS, WST = at(16408, 4, P), at(17432, 4, P)
        NLF = at(17944, 2, HEADS1, P)
        VROWS = at(17944, P)
        lamv = at(18968, 4, HD)
        XN = at(11800, TT, D)
        JUNK = at(14872, D)
        TMP = at(14872, TT, COL)
        TF = at(0, KT, SEQ)
        SILU = at(2048, 2, 4, SEQ)

        def sg(c, t):
            return at(c * 1024 + t * COL if c < 6 else (17944, 16408)[c - 6] + t * COL, COL)

        QT = at(0, KT, SEQ)
        KTT = at(2048, KT, 2 * SEQ)
        V2 = at(6144, 4, D)
        SG2 = at(10240, TT, 2 * D)
        O = at(14336, TT, D)
        FN = at(14336, TT, COL)
        DT = at(15360, 2, 512)
        PP = at(16384, 2, 2, 512)
        RAW = at(16384, 2, 2, SEQ)
        ROT = at(17408, 2, 2, SEQ)
        AA = at(18432, 2, 512)
        CTX = at(14336, TT, D)
        XN2, JUNK2 = at(16384, TT, D), at(18432, D)
        SB = at(0, KT, P)
        G1 = at(1024, D)
        Y = at(2048, TT, D)
        XN3 = at(4096, TT, D)
        G2 = at(6144, D)
        JUNK3 = at(0, D)
        TF2 = at(8192, KT, SEQ)
        ACC = at(2048, TT, D)
        BM = at(16384, 2, D)
        FINAL = at(18432, D)
        wr = at(7168, KT, 20)
        SL = at(10240, 2, 4, SEQ)

        place = acts[:, 0:8192].rearrange("p (r h k q) -> p r h k q", r=2, h=2, k=KT)
        four = acts[:, 8192:10240].rearrange("p (h k q) -> p h k q", h=2, k=4)

        def hidden_at(r):
            return acts[:, 4096 * r:4096 * (r + 1)].rearrange("p (b h k q) -> p b h k q", b=2, h=2, k=4)

        ss = st[:, 0:16]
        rs = st[:, 16:32]
        gm = st[:, 32:64]
        fs = st[:, 64:160]
        ds = st[:, 160:208]
        ms = st[:, 208:416]

        def raw(i):
            q = pieces[i]
            s = i % RING * SLOT
            return ring[:, s:s + q["ks"] * q["n"]].rearrange("p (k n) -> p k n", k=q["ks"])

        def raw_unit(u):
            unit = units[u]
            k = unit["k0"] - pieces[unit["piece"]]["k0"]
            return raw(unit["piece"])[:, k:k + unit["ks"], :]

        def part(w, u):
            unit = units[u]
            b = unit["split"] % UNITS * UNIT
            return w[:, b:b + unit["ks"] * unit["n"]].rearrange("p (k n) -> p k n", k=unit["ks"])

        landed = [sem(f"landed{s}") for s in range(RING)]
        hi_made = sem("hi_made")
        lo_made = {"dve": sem("lo_by_vector"), "pool": sem("lo_by_gpsimd")}

        def landed_wait(eng, i):
            eng.wait_ge(landed[i % RING], 16 * (i // RING + 1))

        def make_hi(act, u):
            unit = units[u]
            landed_wait(act, unit["piece"])
            if unit["split"] >= UNITS:
                act.wait_ge(*unit_done(split_units[unit["split"] - UNITS]))
            nc.scalar.activation(part(w_hi, u), raw_unit(u), ACT.Copy).then_inc(hi_made, 1)

        def make_lo(eng, u):
            unit = units[u]
            eng.wait_ge(hi_made, unit["split"] + 1)
            eng.tensor_tensor(part(w_lo, u), raw_unit(u), part(w_hi, u), ALU.subtract).then_inc(lo_made[unit["maker"]], 1)

        step = {}
        n_steps = 0
        for name, n in (("in", 6), ("gate", 8), ("branch", 8), ("out1", 2), ("ffn", 12),
                        ("mod_T", 8), ("q", 2), ("k", 4), ("v", 4), ("f", 1), ("g2", 4), ("mod_g1", 2),
                        ("y", 4), ("out2", 2), ("mod_g2", 2), ("exp", 2 * NEXP)):
            step[name] = n_steps
            n_steps += n
        made = [sem("pair0_made"), sem("pair1_made")]
        freed = [sem("pair0_freed"), sem("pair1_freed")]

        def pair_wait(eng, p, bank):
            eng.wait_ge(made[p % 2], 2 * (p // 2) + 1 + bank)

        def pair_free_wait(eng, p):
            if p >= 2:
                eng.wait_ge(freed[p % 2], 2 * (p // 2))

        def bank(p, b):
            return PG[:, 2 * (p % 2) + b, :]

        TURN = {"x1": 0, "merged": 1, "x2": 2, "ctx": 3, "x3": 4, "heads": 5, "y2": 6, "x4": 7}
        rows_ready, turned = sem("rows_ready"), sem("turned")
        cols_dve, cols_act = sem("cols_by_vector"), sem("cols_by_scalar")
        NORM = {"x1": 0, "x2": 1, "ctx": 2, "x3": 3, "x4": 4, "last": 5}
        squares = sem("squares")

        block = ctx.enter_context(nc.Block())

        def last_product(i):
            def of_step(p):
                return made[p % 2], 2 * (p // 2) + 2
            name = chunks[i][0]
            c = index[name].index(i)
            if name == "ffn_o":
                return sem("ffn_made"), c + 1
            if name == "ed":
                return sem("expert_made"), 4 * (c + 1)
            steps = {"branch": step["branch"] + 4 * c + 3, "k": step["k"] + 2 * c + 1, "v": step["v"] + 2 * c + 1,
                     "fo": step["y"] + 1, "ao": step["y"] + 2 + c, "ffn_g": step["ffn"] + 2 * c,
                     "ffn_u": step["ffn"] + 2 * c + 1, "eg": step["exp"] + 2 * c, "eu": step["exp"] + 2 * c + 1}
            return of_step(steps[name] if name in steps else step[name] + c)

        def unit_done(u):
            unit = units[u]
            if "used" in unit:
                return sem("unit_used"), unit["used"] + 1
            if chunks[unit["chunk"]][0] == "branch":
                p = step["branch"] + 4 * index["branch"].index(unit["chunk"]) + unit["k0"] // 2
                return made[p % 2], 2 * (p // 2) + 2
            return last_product(unit["chunk"])

        @block.sync
        def _(sp):
            for i, q in enumerate(pieces):
                if i >= RING:
                    u = pieces[i - RING]["units"][-1]
                    if units[u]["maker"]:
                        sp.wait_ge(lo_made[units[u]["maker"]], units[u]["lo"] + 1)
                    else:
                        sp.wait_ge(*last_product(units[u]["chunk"]))
                src = chunks[q["chunk"]][1][:, q["k0"]:q["k0"] + q["ks"], :]
                sp.dma_start(raw(i), src).then_inc(landed[i % RING], 16)
            for t in range(TT):
                sp.wait_ge(sem("out_ready"), t + 1)
                sp.dma_start(out[0, t * P:(t + 1) * P, :], XN3[:, t, :]).then_inc(sem("out_sent"), 16)
            sp.wait_ge(sem("out_sent"), 16 * TT)

        @block.gpsimd
        def _(pool):
            def load(dst, src, name, n=16):
                pool.dma_start(dst, src).then_inc(sem(name), n)

            pool.memset(half_root[:, :], -0.5).then_inc(sem("exponent"), 1)
            pool.memset(XC[:, :, 0:2], 0.0).then_inc(sem("pad_ready"), 1)
            for n, (first, count) in ROWS.items():
                v = a[n]
                if n == "w_conv":
                    v = v[0].rearrange("k (j p) -> (k j) p", p=P)
                elif len(v.shape) == 1:
                    v = v.rearrange("(j p) -> j p", p=P)
                else:
                    v = v[0].rearrange("(j p) -> j p", p=P)
                load(VROWS[first:first + count, :], v, "vec_rows")
            load(WS, a["w_spatial"][0].rearrange("g t s -> t g s"), "ws_in")
            load(lnw[:, 0, :], a["gmlp_ln_g"].partition_broadcast(P), "small")
            load(lnw[:, 1, :], a["gmlp_ln_b"].partition_broadcast(P), "small")
            load(qk_g[:, 0, :], a["fox_q_norm_g"].partition_broadcast(P), "small")
            load(qk_g[:, 1, :], a["fox_k_norm_g"].partition_broadcast(P), "small")
            for g in range(4):
                h = 64 * (g % 2)
                load(bs[h:h + 64, g // 2, :], a["b_spatial"][0, g:g + 1, :].partition_broadcast(64), "small")
            load(bf[:, :], a["fox_forget_b"].partition_broadcast(P), "small")
            load(subln[:, :], a["subln_g_2"].partition_broadcast(P), "small2")
            for j, n in enumerate(("lam_q1_2", "lam_k1_2", "lam_q2_2", "lam_k2_2")):
                load(lamv[:, j, :], a[n].partition_broadcast(P), "small2")
            load(rb[:, 0:4], a["b_router_group_2"].partition_broadcast(P), "small2")
            load(rb[:, 4:20], a["b_router_expert_2"].partition_broadcast(P), "small2")
            pool.wait_ge(sem("exponent"), 1)
            roots = [0]

            def root(v):
                roots[0] += 1
                pool.wait_ge(sem("var_ready"), roots[0])
                nc.gpsimd.tensor_tensor(v, v, half_root[:, 0:v.shape[1]], ALU.pow).then_inc(sem("root_ready"), 1)

            def norm_roots(name):
                for t in range(TT):
                    j = 2 * NORM[name] + t
                    root(rs[:, j:j + 1])

            at_unit = [0]

            def lo_up_to(u):
                while at_unit[0] <= u:
                    if units[at_unit[0]]["maker"] == "pool":
                        make_lo(pool, at_unit[0])
                    at_unit[0] += 1

            def end_of(name, c=-1):
                return units_of[index[name][c]][-1]

            lo_up_to(units_of[0][-1])
            norm_roots("x1")
            lo_up_to(end_of("in", 2) + 3)
            root(gm[:, 2:4])
            lo_up_to(end_of("in", 4) + 3)
            root(fs[:, 40:56])
            lo_up_to(end_of("out1"))
            norm_roots("x2")
            pool.wait_ge(sem("ffn_hidden"), FFN_GROUPS)
            load(CTX, a["ctx_2"][0].rearrange("(t p) d -> p t d", p=P), "ctx_in")
            lo_up_to(units_of[index["q"][0]][-1])
            norm_roots("ctx")
            norm_roots("x3")
            lo_up_to(end_of("g2"))
            pool.wait_ge(sem("heads_rows"), HEADS2 * TT)
            load(BM[0:1, 0, :], a["b_mod_2"][:, 2 * D:3 * D], "late_in")
            load(BM[0:1, 1, :], a["b_mod_2"][:, 5 * D:6 * D], "late_in")
            load(FINAL, a["final_g_2"].rearrange("(o n) -> o n", o=1).partition_broadcast(P), "late_in")
            load(wr[:, :, 0:4], a["w_router_group_2"][0].rearrange("(k p) n -> p k n", p=P), "late_in")
            load(wr[:, :, 4:20], a["w_router_expert_2"][0].rearrange("(k p) n -> p k n", p=P), "late_in")

            lo_up_to(units_of[index["fo"][0]][-1])
            root(ds[:, 32:48])
            lo_up_to(end_of("out2"))
            norm_roots("x4")
            norm_roots("last")

        @block.tensor
        def _(pe):
            mm = nc.tensor.matmul

            def bank_of(j, k):
                return PM[:, k // 2, (k % 2) * SEQ:(k % 2 + 1) * SEQ]

            def turn(name, src):
                j = TURN[name]
                pe.wait_ge(rows_ready, TT * (j + 1))
                for b in range(4):
                    for k in (2 * b, 2 * b + 1):
                        for t in range(TT):
                            last = nc.tensor.transpose(bank_of(j, k)[:, t * P:(t + 1) * P], src[:, t, k * P:(k + 1) * P], ident)
                    last.then_inc(turned, 1)

            def cols_ready(name):
                pe.wait_ge(cols_dve, 2 * (TURN[name] + 1))

            def product(c, outs, first=True, final=True):
                for u in units_of[c]:
                    product_unit(u, outs, first, final)

            def product_unit(u, outs, first, final):
                for _ in (0,):
                    unit = units[u]
                    pe.wait_ge(hi_made, unit["split"] + 1)
                    pe.wait_ge(lo_made[unit["maker"]], unit["lo"] + 1)
                    hi, lo = part(w_hi, u), part(w_lo, u)
                    at_end = u == units_of[unit["chunk"]][-1]
                    for dst, kind, x_of, sel, opens, (s, n) in outs:
                        for j in range(unit["ks"]):
                            k = unit["k0"] + j
                            a_, b_ = first and k == 0 and opens, final and at_end and j == unit["ks"] - 1
                            xh, xl, wh, wl = x_of(0, k), x_of(1, k), hi[:, j, sel], lo[:, j, sel]
                            if kind == "rows":
                                mm(dst, xh, wh, start=a_, stop=False, skip_group_check=True)
                                mm(dst, xh, wl, start=False, stop=False, skip_group_check=True)
                                last = mm(dst, xl, wh, start=False, stop=b_, skip_group_check=True)
                            else:
                                mm(dst, wh, xh, start=a_, stop=False, skip_group_check=True)
                                mm(dst, wh, xl, start=False, stop=False, skip_group_check=True)
                                last = mm(dst, wl, xh, start=False, stop=b_, skip_group_check=True)
                        if at_end and n:
                            last.then_inc(s, n)
                    if not at_end:
                        last.then_inc(sem("unit_used"), 1)

            def tokens(r, t, k0=0, src=None):
                v = place[:, r] if src is None else src
                return lambda h, k: v[:, h, k0 + k, t * P:(t + 1) * P]

            def rows(p, x_of, n=COL):
                return [(bank(p, t)[:, 0:n], "rows", x_of(t), slice(0, n), True, (made[p % 2], 1)) for t in range(TT)]

            def four_cols(p, r, tiles=4):
                return [(bank(p, m // 2)[:, m % 2 * SEQ:(m % 2 + 1) * SEQ], "cols", lambda h, k: place[:, r, h, k, :],
                         slice(m * P, (m + 1) * P), m % 2 == 0,
                         (made[p % 2], m % 2 * (2 if tiles == 2 else 1))) for m in range(tiles)]

            pe.wait_ge(sem("tables_in"), 16)
            pe.wait_ge(sem("vec_rows"), 16 * len(ROWS))
            nc.tensor.transpose(PM[:, 0, 0:N_ROWS], VROWS[0:N_ROWS, :], ident[0:N_ROWS, 0:N_ROWS]).then_inc(sem("consts_turned"), 1)
            pe.wait_ge(sem("ws_in"), 16)
            for g in range(4):
                last = nc.tensor.transpose(PM[:, 1, g * P:(g + 1) * P], WS[:, g, :], ident)
            last.then_inc(sem("consts_turned"), 1)
            pe.wait_ge(sem("consts_read"), 2)
            turn("x1", XN)
            cols_ready("x1")

            i = index["in"][0]
            for c in range(2):
                pair_free_wait(pe, step["in"] + c)
                product(i + c, four_cols(step["in"] + c, 0))
            halves = [slice(0, MIX), slice(MIX, 2 * MIX)]

            def half_rows(p, b, sel, inc=1):
                return [(bank(p, b)[:, t * MIX:(t + 1) * MIX], "rows", tokens(0, t), sel, t == 0, (made[p % 2], t * inc)) for t in range(TT)]

            def half_cols(p, b, start, inc=1):
                return [(bank(p, b)[:, m * SEQ:(m + 1) * SEQ], "cols", lambda h, k: place[:, 0, h, k, :],
                         slice(start + m * P, start + (m + 1) * P), m == 0, (made[p % 2], m * inc)) for m in range(2)]

            p = step["in"] + 2
            pair_free_wait(pe, p)
            product(i + 2, half_rows(p, 0, halves[0]) + half_cols(p, 1, MIX))
            p = step["in"] + 3
            pair_free_wait(pe, p)
            product(i + 3, half_cols(p, 0, 0) + half_rows(p, 1, halves[1]))
            for c in (4, 5):
                pair_free_wait(pe, step["in"] + c)
                product(i + c, rows(step["in"] + c, lambda t: tokens(0, t), n=chunks[i + c][1].shape[2]))

            def stick_scores():
                pe.wait_ge(sem("stick_qk"), 2)
                for hd in range(HEADS1):
                    r, j = HD * (hd % 2), hd // 2
                    mm(PM[:, hd, 0:SEQ], SK[r:r + HD, j, 0:P], SQ[r:r + HD, j, :], start=True, stop=True)
                    last = mm(PM[:, hd, SEQ:384], SK[r:r + HD, j, P:SEQ], SQ[r:r + HD, j, P:SEQ], start=True, stop=True)
                last.then_inc(sem("stick_z"), 1)

            def fox_turn():
                pe.wait_ge(sem("fox_qk"), 1)
                pe.wait_ge(sem("stick_z_read"), 1)
                for j in range(4):
                    for t in range(TT):
                        last = nc.tensor.transpose(PM[:, j // 2, (j % 2) * SEQ + t * P:(j % 2) * SEQ + (t + 1) * P],
                                                   FQK[:, t, j * P:(j + 1) * P], ident)
                last.then_inc(sem("fox_turned"), 1)

            def stick_sums():
                pe.wait_ge(sem("stick_l"), 1)
                pe.wait_ge(sem("fox_T"), 1)
                for hd in range(HEADS1):
                    mm(PM[:, hd, 0:384], tab("from"), T3[:, hd, :], start=True, stop=False)
                    last = mm(PM[:, hd, P:SEQ], ones, T3[:, hd, SEQ:384], start=False, stop=True)
                last.then_inc(sem("stick_c"), 1)

            def weigh(w, v, o, name):
                for hd in range(HEADS1):
                    r, j = HD * (hd % 2), hd // 2
                    dst = o[r:r + HD, j * SEQ:(j + 1) * SEQ]
                    mm(dst, v[:, 0, hd * HD:(hd + 1) * HD], w[:, hd, 0:SEQ], start=True, stop=False)
                    last = mm(dst[:, P:SEQ], v[:, 1, hd * HD:(hd + 1) * HD], w[:, hd, SEQ:384], start=False, stop=True)
                last.then_inc(sem(name), 1)

            def stick_out_and_spatial():
                pe.wait_ge(sem("stick_w"), 1)
                pe.wait_ge(sem("stick_v"), 1)
                weigh(T1, SV, PM[:, 0, :], "stick_o")
                pe.wait_ge(sem("spatial_v"), 1)
                for g in range(4):
                    r, j = HD * (g % 2), g // 2
                    for t in range(TT):
                        last = mm(PM[r:r + HD, 1, j * SEQ + t * P:j * SEQ + (t + 1) * P],
                                  V[:, t, g * HD:(g + 1) * HD], WST[:, g, :], start=True, stop=True)
                last.then_inc(sem("spatial_mix"), 1)

            def fox_scores():
                pe.wait_ge(sem("fox_f"), 1)
                pe.wait_ge(sem("stick_o_read"), 1)
                pe.wait_ge(sem("spatial_read"), 1)
                upto = tab("upto")
                s0, _ = TABLE_AT["upto"]
                upto_ones = tables[:, s0:s0 + 2 * P]
                for hd in range(HEADS1):
                    r, j = HD * (hd % 2), hd // 2
                    q = FT[r:r + HD, j, :]
                    k = FT[r:r + HD, 2 + j, :]
                    s = PM[:, hd, :]
                    mm(s[:, 0:P], q[:, 0:P], k[:, 0:P], start=True, stop=False)
                    mm(s[:, 0:P], NLF[:, 0, hd, :], upto, start=False, stop=False)
                    mm(s[:, 0:P], ident, tab("causal_neg"), start=False, stop=True)
                    mm(s[:, P:384], q[:, P:SEQ], k, start=True, stop=False)
                    mm(s[:, P:384], NLF[:, 0, hd, :], upto_ones, start=False, stop=False)
                    mm(s[:, SEQ:384], NLF[:, 1, hd, :], upto, start=False, stop=False)
                    mm(s[:, SEQ:384], ident, tab("causal_neg"), start=False, stop=True)
                f = PM[:, 0, 384:392]
                mm(f[:, 0:4], upto, NLF[:, 0, :, 0], start=True, stop=True)
                mm(f[:, 4:8], ones, NLF[:, 0, :, 0], start=True, stop=False)
                mm(f[:, 4:8], upto, NLF[:, 1, :, 0], start=False, stop=True).then_inc(sem("fox_s"), 1)

            def fox_probs_turn():
                pe.wait_ge(sem("fox_p"), 1)
                for hd in range(HEADS1):
                    for b in range(3):
                        last = nc.tensor.transpose(PM[:, hd, b * P:(b + 1) * P], T2[:, hd, b * P:(b + 1) * P], ident)
                last.then_inc(sem("fox_p_turned"), 1)

            def fox_out():
                pe.wait_ge(sem("fox_pT"), 1)
                weigh(T3, FV, PM[:, 0, :], "fox_o")

            between = {0: stick_scores, 1: fox_turn, 2: stick_sums, 3: stick_out_and_spatial,
                       4: fox_scores, 5: fox_probs_turn, 6: fox_out}
            for c in range(8):
                pair_free_wait(pe, step["gate"] + c)
                product(index["gate"][c], rows(step["gate"] + c, lambda t: tokens(0, t)))
                if c in between:
                    between[c]()
            pe.wait_ge(sem("branch_T"), 4)
            for half in range(2):
                c = index["branch"][half]
                for u in units_of[c]:
                    unit = units[u]
                    n = unit["k0"] // 2
                    p = step["branch"] + 4 * half + n
                    pair_free_wait(pe, p)
                    pe.wait_ge(hi_made, unit["split"] + 1)
                    pe.wait_ge(lo_made[unit["maker"]], unit["lo"] + 1)
                    hi, lo = part(w_hi, u), part(w_lo, u)
                    for t in range(TT):
                        for k in range(2):
                            xh, xl = (place[:, 1, h, 2 * n + k, t * P:(t + 1) * P] for h in range(2))
                            mm(bank(p, t), xh, hi[:, k, :], start=(k == 0), stop=False)
                            mm(bank(p, t), xh, lo[:, k, :], start=False, stop=False)
                            last = mm(bank(p, t), xl, hi[:, k, :], start=False, stop=(k == 1))
                        last.then_inc(made[p % 2], 1)
            turn("merged", XN)
            cols_ready("merged")
            for half in range(2):
                pair_free_wait(pe, step["out1"] + half)
                product(index["out1"][half], rows(step["out1"] + half, lambda t: tokens(0, t)))
            turn("x2", XN)
            cols_ready("x2")

            def up(chunk, p, r):
                pair_free_wait(pe, p)
                product(chunk, four_cols(p, r, tiles=chunks[chunk][1].shape[2] // P))

            def down(r, e):
                return lambda t: tokens(None, t, src=hidden_at(r)[:, e % 2])

            up(index["ffn_g"][0], step["ffn"], 1)
            for c in range(FFN_GROUPS):
                up(index["ffn_u"][c], step["ffn"] + 2 * c + 1, 1)
                if c + 1 < FFN_GROUPS:
                    up(index["ffn_g"][c + 1], step["ffn"] + 2 * c + 2, 1)
                pe.wait_ge(sem("ffn_hidden"), c + 1)
                outs = [(PM[:, 2 * t + half, :], "rows", down(0, c)(t), slice(half * COL, (half + 1) * COL), True,
                         (sem("ffn_made"), t * half)) for t in range(TT) for half in range(2)]
                product(index["ffn_o"][c], outs, first=(c == 0), final=(c == FFN_GROUPS - 1))
            def whole(c):
                held = sorted({units[u]["piece"] for u in units_of[c]})
                for q in held:
                    landed_wait(pe, q)
                return lambda k: raw(held[k // 4])[:, k % 4, :]

            pe.wait_ge(sem("silu_c"), 1)
            for c in range(8):
                p = step["mod_T"] + c
                pair_free_wait(pe, p)
                w = whole(index["mod_T"][c])
                for m in range(4):
                    for k in range(KT):
                        last = mm(bank(p, 0)[:, 2 * m:2 * m + 2], w(k)[:, m * P:(m + 1) * P], silu_c[:, k, :], start=(k == 0), stop=(k == KT - 1))
                last.then_inc(made[p % 2], 2)
            pe.wait_ge(sem("x_2"), 4)
            turn("ctx", XN2)
            cols_ready("ctx")
            turn("x3", XN2)
            cols_ready("x3")
            for c in range(2):
                pair_free_wait(pe, step["q"] + c)
                product(index["q"][c], four_cols(step["q"] + c, 1))

            def rope_products(j):
                pe.wait_ge(sem("rope_raw"), j + 1)
                if j >= 2:
                    pe.wait_ge(sem("rope_done"), j - 1)
                mm(PM[:, j % 2, :], tab("turn"), RAW[:, j % 2, :, :], start=True, stop=True).then_inc(sem("rope_rot"), 1)

            for j in range(2):
                rope_products(j)
            for c in range(2):
                p = step["k"] + 2 * c
                if c == 1:
                    rope_products(2)
                    rope_products(3)
                pair_free_wait(pe, p)
                pair_free_wait(pe, p + 1)
                product(index["k"][c], [(bank(p + m // 2, m % 2), "cols", lambda h, k: place[:, :, h, k, :],
                                         slice(m * P, (m + 1) * P), True, (made[(p + m // 2) % 2], 1)) for m in range(4)])
            for c in range(2):
                p = step["v"] + 2 * c
                rope_products(4 + 2 * c)
                rope_products(5 + 2 * c)
                pair_free_wait(pe, p)
                pair_free_wait(pe, p + 1)
                product(index["v"][c], [(bank(p + t // 2, t % 2), "rows", tokens(t // 2, t % 2), slice(0, COL), True,
                                         (made[(p + t // 2) % 2], 1)) for t in range(4)])
            pair_free_wait(pe, step["f"])
            product(index["f"][0], rows(step["f"], lambda t: tokens(1, t)))
            pe.wait_ge(sem("four_rows"), 2)
            pe.wait_ge(sem("rope_done"), 8)
            dft = tab("dft_tok", TT, 512)
            for g in range(4):
                if g >= 2:
                    pe.wait_ge(sem("four_A"), g - 1)
                for t in range(TT):
                    last = mm(PM[:, g % 2, :], FN[:, t, g * P:(g + 1) * P], dft[:, t, :], start=(t == 0), stop=(t == 1))
                last.then_inc(sem("four_1"), 1)
                pe.wait_ge(sem("four_A"), g + 1)
                if g >= 2:
                    pe.wait_ge(sem("four_B"), g - 1)
                mm(PM[:, 2 + g % 2, 0:SEQ], tab("dft_cos"), DT[:, g % 2, 0:SEQ], start=True, stop=False)
                mm(PM[:, 2 + g % 2, 0:SEQ], tab("dft_nsin"), DT[:, g % 2, SEQ:512], start=False, stop=True).then_inc(sem("four_2"), 1)

            def scores(n):
                hd, t = n // TT, n % TT
                if n >= 1:
                    pe.wait_ge(sem("probs"), 2 * n)
                for c in range(2):
                    last = mm(PM[:, c, :], QT[c * HD:(c + 1) * HD, hd, t * P:(t + 1) * P], KTT[c * HD:(c + 1) * HD, hd, :], start=True, stop=True)
                last.then_inc(sem("scores"), 1)

            def probs_turn(n):
                pe.wait_ge(sem("diff"), n + 1)
                if n >= 1:
                    pe.wait_ge(sem("diff_T"), n)
                for k in range(4):
                    last = nc.tensor.transpose(PM[:, 2, k * P:(k + 1) * P], PP[:, n % 2, 0, k * P:(k + 1) * P], ident)
                last.then_inc(sem("diff_turned"), 1)

            def heads_out(n):
                hd, t = n // TT, n % TT
                pe.wait_ge(sem("diff_T"), n + 1)
                if n >= 1:
                    pe.wait_ge(sem("heads_rows"), n)
                for k in range(4):
                    last = mm(PM[:, 3, 0:P], AA[:, n % 2, k * P:(k + 1) * P], V2[:, k, hd * P:(hd + 1) * P], start=(k == 0), stop=(k == 3))
                last.then_inc(sem("heads_made"), 1)

            pe.wait_ge(sem("four_B"), 4)
            pe.wait_ge(sem("kv_ready"), 8)
            N = HEADS2 * TT
            for n in range(N + 2):
                if n < N:
                    c, q = n // 4, n % 4
                    p = step["g2"] + c
                    if q == 0:
                        pair_free_wait(pe, p)
                    product_unit(units_of[index["g2"][c]][q], rows(p, lambda t: tokens(1, t)), True, True)
                    scores(n)
                if 1 <= n <= N:
                    probs_turn(n - 1)
                if n >= 2:
                    heads_out(n - 2)

            def mod_rows(name, which):
                for c in range(2):
                    p = step[name] + c
                    pair_free_wait(pe, p)
                    w = whole(index[name][c])
                    for k in range(KT):
                        mm(bank(p, 0), SB[:, k, :], w(k), start=(k == 0), stop=False)
                    pe.wait_ge(sem("late_in"), 80)
                    mm(bank(p, 0), ones[0:1, :], BM[0:1, which, c * COL:(c + 1) * COL], start=False, stop=True).then_inc(made[p % 2], 2)

            pe.wait_ge(sem("sb_ready"), 1)
            mod_rows("mod_g1", 0)
            turn("heads", O)
            p = step["y"]
            pair_free_wait(pe, p)
            pair_free_wait(pe, p + 1)
            product(index["fo"][0], [(bank(p + half, t), "rows", tokens(None, t, src=four), slice(half * COL, (half + 1) * COL), True,
                                      (made[(p + half) % 2], 1)) for half in range(2) for t in range(TT)])
            cols_ready("heads")
            for half in range(2):
                pair_free_wait(pe, step["y"] + 2 + half)
                product(index["ao"][half], rows(step["y"] + 2 + half, lambda t: tokens(0, t)))
            turn("y2", Y)
            cols_ready("y2")
            for half in range(2):
                pair_free_wait(pe, step["out2"] + half)
                product(index["out2"][half], rows(step["out2"] + half, lambda t: tokens(1, t)))
            mod_rows("mod_g2", 1)
            turn("x4", XN3)
            cols_ready("x4")
            for t in range(TT):
                for k in range(KT):
                    last = mm(PM[:, 0, t * 20:(t + 1) * 20], TF2[:, k, t * P:(t + 1) * P], wr[:, k, :], start=(k == 0), stop=(k == KT - 1))
            last.then_inc(sem("logits"), 1)
            up(index["eg"][0], step["exp"], 0)
            for e in range(NEXP):
                up(index["eu"][e], step["exp"] + 2 * e + 1, 0)
                if e + 1 < NEXP:
                    up(index["eg"][e + 1], step["exp"] + 2 * e + 2, 0)
                pe.wait_ge(sem("hidden"), e + 1)
                if e == 0:
                    pe.wait_ge(sem("logits_read"), 1)
                else:
                    pe.wait_ge(sem("added"), 4 * e)
                product(index["ed"][e], [(PM[:, 2 * t + half, :], "rows", down(1, e)(t), slice(half * COL, (half + 1) * COL), True,
                                          (sem("expert_made"), 1)) for t in range(TT) for half in range(2)])

        @block.scalar
        def _(act):
            A = nc.scalar.activation
            chain = [0]

            def link(ins):
                chain[0] += 1
                ins.then_inc(sem("act_chain"), 1)
                act.wait_ge(sem("act_chain"), chain[0])

            at_unit = [0]

            def hi_up_to(u):
                while at_unit[0] <= min(u, len(units) - 1):
                    if units[at_unit[0]]["maker"]:
                        make_hi(act, at_unit[0])
                    at_unit[0] += 1

            def hi_for(name, c=-1):
                hi_up_to(units_of[index[name][c]][-1] + 3)

            def take(p, b, out, fn=ACT.Copy, src=None, **kw):
                pair_wait(act, p, b)
                A(out, bank(p, b) if src is None else src, fn, **kw).then_inc(freed[p % 2], 1)

            def norm_squares(name, src, junk):
                j = NORM[name]
                for t in range(TT):
                    A(junk, src[:, t, :], ACT.Square, accum_out=ss[:, 2 * j + t:2 * j + t + 1]).then_inc(squares, 1)
                    act.wait_ge(squares, 2 * j + t + 1)

            def cols(name, r, full, scale=None, shift=None):
                j = TURN[name]
                for k in range(4, KT):
                    if k % 2 == 0:
                        act.wait_ge(turned, 4 * j + k // 2 + 1)
                    src = PM[:, k // 2, (k % 2) * SEQ:(k % 2 + 1) * SEQ]
                    kw = {}
                    fn = ACT.Copy
                    if scale is not None:
                        kw["scale"] = scale(k)
                    if shift is not None:
                        kw["bias"] = shift(k)
                        fn = ACT.Identity
                    link(A(full[:, k, :], src, fn, **kw))
                A(place[:, r, 0, 4:KT, :], full[:, 4:KT, :], ACT.Copy).then_inc(cols_act, 1)

            act.dma_start(x[:, :, :], a["x"][0].rearrange("(t p) d -> p t d", p=P)).then_inc(sem("x_in"), 16)
            act.dma_start(tables[:, :], a["tables"]).then_inc(sem("tables_in"), 16)
            act.wait_ge(sem("x_in"), 16)
            norm_squares("x1", x, JUNK)
            hi_up_to(3)
            act.wait_ge(sem("consts_read"), 2)
            cols("x1", 0, TF, scale=lambda k: feat("norm_mix_g", k))

            p = step["in"]
            hi_for("in", 0)
            take(p, 0, CB)
            take(p, 1, CC)
            hi_for("in", 1)
            pair_wait(act, p + 1, 1)
            A(U, bank(p + 1, 1), ACT.Gelu_apprx_tanh).then_inc(freed[(p + 1) % 2], 1)
            hi_for("in", 2)
            pair_wait(act, p + 2, 0)
            A(V, bank(p + 2, 0), ACT.Gelu_apprx_tanh).then_inc(sem("v_gelu"), 1)
            act.wait_ge(sem("v_gelu"), 1)
            act.nop().then_inc(freed[(p + 2) % 2], 1)
            pair_wait(act, p + 2, 1)
            A(SQ, bank(p + 2, 1), ACT.Copy).then_inc(sem("stick_qk"), 1)
            act.wait_ge(sem("stick_qk"), 1)
            act.nop().then_inc(freed[(p + 2) % 2], 1)
            hi_for("in", 3)
            pair_wait(act, p + 3, 0)
            A(SK, bank(p + 3, 0), ACT.Copy).then_inc(sem("stick_qk"), 1)
            act.wait_ge(sem("stick_qk"), 2)
            act.nop().then_inc(freed[(p + 3) % 2], 1)
            pair_wait(act, p + 3, 1)
            A(SV, bank(p + 3, 1), ACT.Copy).then_inc(sem("stick_v"), 1)
            act.wait_ge(sem("stick_v"), 1)
            act.nop().then_inc(freed[(p + 3) % 2], 1)
            hi_for("in", 4)
            for t in range(TT):
                take(p + 4, t, FQK[:, t, :])
            hi_for("in", 5)
            for t in range(TT):
                pair_wait(act, p + 5, t)
                link(A(FV[:, t, :], bank(p + 5, t)[:, 0:MIX], ACT.Copy))
                A(FR[:, t, :], bank(p + 5, t)[:, MIX:MIX + 4], ACT.Copy).then_inc(freed[(p + 5) % 2], 1)

            def stick_softplus():
                act.wait_ge(sem("stick_z_read"), 1)
                link(A(T2, T1, ACT.Abs))
                link(A(T2, T2, ACT.Exp, scale=-1.0))
                A(T2, T2, ACT.Ln, bias=1.0).then_inc(sem("stick_ln"), 1)

            def fox_T():
                act.wait_ge(sem("fox_turned"), 1)
                link(A(FT[:, 0:2, :], PM[:, 0, :], ACT.Copy))
                A(FT[:, 2:4, :], PM[:, 1, :], ACT.Copy).then_inc(sem("fox_T"), 1)

            def fox_log():
                act.wait_ge(sem("fox_abs"), 1)
                f = fs[:, 0:8]
                link(A(f, FR.rearrange("p t h -> p (t h)"), ACT.Abs))
                link(A(f, f, ACT.Exp, scale=-1.0))
                A(f, f, ACT.Ln, bias=1.0).then_inc(sem("fox_ln"), 1)

            def stick_exp():
                act.wait_ge(sem("stick_logw"), 1)
                A(T1, T1, ACT.Exp).then_inc(sem("stick_w"), 1)

            def fox_exp():
                act.wait_ge(sem("fox_max"), 1)
                for hd in range(HEADS1):
                    for t in range(TT):
                        s = PM[:, hd, 0:P] if t == 0 else PM[:, hd, P:384]
                        d = T2[:, hd, 0:P] if t == 0 else T2[:, hd, P:384]
                        last = A(d, s, ACT.Exp, bias=fs[:, 24 + 4 * t + hd:25 + 4 * t + hd], accum_out=fs[:, 32 + 4 * t + hd:33 + 4 * t + hd])
                        last.then_inc(sem("fox_e"), 1)

            between = {0: (stick_softplus, fox_log), 1: (fox_T,), 2: (stick_exp,), 4: (fox_exp,)}
            for c in range(8):
                hi_for("gate", c)
                for t in range(TT):
                    take(step["gate"] + c, t, sg(c, t), ACT.Sigmoid)
                for f in between.get(c, ()):
                    f()
            hi_for("branch", 1)
            cols("merged", 0, TF)
            hi_for("out1", 1)
            act.wait_ge(sem("x_1"), 4)
            norm_squares("x2", x, JUNK)
            cols("x2", 1, TF, scale=lambda k: feat("norm_ffn_g", k))
            for c in range(6):
                p = step["ffn"] + 2 * c
                hi_for("ffn_g", c)
                if c >= 2:
                    act.wait_ge(sem("ffn_hidden"), c - 1)
                for b in range(2 if c < FFN_GROUPS - 1 else 1):
                    pair_wait(act, p, b)
                    A(SILU[:, c % 2, 2 * b:2 * b + 2, :], bank(p, b), ACT.Silu).then_inc(sem("silu_done"), 1)
                    act.wait_ge(sem("silu_done"), 2 * c + b + 1)
                    act.nop().then_inc(freed[p % 2], 1 if c < FFN_GROUPS - 1 else 2)
            hi_for("ffn_o")
            A(silu_c[:, :, 0], feats("c_2", 0, 8), ACT.Silu)
            A(silu_c[:, :, 1], feats("c_ctx_2", 0, 8), ACT.Silu).then_inc(sem("silu_c"), 1)
            act.wait_ge(sem("lam_sums"), 2)
            A(ds[:, 2:4], ds[:, 0:2], ACT.Exp).then_inc(sem("lam_exp"), 1)
            hi_up_to(units_of[index["q"][0]][-1])
            act.wait_ge(sem("ctx_in"), 16)
            norm_squares("ctx", CTX, JUNK2)
            act.wait_ge(sem("mod_cols"), 1)
            cols("ctx", 0, TF, scale=lambda k: modT[:, 1, k, 1:2], shift=lambda k: modT[:, 0, k, 1:2])
            act.wait_ge(sem("x_2"), 4)
            norm_squares("x3", x, JUNK2)
            cols("x3", 1, TF, scale=lambda k: modT[:, 1, k, 0:1], shift=lambda k: modT[:, 0, k, 0:1])

            for j in range(4):
                p = step["q"] + j // 2
                hi_for("q", j // 2)
                if j >= 2:
                    act.wait_ge(sem("rope_done"), j - 1)
                pair_wait(act, p, j % 2)
                A(RAW[:, j % 2, :, :], bank(p, j % 2), ACT.Copy).then_inc(sem("rope_raw"), 1)
                act.wait_ge(sem("rope_raw"), j + 1)
                act.nop().then_inc(freed[p % 2], 1)
            for j in range(4):
                p = step["k"] + j
                hi_for("k", j // 2)
                act.wait_ge(sem("rope_done"), 3 + j)
                for b in range(2):
                    pair_wait(act, p, b)
                    link(A(KTT[:, 2 * j + b, 0:SEQ], bank(p, b)[:, 0:SEQ], ACT.Copy))
                    ins = A(RAW[:, j % 2, b, :], bank(p, b)[:, SEQ:512], ACT.Copy)
                    if b == 0:
                        link(ins)
                    else:
                        ins.then_inc(sem("rope_raw"), 1)
                        act.wait_ge(sem("rope_raw"), 5 + j)
                    act.nop().then_inc(freed[p % 2], 1)
            for j in range(4):
                p = step["v"] + j
                hi_for("v", j // 2)
                for b in range(2):
                    pair_wait(act, p, b)
                    c = j // 2
                    A(V2[:, 2 * (j % 2) + b, c * COL:(c + 1) * COL], bank(p, b), ACT.Copy).then_inc(sem("v_copied"), 1)
                    act.wait_ge(sem("v_copied"), 2 * j + b + 1)
                    act.nop().then_inc(freed[p % 2], 1)
            act.nop().then_inc(sem("kv_ready"), 4)
            p = step["f"]
            hi_for("f")
            for t in range(TT):
                pair_wait(act, p, t)
                A(FN[:, t, :], bank(p, t), ACT.Copy).then_inc(sem("four_rows"), 1)
                act.wait_ge(sem("four_rows"), t + 1)
                act.nop().then_inc(freed[p % 2], 1)
            for g in range(4):
                act.wait_ge(sem("four_1"), g + 1)
                if g >= 2:
                    act.wait_ge(sem("four_2"), g - 1)
                A(DT[:, g % 2, :], PM[:, g % 2, :], ACT.Copy).then_inc(sem("four_A"), 1)

            N = HEADS2 * TT
            for n in range(N):
                hi_up_to(units_of[index["g2"][n // 4]][n % 4] + 3)
                act.wait_ge(sem("nmax"), n + 1)
                if n >= 2:
                    act.wait_ge(sem("diff_turned"), n - 1)
                for c in range(2):
                    A(PP[:, n % 2, c, :], PM[:, c, :], ACT.Exp, scale=HD ** -0.5, bias=ds[:, 16 + 2 * (n % 2) + c:17 + 2 * (n % 2) + c],
                      accum_out=ds[:, 20 + 2 * (n % 2) + c:21 + 2 * (n % 2) + c]).then_inc(sem("probs"), 1)
                if n % 4 == 3:
                    c = n // 4
                    for t in range(TT):
                        take(step["g2"] + c, t, SG2[:, t, c * COL:(c + 1) * COL], ACT.Sigmoid)
                if n >= 1:
                    act.wait_ge(sem("heads_made"), n)
                    m = n - 1
                    A(O[:, m % TT, (m // TT) * P:(m // TT + 1) * P], PM[:, 3, 0:P], ACT.Copy).then_inc(sem("heads_rows"), 1)
            act.wait_ge(sem("heads_made"), N)
            m = N - 1
            A(O[:, m % TT, (m // TT) * P:(m // TT + 1) * P], PM[:, 3, 0:P], ACT.Copy).then_inc(sem("heads_rows"), 1)
            hi_up_to(units_of[index["fo"][0]][-1])
            act.wait_ge(sem("heads_rows"), N)
            for c in range(2):
                p = step["mod_g1"] + c
                pair_wait(act, p, 1)
                A(G1[:, c * COL:(c + 1) * COL], bank(p, 0), ACT.Copy).then_inc(sem("g1_rows"), 1)
                act.wait_ge(sem("g1_rows"), c + 1)
                act.nop().then_inc(freed[p % 2], 2)
            cols("heads", 0, TF2)
            hi_for("ao", 1)
            cols("y2", 1, TF2)
            hi_for("out2", 1)
            for c in range(2):
                p = step["mod_g2"] + c
                pair_wait(act, p, 1)
                A(G2[:, c * COL:(c + 1) * COL], bank(p, 0), ACT.Copy).then_inc(sem("g2_rows"), 1)
                act.wait_ge(sem("g2_rows"), c + 1)
                act.nop().then_inc(freed[p % 2], 2)
            act.wait_ge(sem("x_3"), 4)
            norm_squares("x4", x, JUNK3)
            cols("x4", 0, TF2, scale=lambda k: modT[:, 3, k, 0:1], shift=lambda k: modT[:, 2, k, 0:1])
            act.wait_ge(sem("route_d"), 1)
            A(ms[:, 80:88], ms[:, 72:80], ACT.Exp).then_inc(sem("route_e"), 1)
            act.wait_ge(sem("route_r"), 1)
            A(ms[:, 130:132], ms[:, 128:130], ACT.Exp).then_inc(sem("route_e"), 1)
            for e in range(NEXP):
                p = step["exp"] + 2 * e
                hi_for("eg", e)
                if e >= 2:
                    act.wait_ge(sem("hidden"), e - 1)
                for b in range(2):
                    pair_wait(act, p, b)
                    A(SL[:, e % 2, 2 * b:2 * b + 2, :], bank(p, b), ACT.Silu).then_inc(sem("exp_silu"), 1)
                    act.wait_ge(sem("exp_silu"), 2 * e + b + 1)
                    act.nop().then_inc(freed[p % 2], 1)
            hi_up_to(len(units))
            act.wait_ge(sem("x_4"), 2)
            norm_squares("last", x, JUNK3)

        @block.vector
        def _(dve):
            V_ = nc.vector
            chain = [0]

            def link(ins):
                chain[0] += 1
                ins.then_inc(sem("vec_chain"), 1)
                dve.wait_ge(sem("vec_chain"), chain[0])

            roots = [0]

            def inv_sqrt(ins):
                roots[0] += 1
                ins.then_inc(sem("var_ready"), 1)
                dve.wait_ge(sem("root_ready"), roots[0])

            def norm_rows(name, src, dst, g_turn, turn_free=None):
                j = NORM[name]
                for t in range(TT):
                    s, r = ss[:, 2 * j + t:2 * j + t + 1], rs[:, 2 * j + t:2 * j + t + 1]
                    dve.wait_ge(squares, 2 * j + t + 1)
                    inv_sqrt(V_.tensor_scalar(r, s, 1.0 / D, EPS, ALU.mult, ALU.add))
                    ins = V_.tensor_scalar(dst[:, t, :], src[:, t, :], r, None, ALU.mult)
                    if g_turn:
                        ins.then_inc(rows_ready, 1)
                    else:
                        link(ins)

            at_unit = [0]

            def lo_up_to(u):
                while at_unit[0] <= min(u, len(units) - 1):
                    if units[at_unit[0]]["maker"] == "dve":
                        make_lo(dve, at_unit[0])
                    at_unit[0] += 1

            def lo_for(name, c=-1):
                lo_up_to(units_of[index[name][c]][-1] + 3)

            def split(dst_hi, dst_lo, src, last_sem):
                link(V_.tensor_copy(dst_hi, src))
                V_.tensor_tensor(dst_lo, src, dst_hi, ALU.subtract).then_inc(sem(last_sem), 1)

            def cols(name, r, full, scale=None, shift=None):
                j = TURN[name]
                for k in range(4):
                    if k % 2 == 0:
                        dve.wait_ge(turned, 4 * j + k // 2 + 1)
                    src = PM[:, k // 2, (k % 2) * SEQ:(k % 2 + 1) * SEQ]
                    if scale is None:
                        ins = V_.tensor_copy(full[:, k, :], src)
                    elif shift is None:
                        ins = V_.tensor_scalar(full[:, k, :], src, scale(k), None, ALU.mult)
                    else:
                        ins = V_.tensor_scalar(full[:, k, :], src, scale(k), shift(k), ALU.mult, ALU.add)
                link(ins)
                link(V_.tensor_copy(place[:, r, 0, 0:4, :], full[:, 0:4, :]))
                V_.tensor_tensor(place[:, r, 1, 0:4, :], full[:, 0:4, :], place[:, r, 0, 0:4, :], ALU.subtract).then_inc(cols_dve, 1)
                dve.wait_ge(cols_act, j + 1)
                V_.tensor_tensor(place[:, r, 1, 4:KT, :], full[:, 4:KT, :], place[:, r, 0, 4:KT, :], ALU.subtract).then_inc(cols_dve, 1)

            dve.wait_ge(sem("consts_turned"), 1)
            V_.tensor_copy(feat_cols[:, :], PM[:, 0, 0:N_ROWS]).then_inc(sem("consts_read"), 1)
            dve.wait_ge(sem("consts_turned"), 2)
            dve.wait_ge(sem("tables_in"), 16)
            V_.tensor_tensor(WST, PM[:, 1, :].rearrange("p (g t) -> p g t", g=4), tab("upto").unsqueeze(1).to_broadcast([P, 4, P]),
                             ALU.mult).then_inc(sem("consts_read"), 1)
            dve.wait_ge(sem("x_in"), 16)
            norm_rows("x1", x, XN, True)
            dve.wait_ge(sem("consts_read"), 2)
            cols("x1", 0, TF, scale=lambda k: feat("norm_mix_g", k))

            p = step["in"]
            pair_wait(dve, p + 1, 0)
            dve.wait_ge(sem("pad_ready"), 1)
            dve.wait_ge(freed[p % 2], 2)
            V_.tensor_tensor(XC[:, :, 2:SEQ + 2], CC, bank(p + 1, 0).rearrange("p (j q) -> p j q", j=2), ALU.mult).then_inc(freed[(p + 1) % 2], 1)
            dve.wait_ge(freed[(p + 1) % 2], 2)
            for j in range(2):
                y = CC[:, j, :]
                link(V_.tensor_scalar(y, XC[:, j, 0:SEQ], feat("w_conv", j), None, ALU.mult))
                link(V_.scalar_tensor_tensor(y, XC[:, j, 1:SEQ + 1], feat("w_conv", 2 + j), y, ALU.mult, ALU.add))
                link(V_.scalar_tensor_tensor(y, XC[:, j, 2:SEQ + 2], feat("w_conv", 4 + j), y, ALU.mult, ALU.add))
            link(V_.tensor_tensor(CC, CC, CB, ALU.mult))
            split(place[:, 1, 0, 0:2, :], place[:, 1, 1, 0:2, :], CC, "branch_T")

            dve.wait_ge(sem("v_gelu"), 1)
            dve.wait_ge(sem("small"), 16 * 9)
            sq = T3[:, :, 0:P].rearrange("p a b -> p a b")
            mean, var = gm[:, 0:2], gm[:, 2:4]
            link(V_.tensor_reduce(mean, V, AX.X, ALU.add))
            link(V_.tensor_scalar(mean, mean, 1.0 / MIX, None, ALU.mult))
            for t in range(TT):
                link(V_.tensor_scalar(V[:, t, :], V[:, t, :], mean[:, t:t + 1], None, ALU.subtract))
            sq = TMP[:, :, 0:MIX]
            link(V_.tensor_tensor(sq, V, V, ALU.mult))
            link(V_.tensor_reduce(var, sq, AX.X, ALU.add))
            inv_sqrt(V_.tensor_scalar(var, var, 1.0 / MIX, EPS, ALU.mult, ALU.add))
            for t in range(TT):
                link(V_.scalar_tensor_tensor(V[:, t, :], V[:, t, :], var[:, t:t + 1], lnw[:, 0, :], ALU.mult, ALU.mult))
            V_.tensor_tensor(V, V, lnw[:, 1, :].unsqueeze(1).to_broadcast([P, TT, MIX]), ALU.add).then_inc(sem("spatial_v"), 1)

            dve.wait_ge(freed[(p + 4) % 2], 2 * ((p + 4) // 2 + 1))
            nh = 2 * HEADS1
            heads = FQK.rearrange("p t (h d) -> p t h d", d=HD)
            sq4 = TMP
            r = fs[:, 40:40 + 2 * nh].rearrange("p (t h) -> p t h", t=TT)
            link(V_.tensor_tensor(sq4, FQK, FQK, ALU.mult))
            link(V_.tensor_reduce(r, sq4.rearrange("p t (h d) -> p t h d", d=HD), AX.X, ALU.add))
            inv_sqrt(V_.tensor_scalar(r, r, 1.0 / HD, EPS, ALU.mult, ALU.add))
            link(V_.tensor_scalar(r[:, :, 0:HEADS1], r[:, :, 0:HEADS1], HD ** -0.5, None, ALU.mult))
            link(V_.tensor_tensor(heads, heads, r.unsqueeze(3).to_broadcast([P, TT, nh, HD]), ALU.mult))
            for n in range(2):
                hv = heads[:, :, n * HEADS1:(n + 1) * HEADS1, :]
                for t in range(TT):
                    ins = V_.tensor_tensor(hv[:, t], hv[:, t], qk_g[:, n, :].unsqueeze(1).to_broadcast([P, HEADS1, HD]), ALU.mult)
                    if (n, t) == (1, TT - 1):
                        ins.then_inc(sem("fox_qk"), 1)
                    else:
                        link(ins)
            dve.wait_ge(freed[(p + 5) % 2], 2 * ((p + 5) // 2 + 1))
            V_.tensor_tensor(FR, FR, bf[:, :].unsqueeze(1).to_broadcast([P, TT, HEADS1]), ALU.add).then_inc(sem("fox_abs"), 1)
            dve.wait_ge(sem("fox_abs"), 1)
            fflat = FR.rearrange("p t h -> p (t h)")
            link(V_.tensor_scalar(fs[:, 8:16], fflat, 0.0, None, ALU.min))

            dve.wait_ge(sem("stick_z"), 1)
            V_.tensor_scalar(T1, PM[:, :, 0:384], HD ** -0.5, None, ALU.mult).then_inc(sem("stick_z_read"), 1)
            dve.wait_ge(sem("stick_z_read"), 1)
            link(V_.tensor_scalar(T3, T1, 0.0, None, ALU.max))
            dve.wait_ge(sem("stick_ln"), 1)
            link(V_.tensor_tensor(T3, T3, T2, ALU.add))
            V_.tensor_tensor(T3, T3, tab("strict").unsqueeze(1).to_broadcast([P, 4, 384]), ALU.mult).then_inc(sem("stick_l"), 1)
            link(V_.tensor_tensor(T1, T1, tab("strict_neg").unsqueeze(1).to_broadcast([P, 4, 384]), ALU.add))
            dve.wait_ge(sem("fox_ln"), 1)
            link(V_.tensor_tensor(fs[:, 0:8], fs[:, 0:8], fs[:, 8:16], ALU.subtract))
            V_.tensor_copy(NLF.rearrange("p t h n -> p (t h) n"), fs[:, 0:8].unsqueeze(2).to_broadcast([P, 8, P])).then_inc(sem("fox_f"), 1)
            dve.wait_ge(sem("stick_c"), 1)
            V_.tensor_tensor(T1, T1, PM[:, :, 0:384], ALU.subtract).then_inc(sem("stick_logw"), 1)

            dve.wait_ge(sem("spatial_mix"), 1)
            dve.wait_ge(freed[(p + 1) % 2], 2)
            m4 = PM[:, 1, :].rearrange("p (j t n) -> p j t n", j=2, t=TT)
            mixed = XC[:, :, 0:SEQ]
            y4 = mixed.rearrange("p j (t n) -> p j t n", t=TT)
            for j in range(2):
                ins = V_.tensor_tensor(y4[:, j], m4[:, j], bs[:, j, :].unsqueeze(1).to_broadcast([P, TT, P]), ALU.add)
                if j == 0:
                    link(ins)
                else:
                    ins.then_inc(sem("spatial_read"), 1)
            dve.wait_ge(sem("spatial_read"), 1)
            link(V_.tensor_tensor(U, mixed, U, ALU.mult))
            split(place[:, 1, 0, 2:4, :], place[:, 1, 1, 2:4, :], U, "branch_T")
            dve.wait_ge(sem("stick_o"), 1)
            o = PM[:, 0, :].rearrange("p (j q) -> p j q", j=2)
            split(place[:, 1, 0, 4:6, :], place[:, 1, 1, 4:6, :], o, "branch_T")
            dve.wait_ge(sem("branch_T"), 3)
            V_.nop().then_inc(sem("stick_o_read"), 1)

            dve.wait_ge(sem("fox_s"), 1)
            mx = fs[:, 16:24]
            link(V_.tensor_reduce(mx[:, 0:4], PM[:, :, 0:P], AX.X, ALU.max))
            link(V_.tensor_reduce(mx[:, 4:8], PM[:, :, P:384], AX.X, ALU.max))
            nF = fs[:, 60:68]
            link(V_.tensor_copy(nF, PM[:, 0, 384:392]))
            link(V_.tensor_tensor(mx, mx, nF, ALU.subtract))
            link(V_.tensor_tensor(fs[:, 24:32], mx, nF, ALU.add))
            V_.tensor_scalar(fs[:, 24:32], fs[:, 24:32], -1.0, None, ALU.mult).then_inc(sem("fox_max"), 1)
            dve.wait_ge(sem("fox_e"), 8)
            link(V_.reciprocal(fs[:, 32:40], fs[:, 32:40]))
            link(V_.tensor_tensor(T2[:, :, 0:P], T2[:, :, 0:P], fs[:, 32:36].unsqueeze(2).to_broadcast([P, 4, P]), ALU.mult))
            V_.tensor_tensor(T2[:, :, P:384], T2[:, :, P:384], fs[:, 36:40].unsqueeze(2).to_broadcast([P, 4, 2 * P]), ALU.mult).then_inc(sem("fox_p"), 1)
            dve.wait_ge(sem("fox_p_turned"), 1)
            V_.tensor_copy(T3, PM[:, :, 0:384]).then_inc(sem("fox_pT"), 1)
            dve.wait_ge(sem("fox_o"), 1)
            split(place[:, 1, 0, 6:8, :], place[:, 1, 1, 6:8, :], o, "branch_T")

            for half in range(2):
                for n in range(4):
                    p = step["branch"] + 4 * half + n
                    for t in range(TT):
                        pair_wait(dve, p, t)
                        if (half, n, t) == (0, 0, 0):
                            dve.wait_ge(freed[(step["gate"] + 7) % 2], 2 * ((step["gate"] + 7) // 2 + 1))
                            dve.wait_ge(freed[(step["gate"] + 6) % 2], 2 * ((step["gate"] + 6) // 2 + 1))
                        g = sg(2 * n + half, t)
                        m = XN[:, t, half * COL:(half + 1) * COL]
                        if n == 0:
                            V_.tensor_tensor(m, g, bank(p, t), ALU.mult).then_inc(freed[p % 2], 1)
                        else:
                            tmp = TMP[:, t, :]
                            V_.tensor_tensor(tmp, g, bank(p, t), ALU.mult).then_inc(freed[p % 2], 1)
                            dve.wait_ge(freed[p % 2], 2 * (p // 2) + t + 1)
                            ins = V_.tensor_tensor(m, m, tmp, ALU.add)
                            if half == 1 and n == 3:
                                ins.then_inc(rows_ready, 1)
                            else:
                                link(ins)
            cols("merged", 0, TF)
            for half in range(2):
                p = step["out1"] + half
                for t in range(TT):
                    pair_wait(dve, p, t)
                    xs = x[:, t, half * COL:(half + 1) * COL]
                    V_.tensor_tensor(xs, xs, bank(p, t), ALU.add).then_inc(sem("x_1"), 1)
                    dve.wait_ge(sem("x_1"), 2 * half + t + 1)
                    V_.nop().then_inc(freed[p % 2], 1)
            lo_for("out1")
            norm_rows("x2", x, XN, True)
            cols("x2", 1, TF, scale=lambda k: feat("norm_ffn_g", k))
            def hidden(p, buf, dst, tiles, done):
                for b in range(tiles // 2):
                    pair_wait(dve, p, b)
                    V_.tensor_tensor(buf[:, 2 * b:2 * b + 2, :], buf[:, 2 * b:2 * b + 2, :],
                                     bank(p, b).rearrange("p (j q) -> p j q", j=2), ALU.mult).then_inc(freed[p % 2], 1 if tiles == 4 else 2)
                dve.wait_ge(freed[p % 2], 2 * (p // 2 + 1))
                split(dst[:, 0, 0:tiles, :], dst[:, 1, 0:tiles, :], buf[:, 0:tiles, :], done)

            for c in range(FFN_GROUPS):
                lo_for("ffn_u", c)
                dve.wait_ge(sem("silu_done"), 2 * c + (2 if c < FFN_GROUPS - 1 else 1))
                if c >= 2:
                    dve.wait_ge(sem("ffn_made"), c - 1)
                hidden(step["ffn"] + 2 * c + 1, SILU[:, c % 2], hidden_at(0)[:, c % 2],
                       4 if c < FFN_GROUPS - 1 else 2, "ffn_hidden")
            lo_for("ffn_o")
            dve.wait_ge(sem("small2"), 16 * 7)
            for j in range(2):
                link(V_.tensor_tensor(lamv[:, 2 * j, :], lamv[:, 2 * j, :], lamv[:, 2 * j + 1, :], ALU.mult))
                V_.tensor_reduce(ds[:, j:j + 1], lamv[:, 2 * j, :], AX.X, ALU.add).then_inc(sem("lam_sums"), 1)
            dve.wait_ge(sem("lam_exp"), 1)
            link(V_.tensor_tensor(ds[:, 4:5], ds[:, 2:3], ds[:, 3:4], ALU.subtract))
            lam = ds[:, 5:6]
            link(V_.tensor_scalar(lam, ds[:, 4:5], 0.2, None, ALU.add))
            link(V_.tensor_scalar(subln[:, :], subln[:, :], 0.8, None, ALU.mult))
            dve.wait_ge(sem("ffn_made"), FFN_GROUPS)
            for t in range(TT):
                for half in range(2):
                    xs = x[:, t, half * COL:(half + 1) * COL]
                    V_.tensor_tensor(xs, xs, PM[:, 2 * t + half, :], ALU.add).then_inc(sem("x_2"), 1)
            dve.wait_ge(sem("x_2"), 4)
            for c in range(8):
                p = step["mod_T"] + c
                part, half = c // 2, c % 2
                pair_wait(dve, p, 1)
                b0 = (0, 1, 3, 4)[part] * 8 + 4 * half
                dst = modT[:, part, 4 * half:4 * half + 4, :]
                V_.tensor_tensor(dst, bank(p, 0)[:, 0:8].rearrange("p (m c) -> p m c", c=2),
                                 feats("b_mod_2", b0, 4).unsqueeze(2).to_broadcast([P, 4, 2]), ALU.add).then_inc(freed[p % 2], 2)
                dve.wait_ge(freed[p % 2], 2 * (p // 2 + 1))
            for part, g in ((1, "norm1_g_2"), (3, "norm2_g_2")):
                ins = V_.scalar_tensor_tensor(modT[:, part, :, :], modT[:, part, :, :], 1.0,
                                              feats(g, 0, 8).unsqueeze(2).to_broadcast([P, KT, 2]), ALU.add, ALU.mult)
                if part == 3:
                    ins.then_inc(sem("mod_cols"), 1)
                else:
                    link(ins)
            norm_rows("ctx", CTX, XN2, True)
            dve.wait_ge(sem("mod_cols"), 1)
            cols("ctx", 0, TF, scale=lambda k: modT[:, 1, k, 1:2], shift=lambda k: modT[:, 0, k, 1:2])
            norm_rows("x3", x, XN2, True)
            cols("x3", 1, TF, scale=lambda k: modT[:, 1, k, 0:1], shift=lambda k: modT[:, 0, k, 0:1])

            for j in range(8):
                dst = QT[:, 2 * j:2 * j + 2, :] if j < 4 else KTT[:, 2 * (j - 4):2 * (j - 4) + 2, SEQ:2 * SEQ]
                raw, rot = RAW[:, j % 2, :, :], ROT[:, j % 2, :, :]
                dve.wait_ge(sem("rope_raw"), j + 1)
                dve.wait_ge(sem("rope_rot"), j + 1)
                link(V_.tensor_tensor(rot, PM[:, j % 2, :].rearrange("p (a q) -> p a q", a=2),
                                      tab("sin").unsqueeze(1).to_broadcast([P, 2, SEQ]), ALU.mult))
                link(V_.tensor_tensor(dst, raw, tab("cos").unsqueeze(1).to_broadcast([P, 2, SEQ]), ALU.mult))
                V_.tensor_tensor(dst, dst, rot, ALU.add).then_inc(sem("rope_done"), 1)
                dve.wait_ge(sem("rope_done"), j + 1)
            V_.nop().then_inc(sem("kv_ready"), 4)
            for g in range(4):
                dve.wait_ge(sem("four_2"), g + 1)
                split(four[:, 0, g, :], four[:, 1, g, :], PM[:, 2 + g % 2, 0:SEQ], "four_B")

            N = HEADS2 * TT
            for n in range(N):
                nm = ds[:, 16 + 2 * (n % 2):18 + 2 * (n % 2)]
                sums = ds[:, 20 + 2 * (n % 2):22 + 2 * (n % 2)]
                dve.wait_ge(sem("scores"), n + 1)
                link(V_.tensor_reduce(ds[:, 8:10], PM[:, 0:2, :], AX.X, ALU.max))
                V_.tensor_scalar(nm, ds[:, 8:10], -HD ** -0.5, None, ALU.mult).then_inc(sem("nmax"), 1)
                if n >= 1:
                    dve.wait_ge(sem("diff_turned"), n)
                    if n >= 3:
                        dve.wait_ge(sem("heads_made"), n - 2)
                    V_.tensor_copy(AA[:, (n - 1) % 2, :], PM[:, 2, :]).then_inc(sem("diff_T"), 1)
                dve.wait_ge(sem("probs"), 2 * n + 2)
                link(V_.reciprocal(ds[:, 12:14], sums))
                link(V_.tensor_tensor(ds[:, 14:15], ds[:, 13:14], lam, ALU.mult))
                link(V_.tensor_scalar(PP[:, n % 2, 1, :], PP[:, n % 2, 1, :], ds[:, 14:15], None, ALU.mult))
                V_.scalar_tensor_tensor(PP[:, n % 2, 0, :], PP[:, n % 2, 0, :], ds[:, 12:13], PP[:, n % 2, 1, :],
                                        ALU.mult, ALU.subtract).then_inc(sem("diff"), 1)
            dve.wait_ge(sem("diff_turned"), N)
            V_.tensor_copy(AA[:, (N - 1) % 2, :], PM[:, 2, :]).then_inc(sem("diff_T"), 1)
            V_.tensor_copy(SB, silu_c[:, :, 0:1].to_broadcast([P, KT, P])).then_inc(sem("sb_ready"), 1)
            dve.wait_ge(sem("heads_rows"), N)
            hv = O.rearrange("p t (h d) -> p (t h) d", d=P)
            sq = XN3.rearrange("p t (h d) -> p (t h) d", d=P)
            r = ds[:, 32:48]
            link(V_.tensor_tensor(sq, hv, hv, ALU.mult))
            link(V_.tensor_reduce(r, sq, AX.X, ALU.add))
            inv_sqrt(V_.tensor_scalar(r, r, 1.0 / P, EPS, ALU.mult, ALU.add))
            link(V_.tensor_tensor(hv, hv, r.unsqueeze(2).to_broadcast([P, 16, P]), ALU.mult))
            for t in range(TT):
                ht = O[:, t, :].rearrange("p (h d) -> p h d", d=P)
                V_.tensor_tensor(ht, ht, subln[:, :].unsqueeze(1).to_broadcast([P, HEADS2, P]), ALU.mult).then_inc(rows_ready, 1)
            cols("heads", 0, TF2)
            for half in range(2):
                p = step["y"] + half
                for t in range(TT):
                    pair_wait(dve, p, t)
                    g = SG2[:, t, D + half * COL:D + (half + 1) * COL]
                    V_.tensor_tensor(Y[:, t, half * COL:(half + 1) * COL], g, bank(p, t), ALU.mult).then_inc(freed[p % 2], 1)
            for half in range(2):
                p = step["y"] + 2 + half
                for t in range(TT):
                    pair_wait(dve, p, t)
                    g = SG2[:, t, half * COL:(half + 1) * COL]
                    tmp = XN3[:, t, 0:COL]
                    ys = Y[:, t, half * COL:(half + 1) * COL]
                    V_.tensor_tensor(tmp, g, bank(p, t), ALU.mult).then_inc(freed[p % 2], 1)
                    dve.wait_ge(freed[p % 2], 2 * (p // 2) + t + 1)
                    ins = V_.tensor_tensor(ys, ys, tmp, ALU.add)
                    if half == 1:
                        ins.then_inc(rows_ready, 1)
                    else:
                        link(ins)
            cols("y2", 1, TF2)
            dve.wait_ge(sem("g1_rows"), 2)
            for half in range(2):
                p = step["out2"] + half
                for t in range(TT):
                    pair_wait(dve, p, t)
                    xs = x[:, t, half * COL:(half + 1) * COL]
                    tmp = XN3[:, t, half * COL:(half + 1) * COL]
                    V_.tensor_tensor(tmp, G1[:, half * COL:(half + 1) * COL], bank(p, t), ALU.mult).then_inc(freed[p % 2], 1)
                    dve.wait_ge(freed[p % 2], 2 * (p // 2) + t + 1)
                    V_.tensor_tensor(xs, xs, tmp, ALU.add).then_inc(sem("x_3"), 1)
                    dve.wait_ge(sem("x_3"), 2 * half + t + 1)
            norm_rows("x4", x, XN3, True)
            cols("x4", 0, TF2, scale=lambda k: modT[:, 3, k, 0:1], shift=lambda k: modT[:, 2, k, 0:1])

            dve.wait_ge(sem("logits"), 1)
            L = ms[:, 0:40].rearrange("p (t n) -> p t n", t=TT)
            V_.tensor_tensor(L, PM[:, 0, 0:40].rearrange("p (t n) -> p t n", t=TT), rb[:, :].unsqueeze(1).to_broadcast([P, TT, 20]),
                             ALU.add).then_inc(sem("logits_read"), 1)
            dve.wait_ge(sem("logits_read"), 1)
            lg, le = L[:, :, 0:4], L[:, :, 4:20]
            rev = tab("rev").unsqueeze(1).to_broadcast([P, TT, 4])

            def small(s, n):
                return ms[:, s:s + TT * n].rearrange("p (t n) -> p t n", t=TT) if n > 1 else ms[:, s:s + TT]

            def spread(v, n=4):
                return v.unsqueeze(2).to_broadcast([P, TT, n])

            def first_max(src, top, hot, tmp):
                link(V_.tensor_reduce(top, src, AX.X, ALU.max))
                link(V_.tensor_tensor(hot, src, spread(top), ALU.is_equal))
                link(V_.tensor_tensor(hot, hot, rev, ALU.mult))
                link(V_.tensor_reduce(tmp, hot, AX.X, ALU.max))
                link(V_.tensor_tensor(hot, hot, spread(tmp), ALU.is_equal))

            gmax, ghot, t1 = small(40, 1), small(44, 4), small(42, 1)
            first_max(lg, gmax, ghot, t1)
            V_.tensor_tensor(small(72, 4), lg, spread(gmax), ALU.subtract).then_inc(sem("route_d"), 1)
            prod = ms[:, 144:176].rearrange("p (t g e) -> p t g e", t=TT, g=4)
            for t in range(TT):
                link(V_.tensor_tensor(prod[:, t], le[:, t, :].rearrange("p (g e) -> p g e", g=4),
                                      ghot[:, t, :].unsqueeze(2).to_broadcast([P, 4, 4]), ALU.mult))
            leg = small(52, 4)
            for t in range(TT):
                link(V_.tensor_reduce(leg[:, t, :], prod[:, t].rearrange("p g e -> p e g"), AX.X, ALU.add))
            v1, h1, v2, h2 = small(60, 1), small(92, 4), small(62, 1), small(100, 4)
            first_max(leg, v1, h1, t1)
            rest = small(108, 4)
            link(V_.scalar_tensor_tensor(rest, h1, NEG, leg, ALU.mult, ALU.add))
            first_max(rest, v2, h2, t1)
            V_.tensor_tensor(small(128, 1), v2, v1, ALU.subtract).then_inc(sem("route_r"), 1)
            dve.wait_ge(sem("route_e"), 1)
            wg = small(64, 1)
            link(V_.tensor_reduce(wg, small(80, 4), AX.X, ALU.add))
            dve.wait_ge(sem("route_e"), 2)
            r = small(130, 1)
            den, w1, w2 = small(66, 1), small(68, 1), small(70, 1)
            link(V_.tensor_scalar(den, r, 1.0, None, ALU.add))
            link(V_.tensor_tensor(den, den, wg, ALU.mult))
            link(V_.reciprocal(w1, den))
            link(V_.tensor_tensor(w2, w1, r, ALU.mult))
            link(V_.tensor_tensor(h1, h1, spread(w1), ALU.mult))
            link(V_.tensor_tensor(h2, h2, spread(w2), ALU.mult))
            link(V_.tensor_tensor(h1, h1, h2, ALU.add))
            gates = ms[:, 176:208].rearrange("p (t g e) -> p t g e", t=TT, g=4)
            for t in range(TT):
                link(V_.tensor_tensor(gates[:, t], ghot[:, t, :].unsqueeze(2).to_broadcast([P, 4, 4]),
                                      h1[:, t, :].unsqueeze(1).to_broadcast([P, 4, 4]), ALU.mult))

            def add_expert(e):
                for t in range(TT):
                    g = ms[:, 176 + t * NEXP + e:177 + t * NEXP + e]
                    for half in range(2):
                        n = 4 * e + 2 * t + half
                        dve.wait_ge(sem("expert_made"), n + 1)
                        acc = ACC[:, t, half * COL:(half + 1) * COL]
                        if e >= 1:
                            dve.wait_ge(sem("added"), n - 3)
                        if e == 0:
                            V_.tensor_scalar(acc, PM[:, 2 * t + half, :], g, None, ALU.mult).then_inc(sem("added"), 1)
                        else:
                            V_.scalar_tensor_tensor(acc, PM[:, 2 * t + half, :], g, acc, ALU.mult, ALU.add).then_inc(sem("added"), 1)

            for e in range(NEXP):
                lo_for("eu", e)
                dve.wait_ge(sem("exp_silu"), 2 * e + 2)
                if e >= 2:
                    dve.wait_ge(sem("expert_made"), 4 * (e - 1))
                hidden(step["exp"] + 2 * e + 1, SL[:, e % 2], hidden_at(1)[:, e % 2], 4, "hidden")
                lo_for("ed", e)
                add_expert(e)
            dve.wait_ge(sem("added"), 4 * NEXP)
            dve.wait_ge(sem("g2_rows"), 2)
            for t in range(TT):
                link(V_.tensor_tensor(ACC[:, t, :], ACC[:, t, :], G2, ALU.mult))
                V_.tensor_tensor(x[:, t, :], x[:, t, :], ACC[:, t, :], ALU.add).then_inc(sem("x_4"), 1)
            norm_rows("last", x, XN3, False)
            dve.wait_ge(sem("late_in"), 80)
            for t in range(TT):
                V_.tensor_tensor(XN3[:, t, :], XN3[:, t, :], FINAL, ALU.mult).then_inc(sem("out_ready"), 1)


_INS = ["x", "norm_mix_g", "w_in", "w_conv", "w_spatial", "b_spatial", "gmlp_ln_g", "gmlp_ln_b", "fox_q_norm_g",
        "fox_k_norm_g", "fox_forget_b", "w_branch", "w_out", "norm_ffn_g", "w_ffn_in", "w_ffn_out", "c_2", "ctx_2",
        "c_ctx_2", "w_mod_2", "b_mod_2", "norm1_g_2", "norm2_g_2", "w_in_2", "lam_q1_2", "lam_k1_2", "lam_q2_2",
        "lam_k2_2", "subln_g_2", "w_attn_out_2", "w_four_out_2", "w_out_2", "w_router_group_2", "b_router_group_2",
        "w_router_expert_2", "b_router_expert_2", "w_exp_gate_2", "w_exp_up_2", "w_exp_down_2", "final_g_2"]


def kernel(**inputs):
    import numpy as _np
    import concourse.bacc as _bacc
    from concourse.bass_utils import run_bass_kernel_spmd as _run

    nc = _bacc.Bacc("TRN2", target_bir_lowering=False, num_devices=1)
    arrays = {f"in_{n}_dram": _np.ascontiguousarray(inputs[n]) for n in _INS}
    arrays["in_tables_dram"] = TABLES
    a = {n: nc.dram_tensor(f"in_{n}_dram", arrays[f"in_{n}_dram"].shape, F32, kind="ExternalInput").ap()
         for n in [*_INS, "tables"]}
    out = nc.dram_tensor("out_0_dram", (1, SEQ, D), F32, kind="ExternalOutput").ap()
    block_pair_kernel(nc, a, out)
    r = _run(nc, [arrays], core_ids=[0])
    return r.results[0]["out_0_dram"]
```

```python
from contextlib import ExitStack

import numpy as np
import concourse.bass as bass
from concourse import mybir

F32 = mybir.dt.float32
F32R = mybir.dt.float32r
ALU = mybir.AluOpType
ACT = mybir.ActivationFunctionType
AX = mybir.AxisListType

P = 128
D = 1024
SEQ = 256
KT = D // P
TT = SEQ // P
MIX = 256
FFN = 2816
FT_TILES = FFN // P
FFN_GROUPS = -(-FFN // 512)
HEADS1 = 4
HD = 64
HEADS2 = 8
NEXP = 16
PER_GROUP = 4
GROUPS = NEXP // PER_GROUP
WINDOWS = GROUPS + 1
HID = 512
EPS = 1e-6
NEG = -1e30
COL = 512
SLOT = 4 * COL
RING = 4
UNIT = 2 * COL
UNITS = 4

W_IN_STARTS = (0, 512, 1024, 1536, 2048, 2560)
F_RAW = 2816
GATE_RAW = 2820
Q_OFF, K_OFF, V_OFF, F_OFF, GA_OFF, GF_OFF = 0, 1024, 2048, 3072, 3584, 4608


def shape_tables():
    i = np.arange(P)
    parts = {}
    parts["ident"] = np.eye(P)
    parts["upto"] = (i[:, None] <= i[None, :]) * 1.0
    parts["ones"] = np.ones((P, P))
    parts["from"] = (i[:, None] >= i[None, :]) * 1.0
    strict = (i[:, None] < i[None, :]) * 1.0
    parts["strict"] = np.concatenate([strict, np.ones((P, P)), strict], 1)
    parts["strict_neg"] = np.where(parts["strict"] > 0, 0.0, NEG)
    parts["causal_neg"] = np.where(i[None, :] <= i[:, None], 0.0, NEG)
    turn = np.zeros((P, P))
    for b in range(0, P, 32):
        for j in range(16):
            turn[b + 16 + j, b + j] = -1.0
            turn[b + j, b + 16 + j] = 1.0
    parts["turn"] = turn
    inv = (1.0 / (np.float32(10000.0) ** (np.arange(16, dtype=np.float32) / np.float32(16)))).astype(np.float32)
    tok = np.arange(SEQ)
    row = (tok // 64).astype(np.float32)
    col = (tok % 64).astype(np.float32)
    d = i % 64
    angle = np.where((d < 32)[:, None], row[None, :] * inv[d % 16][:, None], col[None, :] * inv[d % 16][:, None])
    parts["cos"] = np.cos(angle.astype(np.float64))
    parts["sin"] = np.sin(angle.astype(np.float64))
    w = 2 * np.pi * np.outer(tok, tok) / SEQ
    dft = np.concatenate([np.cos(w), np.sin(w)], 1) / np.sqrt(SEQ)
    parts["dft_tok"] = dft.reshape(TT, P, 2 * SEQ).transpose(1, 0, 2).reshape(P, -1)
    w = 2 * np.pi * np.outer(i, i) / P
    parts["dft_cos"] = np.cos(w) / np.sqrt(P)
    parts["dft_nsin"] = -np.sin(w) / np.sqrt(P)
    parts["rev"] = np.tile(np.array([4.0, 3.0, 2.0, 1.0]), (P, 1))
    parts["slots"] = np.tile(np.arange(WINDOWS * P), (P, 1))
    at, start = {}, 0
    for name, a in parts.items():
        at[name] = (start, a.shape[1])
        start += a.shape[1]
    return np.concatenate(list(parts.values()), 1).astype(np.float32), at


TABLES, TABLE_AT = shape_tables()
RESIDENT = TABLE_AT["slots"][0]

ROWS = {}
for _name, _n in (("norm_mix_g", 8), ("norm_ffn_g", 8), ("norm1_g_2", 8), ("norm2_g_2", 8), ("c_2", 8),
                  ("c_ctx_2", 8), ("b_mod_2", 48), ("w_conv", 6)):
    ROWS[_name] = (sum(n for _, n in ROWS.values()), _n)
N_ROWS = sum(n for _, n in ROWS.values())


def plan_chunks(a):
    def cols(w, start, n=COL):
        return w[:, start:start + n].rearrange("(k p) n -> p k n", p=P)

    w_in, w_ffn, w_in2, w_mod = a["w_in"][0], a["w_ffn_in"][0], a["w_in_2"][0], a["w_mod_2"][0]
    out = [("in", cols(w_in, s, min(COL, GATE_RAW - s))) for s in W_IN_STARTS]
    out += [("gate", cols(w_in, GATE_RAW + COL * i)) for i in range(8)]
    wb = a["w_branch"][0].rearrange("n c d -> (n c) d")
    out += [("branch", cols(wb, COL * h)) for h in range(2)]
    out += [("out1", cols(a["w_out"][0], COL * h)) for h in range(2)]
    wo = a["w_ffn_out"][0]

    def ffn(kind, i):
        n = min(COL, FFN - COL * i)
        if kind == "ffn_o":
            return kind, wo[COL * i:COL * i + n, :].rearrange("(k p) n -> p k n", p=P)
        return kind, cols(w_ffn, COL * i + (FFN if kind == "ffn_u" else 0), n)

    mod = [("mod_T", cols(w_mod, D * part + COL * h)) for part in (0, 1, 3, 4) for h in range(2)]
    out += mod[0:2]
    out.append(ffn("ffn_g", 0))
    for i in range(FFN_GROUPS):
        out.append(ffn("ffn_u", i))
        if i + 1 < FFN_GROUPS:
            out.append(ffn("ffn_g", i + 1))
        out += [ffn("ffn_o", i), mod[i + 2]]
    for name, start, n in (("q", Q_OFF, 2), ("k", K_OFF, 2), ("v", V_OFF, 2), ("f", F_OFF, 1), ("g2", GA_OFF, 4)):
        out += [(name, cols(w_in2, start + COL * i)) for i in range(n)]
    out.append(("fo", a["w_four_out_2"][0].rearrange("(k p) n -> p k n", p=P)))
    out.append(("mod_g1", cols(w_mod, 2 * D)))
    out += [("ao", cols(a["w_attn_out_2"][0], COL * h)) for h in range(2)]
    out.append(("mod_g1", cols(w_mod, 2 * D + COL)))
    out += [("out2", cols(a["w_out_2"][0], COL * h)) for h in range(2)]
    out += [("mod_g2", cols(w_mod, 5 * D + COL * h)) for h in range(2)]
    gate, up, down = (a[f"w_exp_{n}_2"][0] for n in ("gate", "up", "down"))
    out.append(("eg", cols(gate[0], 0)))
    for e in range(NEXP):
        out.append(("eu", cols(up[e], 0)))
        if e + 1 < NEXP:
            out.append(("eg", cols(gate[e + 1], 0)))
        out.append(("ed", down[e].rearrange("(k p) n -> p k n", p=P)))
    return out


def plan_units(chunks):
    pieces, units, of_chunk = [], [], []
    for c, (name, src) in enumerate(chunks):
        _, ks, n = src.shape
        split = not name.startswith("mod")
        per_piece = 4 if n <= COL else 2
        per_unit = per_piece // 2 if split else per_piece
        maker = None if not split else "dve" if c < 2 or name in ("ffn_g", "ffn_u", "ffn_o", "eg", "eu", "ed") else "pool"
        of_chunk.append([])
        for k0 in range(0, ks, per_piece):
            kn = min(per_piece, ks - k0)
            pieces.append(dict(chunk=c, k0=k0, ks=kn, n=n, units=[]))
            for k in range(k0, k0 + kn, per_unit):
                pieces[-1]["units"].append(len(units))
                of_chunk[c].append(len(units))
                maker_of = "pool" if name in ("eg", "eu", "ed") and len(of_chunk[c]) == 2 else maker
                units.append(dict(piece=len(pieces) - 1, chunk=c, k0=k, ks=min(per_unit, k0 + kn - k), n=n, maker=maker_of))
    counts = dict(split=0, dve=0, pool=0, used=0)
    for u, unit in enumerate(units):
        if unit["maker"]:
            unit["split"] = counts["split"]
            unit["lo"] = counts[unit["maker"]]
            counts["split"] += 1
            counts[unit["maker"]] += 1
            if u != of_chunk[unit["chunk"]][-1] and chunks[unit["chunk"]][0] != "branch":
                unit["used"] = counts["used"]
                counts["used"] += 1
    return pieces, units, of_chunk


def block_pair_kernel(nc, a, out):
    chunks = plan_chunks(a)
    pieces, units, units_of = plan_units(chunks)
    index = {}
    for i, (name, _) in enumerate(chunks):
        index.setdefault(name, []).append(i)
    split_units = [u for u, unit in enumerate(units) if unit["maker"]]

    ctx = ExitStack()
    with ctx:
        def sb(name, shape, dt=F32):
            return ctx.enter_context(nc.sbuf_tensor(name, shape, dt))

        sems = {}

        def sem(name):
            if name not in sems:
                sems[name] = ctx.enter_context(nc.semaphore(name))
            return sems[name]

        ring = sb("ring", [P, RING * SLOT])
        tables = sb("tables_sb", [P, RESIDENT])
        x = sb("x_sb", [P, TT, D])
        w_hi = sb("w_hi", [P, UNITS * UNIT], F32R)
        w_lo = sb("w_lo", [P, UNITS * UNIT], F32R)
        acts = sb("acts", [P, 10240], F32R)
        arena = sb("arena", [P, 19456])
        feat_cols = sb("feat_cols", [P, N_ROWS])
        lnw = sb("lnw", [P, 2, MIX])
        qk_g = sb("qk_g", [P, 2, HD])
        subln = sb("subln", [P, P])
        bs = sb("bs", [P, 2, P])
        bf = sb("bf", [P, HEADS1])
        rb = sb("rb", [P, 20])
        modT = sb("modT", [P, 4, KT, 2])
        silu_c = sb("silu_c", [P, KT, 2])
        crowded = sb("crowded", [1, 1], mybir.dt.int32)
        half_root = sb("half_root", [P, 16])
        st = sb("st", [P, 416])
        PG = ctx.enter_context(nc.psum_tensor("gemm_ps", [P, 4, 512], F32))
        PM = ctx.enter_context(nc.psum_tensor("mix_ps", [P, 4, 512], F32))

        def at(start, *dims):
            n = int(np.prod(dims))
            v = arena[:, start:start + n]
            if len(dims) == 1:
                return v
            names = "abcd"[:len(dims)]
            return v.rearrange(f"p ({' '.join(names)}) -> p {' '.join(names)}", **dict(zip(names, dims)))

        def tab(name, *dims):
            s, n = TABLE_AT[name]
            v = tables[:, s:s + n]
            if not dims:
                return v
            names = "abcd"[:len(dims)]
            return v.rearrange(f"p ({' '.join(names)}) -> p {' '.join(names)}", **dict(zip(names, dims)))

        def feat(name, j=0):
            s, _ = ROWS[name]
            return feat_cols[:, s + j:s + j + 1]

        def feats(name, j, n):
            s, _ = ROWS[name]
            return feat_cols[:, s + j:s + j + n]

        ident = tab("ident")
        ones = tab("ones")

        CB, CC = at(6144, 2, SEQ), at(6656, 2, SEQ)
        XC = at(7168, 2, SEQ + 2)
        U, V = at(7688, 2, SEQ), at(8200, TT, MIX)
        SQ, SK, SV = at(8712, 2, SEQ), at(9224, 2, SEQ), at(9736, TT, MIX)
        FQK = at(10248, TT, 512)
        FV = at(11272, TT, MIX)
        FR = at(11784, TT, HEADS1)
        T1, T2, T3 = at(11800, 4, 384), at(13336, 4, 384), at(14872, 4, 384)
        FT = at(16408, 4, SEQ)
        WS, WST = at(16408, 4, P), at(17432, 4, P)
        NLF = at(17944, 2, HEADS1, P)
        VROWS = at(17944, P)
        lamv = at(18968, 4, HD)
        XN = at(11800, TT, D)
        JUNK = at(14872, D)
        TMP = at(14872, TT, COL)
        TF = at(0, KT, SEQ)
        SILU = at(2048, 2, 4, SEQ)

        def sg(c, t):
            return at(c * 1024 + t * COL if c < 6 else (17944, 16408)[c - 6] + t * COL, COL)

        QT = at(0, KT, SEQ)
        KTT = at(2048, KT, 2 * SEQ)
        V2 = at(6144, 4, D)
        SG2 = at(10240, TT, 2 * D)
        O = at(14336, TT, D)
        FN = at(14336, TT, COL)
        DT = at(15360, 2, 512)
        PP = at(16384, 2, 2, 512)
        RAW = at(16384, 2, 2, SEQ)
        ROT = at(17408, 2, 2, SEQ)
        AA = at(18432, 2, 512)
        CTX = at(14336, TT, D)
        JUNK_CTX, X3_ROWS = at(11800, D), at(12288, TT, D)
        XN2, JUNK2 = at(16384, TT, D), at(18432, D)
        SB = at(0, KT, P)
        G1 = at(1024, D)
        Y = at(2048, TT, D)
        XN3 = at(4096, TT, D)
        G2 = at(6144, D)
        JUNK3 = at(0, D)
        TF2 = at(8192, KT, SEQ)
        ACC = at(2048, TT, D)
        BM = at(16384, 2, D)
        FINAL = at(18432, D)
        wr = at(7168, KT, 20)
        JUNK4 = at(10240, D)
        IOTA = at(7328, WINDOWS * P)
        ACCG = at(8192, 2, D)
        SL = at(10240, 2, COL)
        HROW = at(11264, 2, COL)
        PICK = at(12288, TT, WINDOWS * P)
        PICK_T = at(13568, WINDOWS, SEQ)
        XF = at(14848, KT, P)
        SLOT_GATES = at(15872, WINDOWS, NEXP)
        rank = at(15952, TT, 4)
        place_of = at(15960, 8)
        XO = at(0, KT, P)
        HO = at(1024, 4, P)

        place = acts[:, 0:8192].rearrange("p (r h k q) -> p r h k q", r=2, h=2, k=KT)
        four = acts[:, 8192:10240].rearrange("p (h k q) -> p h k q", h=2, k=4)

        def hidden_at(r):
            return acts[:, 4096 * r:4096 * (r + 1)].rearrange("p (b h k q) -> p b h k q", b=2, h=2, k=4)

        win_T = acts[:, 0:4096].rearrange("p (b h k q) -> p b h k q", b=2, h=2, k=KT)
        hs = acts[:, 4096:6144].rearrange("p (b h k q) -> p b h k q", b=2, h=2, k=4)

        ss = st[:, 0:16]
        rs = st[:, 16:32]
        gm = st[:, 32:64]
        fs = st[:, 64:160]
        ds = st[:, 160:208]
        ms = st[:, 208:416]

        def raw(i):
            q = pieces[i]
            s = i % RING * SLOT
            return ring[:, s:s + q["ks"] * q["n"]].rearrange("p (k n) -> p k n", k=q["ks"])

        def raw_unit(u):
            unit = units[u]
            k = unit["k0"] - pieces[unit["piece"]]["k0"]
            return raw(unit["piece"])[:, k:k + unit["ks"], :]

        def part(w, u):
            unit = units[u]
            b = unit["split"] % UNITS * UNIT
            return w[:, b:b + unit["ks"] * unit["n"]].rearrange("p (k n) -> p k n", k=unit["ks"])

        landed = [sem(f"landed{s}") for s in range(RING)]
        hi_made = sem("hi_made")
        lo_made = {"dve": sem("lo_by_vector"), "pool": sem("lo_by_gpsimd")}

        def landed_wait(eng, i):
            eng.wait_ge(landed[i % RING], 16 * (i // RING + 1))

        def after(u, n=3):
            v = split_units[min(units[u]["split"] + n, len(split_units) - 1)]
            late = units_of[index["mod_g2"][0]][0]
            return min(v, late) if u < late else v

        def make_hi(act, u):
            unit = units[u]
            landed_wait(act, unit["piece"])
            if unit["split"] >= UNITS:
                act.wait_ge(*unit_done(split_units[unit["split"] - UNITS]))
            nc.scalar.activation(part(w_hi, u), raw_unit(u), ACT.Copy).then_inc(hi_made, 1)

        def make_lo(eng, u):
            unit = units[u]
            eng.wait_ge(hi_made, unit["split"] + 1)
            eng.tensor_tensor(part(w_lo, u), raw_unit(u), part(w_hi, u), ALU.subtract).then_inc(lo_made[unit["maker"]], 1)

        step = {}
        n_steps = 0
        for name, n in (("in", 6), ("gate", 8), ("branch", 8), ("out1", 2), ("ffn", 20),
                        ("q", 2), ("k", 4), ("v", 4), ("f", 1), ("g2", 4), 
                        ("y", 6), ("out2", 2), ("mod_g2", 2), ("exp", NEXP)):
            step[name] = n_steps
            n_steps += n

        def mod_step(c):
            return step["ffn"] + (c if c < 2 else 5 + 3 * (c - 2) if c < 7 else 19)

        def gate_step(c):
            return step["ffn"] + (2 if c == 0 else 1 + 3 * c)

        def up_step(c):
            return step["ffn"] + 3 + 3 * c

        made = [sem("pair0_made"), sem("pair1_made")]
        freed = [sem("pair0_freed"), sem("pair1_freed")]

        def pair_wait(eng, p, bank):
            eng.wait_ge(made[p % 2], 2 * (p // 2) + 1 + bank)

        def pair_free_wait(eng, p):
            if p >= 2:
                eng.wait_ge(freed[p % 2], 2 * (p // 2))

        def bank(p, b):
            return PG[:, 2 * (p % 2) + b, :]

        TURN = {"x1": 0, "merged": 1, "x2": 2, "ctx": 3, "x3": 4, "heads": 5, "y2": 6, "x4": 7}
        rows_ready, turned = sem("rows_ready"), sem("turned")
        cols_dve, cols_act = sem("cols_by_vector"), sem("cols_by_scalar")
        NORM = {"x1": 0, "x2": 1, "ctx": 2, "x3": 3, "x4": 4, "last": 5}
        squares = sem("squares")

        SIDE = {}
        for g in range(GROUPS):
            e = PER_GROUP * g
            if g >= 1:
                SIDE[e, "down"] = ("scatter", g - 1, 0)
                SIDE[e + 1, "up"] = ("scatter", g - 1, 1)
                SIDE[e + 1, "down"] = ("scatter", g - 1, 2)
                SIDE[e + 2, "up"] = ("scatter", g - 1, 3)
            if g + 1 < GROUPS:
                SIDE[e + 1, "gate"] = ("gather", g + 1, 0)
                SIDE[e + 2, "down"] = ("gather", g + 1, 1)
        side_order = [("gather", 0, 0), ("gather", 0, 1)]
        side_order += [SIDE[e, at_] for e in range(NEXP) for at_ in ("up", "gate", "down") if (e, at_) in SIDE]
        side_at = {job: j for j, job in enumerate(side_order)}
        side_made, side_read = sem("side_made"), sem("side_read")

        def gathers_before(g, half):
            return 2 * g + half

        block = ctx.enter_context(nc.Block())

        def last_product(i):
            def of_step(p):
                return made[p % 2], 2 * (p // 2) + 2
            name = chunks[i][0]
            c = index[name].index(i)
            if name == "ffn_o":
                return sem("ffn_made"), c + 1
            if name == "ed":
                return sem("expert_made"), 2 * (c + 1)
            if name in ("eg", "eu"):
                p = step["exp"] + c
                return made[p % 2], 2 * (p // 2) + (1 if name == "eg" else 2)
            steps = {"branch": step["branch"] + 4 * c + 3, "k": step["k"] + 2 * c + 1, "v": step["v"] + 2 * c + 1,
                     "fo": step["y"] + 1, "ao": step["y"] + 3 + c,
                     "mod_g1": step["y"] + 2 + 3 * c}
            of = {"ffn_g": gate_step, "ffn_u": up_step, "mod_T": mod_step}
            return of_step(of[name](c) if name in of else steps[name] if name in steps else step[name] + c)

        def unit_done(u):
            unit = units[u]
            if "used" in unit:
                return sem("unit_used"), unit["used"] + 1
            if chunks[unit["chunk"]][0] == "branch":
                p = step["branch"] + 4 * index["branch"].index(unit["chunk"]) + unit["k0"] // 2
                return made[p % 2], 2 * (p // 2) + 2
            return last_product(unit["chunk"])

        def whole_chunk(half, k=KT):
            v = ring[:, half * KT * COL:(half + 1) * KT * COL]
            return v.rearrange("p (k n) -> p k n", k=k)

        @block.sync
        def _(sp):
            for n, (first, count) in ROWS.items():
                v = a[n]
                if n == "w_conv":
                    v = v[0].rearrange("k (j p) -> (k j) p", p=P)
                elif len(v.shape) == 1:
                    v = v.rearrange("(j p) -> j p", p=P)
                else:
                    v = v[0].rearrange("(j p) -> j p", p=P)
                sp.dma_start(VROWS[first:first + count, :], v).then_inc(sem("vec_rows"), 16)
            sp.dma_start(WS, a["w_spatial"][0].rearrange("g t s -> t g s")).then_inc(sem("ws_in"), 16)
            for i, q in enumerate(pieces):
                if i >= RING:
                    for u in pieces[i - RING]["units"]:
                        if units[u]["maker"]:
                            sp.wait_ge(lo_made[units[u]["maker"]], units[u]["lo"] + 1)
                        else:
                            sp.wait_ge(*last_product(units[u]["chunk"]))
                src = chunks[q["chunk"]][1][:, q["k0"]:q["k0"] + q["ks"], :]
                sp.dma_start(raw(i), src).then_inc(landed[i % RING], 16)
            sp.wait_ge(sem("crowded_ready"), 1)
            again = sp.value_load(crowded[0:1, 0:1], min_val=0, max_val=1)
            with sp.If(again == 1):
                for maker in lo_made:
                    sp.wait_ge(lo_made[maker], 1 + max(unit["lo"] for unit in units if unit["maker"] == maker))
                for e in range(NEXP):
                    if e >= 1:
                        sp.wait_ge(sem("rest_down"), e)
                    sp.dma_start(whole_chunk(0), chunks[index["eg"][e]][1]).then_inc(sem("rest_in"), 16)
                    sp.dma_start(whole_chunk(1), chunks[index["eu"][e]][1]).then_inc(sem("rest_in"), 16)
                    sp.wait_ge(sem("rest_up"), e + 1)
                    sp.dma_start(whole_chunk(0, 4), chunks[index["ed"][e]][1]).then_inc(sem("rest_in"), 16)
            for t in range(TT):
                sp.wait_ge(sem("out_ready"), t + 1)
                sp.dma_start(out[0, t * P:(t + 1) * P, :], XN3[:, t, :]).then_inc(sem("out_sent"), 16)
            sp.wait_ge(sem("out_sent"), 16 * TT)

        @block.gpsimd
        def _(pool):
            def load(dst, src, name, n=16):
                pool.dma_start(dst, src).then_inc(sem(name), n)

            roots = [0]

            def root(v):
                roots[0] += 1
                pool.wait_ge(sem("var_ready"), roots[0])
                nc.gpsimd.tensor_tensor(v, v, half_root[:, 0:v.shape[1]], ALU.pow).then_inc(sem("root_ready"), 1)

            def norm_roots(name):
                for t in range(TT):
                    j = 2 * NORM[name] + t
                    root(rs[:, j:j + 1])

            pool.memset(half_root[:, :], -0.5).then_inc(sem("exponent"), 1)
            pool.memset(XC[:, :, 0:2], 0.0).then_inc(sem("pad_ready"), 1)
            pool.wait_ge(sem("exponent"), 1)
            norm_roots("x1")
            load(lnw[:, 0, :], a["gmlp_ln_g"].partition_broadcast(P), "small")
            load(lnw[:, 1, :], a["gmlp_ln_b"].partition_broadcast(P), "small")
            load(qk_g[:, 0, :], a["fox_q_norm_g"].partition_broadcast(P), "small")
            load(qk_g[:, 1, :], a["fox_k_norm_g"].partition_broadcast(P), "small")
            for g in range(4):
                h = 64 * (g % 2)
                load(bs[h:h + 64, g // 2, :], a["b_spatial"][0, g:g + 1, :].partition_broadcast(64), "small")
            load(bf[:, :], a["fox_forget_b"].partition_broadcast(P), "small")
            load(subln[:, :], a["subln_g_2"].partition_broadcast(P), "small2")
            for j, n in enumerate(("lam_q1_2", "lam_k1_2", "lam_q2_2", "lam_k2_2")):
                load(lamv[:, j, :], a[n].partition_broadcast(P), "small2")
            load(rb[:, 0:4], a["b_router_group_2"].partition_broadcast(P), "small2")
            load(rb[:, 4:20], a["b_router_expert_2"].partition_broadcast(P), "small2")
            at_unit = [0]

            def lo_up_to(u):
                while at_unit[0] <= u:
                    if units[at_unit[0]]["maker"] == "pool":
                        make_lo(pool, at_unit[0])
                    at_unit[0] += 1

            def end_of(name, c=-1):
                return units_of[index[name][c]][-1]

            lo_up_to(end_of("in", 2) + 3)
            root(gm[:, 2:4])
            lo_up_to(end_of("in", 4) + 3)
            root(fs[:, 40:56])
            lo_up_to(end_of("out1"))
            norm_roots("x2")
            pool.wait_ge(squares, 2 * NORM["x2"] + 2)
            load(CTX, a["ctx_2"][0].rearrange("(t p) d -> p t d", p=P), "ctx_in")
            norm_roots("ctx")
            lo_up_to(units_of[index["q"][0]][-1])
            norm_roots("x3")
            lo_up_to(end_of("g2"))
            lo_up_to(units_of[index["fo"][0]][1])
            root(ds[:, 32:48])
            lo_up_to(units_of[index["fo"][0]][-1])
            pool.wait_ge(sem("heads_rows"), HEADS2 * TT)
            load(BM[0:1, 0, :], a["b_mod_2"][:, 2 * D:3 * D], "late_in")
            load(BM[0:1, 1, :], a["b_mod_2"][:, 5 * D:6 * D], "late_in")
            load(FINAL, a["final_g_2"].rearrange("(o n) -> o n", o=1).partition_broadcast(P), "late_in")
            load(wr[:, :, 0:4], a["w_router_group_2"][0].rearrange("(k p) n -> p k n", p=P), "late_in")
            load(wr[:, :, 4:20], a["w_router_expert_2"][0].rearrange("(k p) n -> p k n", p=P), "late_in")
            load(IOTA, a["tables"][:, RESIDENT:RESIDENT + WINDOWS * P], "late_in")

            lo_up_to(end_of("out2"))
            norm_roots("x4")
            lo_up_to(len(units) - 1)
            norm_roots("last")

        @block.tensor
        def _(pe):
            mm = nc.tensor.matmul

            def bank_of(j, k):
                return PM[:, k // 2, (k % 2) * SEQ:(k % 2 + 1) * SEQ]

            def turn(name, src):
                j = TURN[name]
                pe.wait_ge(rows_ready, TT * (j + 1))
                for b in range(4):
                    for k in (2 * b, 2 * b + 1):
                        for t in range(TT):
                            last = nc.tensor.transpose(bank_of(j, k)[:, t * P:(t + 1) * P], src[:, t, k * P:(k + 1) * P], ident)
                    last.then_inc(turned, 1)

            second_half = []

            def cols_ready(name):
                pe.wait_ge(cols_dve, 2 * TURN[name] + 1)
                second_half.append(2 * TURN[name] + 2)

            def product(c, outs, first=True, final=True, after_unit=()):
                for n, u in enumerate(units_of[c]):
                    product_unit(u, outs, first, final)
                    if n < len(after_unit):
                        after_unit[n]()

            def product_unit(u, outs, first, final):
                unit = units[u]
                if second_half and unit["k0"] + unit["ks"] > 4 and chunks[unit["chunk"]][0] != "fo":
                    pe.wait_ge(cols_dve, max(second_half))
                    second_half.clear()
                pe.wait_ge(hi_made, unit["split"] + 1)
                pe.wait_ge(lo_made[unit["maker"]], unit["lo"] + 1)
                hi, lo = part(w_hi, u), part(w_lo, u)
                at_end = u == units_of[unit["chunk"]][-1]
                for dst, kind, x_of, sel, opens, (s, n) in outs:
                    for j in range(unit["ks"]):
                        k = unit["k0"] + j
                        a_, b_ = first and k == 0 and opens, final and at_end and j == unit["ks"] - 1
                        xh, xl, wh, wl = x_of(0, k), x_of(1, k), hi[:, j, sel], lo[:, j, sel]
                        if kind == "rows":
                            mm(dst, xh, wh, start=a_, stop=False, skip_group_check=True)
                            mm(dst, xh, wl, start=False, stop=False, skip_group_check=True)
                            last = mm(dst, xl, wh, start=False, stop=b_, skip_group_check=True)
                        else:
                            mm(dst, wh, xh, start=a_, stop=False, skip_group_check=True)
                            mm(dst, wh, xl, start=False, stop=False, skip_group_check=True)
                            last = mm(dst, wl, xh, start=False, stop=b_, skip_group_check=True)
                    if at_end and n:
                        last.then_inc(s, n)
                if not at_end:
                    last.then_inc(sem("unit_used"), 1)

            def tokens(r, t, k0=0, src=None):
                v = place[:, r] if src is None else src
                return lambda h, k: v[:, h, k0 + k, t * P:(t + 1) * P]

            def rows(p, x_of, n=COL):
                return [(bank(p, t)[:, 0:n], "rows", x_of(t), slice(0, n), True, (made[p % 2], 1)) for t in range(TT)]

            def four_cols(p, r, tiles=4):
                return [(bank(p, m // 2)[:, m % 2 * SEQ:(m % 2 + 1) * SEQ], "cols", lambda h, k: place[:, r, h, k, :],
                         slice(m * P, (m + 1) * P), m % 2 == 0,
                         (made[p % 2], m % 2 * (2 if tiles == 2 else 1))) for m in range(tiles)]

            pe.wait_ge(sem("tables_in"), 16)
            pe.wait_ge(sem("vec_rows"), 16 * len(ROWS))
            nc.tensor.transpose(PM[:, 0, 0:N_ROWS], VROWS[0:N_ROWS, :], ident[0:N_ROWS, 0:N_ROWS]).then_inc(sem("consts_turned"), 1)
            pe.wait_ge(sem("ws_in"), 16)
            for g in range(4):
                last = nc.tensor.transpose(PM[:, 1, g * P:(g + 1) * P], WS[:, g, :], ident)
            last.then_inc(sem("consts_turned"), 1)
            pe.wait_ge(sem("consts_read"), 2)
            turn("x1", XN)
            cols_ready("x1")

            i = index["in"][0]
            for c in range(2):
                pair_free_wait(pe, step["in"] + c)
                product(i + c, four_cols(step["in"] + c, 0))
            halves = [slice(0, MIX), slice(MIX, 2 * MIX)]

            def half_rows(p, b, sel, inc=1):
                return [(bank(p, b)[:, t * MIX:(t + 1) * MIX], "rows", tokens(0, t), sel, t == 0, (made[p % 2], t * inc)) for t in range(TT)]

            def half_cols(p, b, start, inc=1):
                return [(bank(p, b)[:, m * SEQ:(m + 1) * SEQ], "cols", lambda h, k: place[:, 0, h, k, :],
                         slice(start + m * P, start + (m + 1) * P), m == 0, (made[p % 2], m * inc)) for m in range(2)]

            p = step["in"] + 2
            pair_free_wait(pe, p)
            product(i + 2, half_rows(p, 0, halves[0]) + half_cols(p, 1, MIX))
            p = step["in"] + 3
            pair_free_wait(pe, p)
            product(i + 3, half_cols(p, 0, 0) + half_rows(p, 1, halves[1]))
            for c in (4, 5):
                pair_free_wait(pe, step["in"] + c)
                product(i + c, rows(step["in"] + c, lambda t: tokens(0, t), n=chunks[i + c][1].shape[2]))

            def stick_scores():
                pe.wait_ge(sem("stick_qk"), 2)
                for hd in range(HEADS1):
                    r, j = HD * (hd % 2), hd // 2
                    mm(PM[:, hd, 0:SEQ], SK[r:r + HD, j, 0:P], SQ[r:r + HD, j, :], start=True, stop=True)
                    last = mm(PM[:, hd, SEQ:384], SK[r:r + HD, j, P:SEQ], SQ[r:r + HD, j, P:SEQ], start=True, stop=True)
                last.then_inc(sem("stick_z"), 1)

            def fox_turn():
                pe.wait_ge(sem("fox_qk"), 1)
                pe.wait_ge(sem("stick_z_read"), 1)
                for j in range(4):
                    for t in range(TT):
                        last = nc.tensor.transpose(PM[:, j // 2, (j % 2) * SEQ + t * P:(j % 2) * SEQ + (t + 1) * P],
                                                   FQK[:, t, j * P:(j + 1) * P], ident)
                last.then_inc(sem("fox_turned"), 1)

            def stick_sums():
                pe.wait_ge(sem("stick_l"), 1)
                pe.wait_ge(sem("fox_T"), 1)
                for hd in range(HEADS1):
                    mm(PM[:, hd, 0:384], tab("from"), T3[:, hd, :], start=True, stop=False)
                    last = mm(PM[:, hd, P:SEQ], ones, T3[:, hd, SEQ:384], start=False, stop=True)
                last.then_inc(sem("stick_c"), 1)

            def weigh(w, v, o, name):
                for hd in range(HEADS1):
                    r, j = HD * (hd % 2), hd // 2
                    dst = o[r:r + HD, j * SEQ:(j + 1) * SEQ]
                    mm(dst, v[:, 0, hd * HD:(hd + 1) * HD], w[:, hd, 0:SEQ], start=True, stop=False)
                    last = mm(dst[:, P:SEQ], v[:, 1, hd * HD:(hd + 1) * HD], w[:, hd, SEQ:384], start=False, stop=True)
                last.then_inc(sem(name), 1)

            def stick_out_and_spatial():
                pe.wait_ge(sem("stick_w"), 1)
                pe.wait_ge(sem("stick_v"), 1)
                weigh(T1, SV, PM[:, 0, :], "stick_o")
                pe.wait_ge(sem("spatial_v"), 1)
                for g in range(4):
                    r, j = HD * (g % 2), g // 2
                    for t in range(TT):
                        last = mm(PM[r:r + HD, 1, j * SEQ + t * P:j * SEQ + (t + 1) * P],
                                  V[:, t, g * HD:(g + 1) * HD], WST[:, g, :], start=True, stop=True)
                last.then_inc(sem("spatial_mix"), 1)

            def fox_scores():
                pe.wait_ge(sem("fox_f"), 1)
                pe.wait_ge(sem("stick_o_read"), 1)
                pe.wait_ge(sem("spatial_read"), 1)
                upto = tab("upto")
                s0, _ = TABLE_AT["upto"]
                upto_ones = tables[:, s0:s0 + 2 * P]
                for hd in range(HEADS1):
                    r, j = HD * (hd % 2), hd // 2
                    q = FT[r:r + HD, j, :]
                    k = FT[r:r + HD, 2 + j, :]
                    s = PM[:, hd, :]
                    mm(s[:, 0:P], q[:, 0:P], k[:, 0:P], start=True, stop=False)
                    mm(s[:, 0:P], NLF[:, 0, hd, :], upto, start=False, stop=False)
                    mm(s[:, 0:P], ident, tab("causal_neg"), start=False, stop=True)
                    mm(s[:, P:384], q[:, P:SEQ], k, start=True, stop=False)
                    mm(s[:, P:384], NLF[:, 0, hd, :], upto_ones, start=False, stop=False)
                    mm(s[:, SEQ:384], NLF[:, 1, hd, :], upto, start=False, stop=False)
                    mm(s[:, SEQ:384], ident, tab("causal_neg"), start=False, stop=True)
                f = PM[:, 0, 384:392]
                mm(f[:, 0:4], upto, NLF[:, 0, :, 0], start=True, stop=True)
                mm(f[:, 4:8], ones, NLF[:, 0, :, 0], start=True, stop=False)
                mm(f[:, 4:8], upto, NLF[:, 1, :, 0], start=False, stop=True).then_inc(sem("fox_s"), 1)

            def fox_probs_turn():
                pe.wait_ge(sem("fox_p"), 1)
                for hd in range(HEADS1):
                    for b in range(3):
                        last = nc.tensor.transpose(PM[:, hd, b * P:(b + 1) * P], T2[:, hd, b * P:(b + 1) * P], ident)
                last.then_inc(sem("fox_p_turned"), 1)

            def fox_out():
                pe.wait_ge(sem("fox_pT"), 1)
                weigh(T3, FV, PM[:, 0, :], "fox_o")

            between = {0: stick_scores, 1: fox_turn, 2: stick_sums, 3: stick_out_and_spatial,
                       4: fox_scores, 5: fox_probs_turn, 6: fox_out}
            for c in range(8):
                pair_free_wait(pe, step["gate"] + c)
                product(index["gate"][c], rows(step["gate"] + c, lambda t: tokens(0, t)))
                if c in between:
                    between[c]()
            pe.wait_ge(sem("branch_T"), 4)
            for half in range(2):
                c = index["branch"][half]
                for u in units_of[c]:
                    unit = units[u]
                    n = unit["k0"] // 2
                    p = step["branch"] + 4 * half + n
                    pair_free_wait(pe, p)
                    pe.wait_ge(hi_made, unit["split"] + 1)
                    pe.wait_ge(lo_made[unit["maker"]], unit["lo"] + 1)
                    hi, lo = part(w_hi, u), part(w_lo, u)
                    for t in range(TT):
                        for k in range(2):
                            xh, xl = (place[:, 1, h, 2 * n + k, t * P:(t + 1) * P] for h in range(2))
                            mm(bank(p, t), xh, hi[:, k, :], start=(k == 0), stop=False)
                            mm(bank(p, t), xh, lo[:, k, :], start=False, stop=False)
                            last = mm(bank(p, t), xl, hi[:, k, :], start=False, stop=(k == 1))
                        last.then_inc(made[p % 2], 1)
            turn("merged", XN)
            cols_ready("merged")
            for half in range(2):
                pair_free_wait(pe, step["out1"] + half)
                product(index["out1"][half], rows(step["out1"] + half, lambda t: tokens(0, t)))
            def whole(c):
                held = sorted({units[u]["piece"] for u in units_of[c]})
                for q in held:
                    landed_wait(pe, q)
                return lambda k: raw(held[k // 4])[:, k % 4, :]

            def modulation(c):
                p = mod_step(c)
                pair_free_wait(pe, p)
                w = whole(index["mod_T"][c])
                for m in range(4):
                    for k in range(KT):
                        last = mm(bank(p, 0)[:, 2 * m:2 * m + 2], w(k)[:, m * P:(m + 1) * P], silu_c[:, k, :], start=(k == 0), stop=(k == KT - 1))
                last.then_inc(made[p % 2], 2)

            pe.wait_ge(sem("silu_c"), 1)
            for c in range(2):
                modulation(c)
            turn("x2", XN)
            cols_ready("x2")

            def up(chunk, p, r):
                pair_free_wait(pe, p)
                product(chunk, four_cols(p, r, tiles=chunks[chunk][1].shape[2] // P))

            def down(r, e):
                return lambda t: tokens(None, t, src=hidden_at(r)[:, e % 2])

            up(index["ffn_g"][0], gate_step(0), 1)
            for c in range(FFN_GROUPS):
                up(index["ffn_u"][c], up_step(c), 1)
                if c + 1 < FFN_GROUPS:
                    up(index["ffn_g"][c + 1], gate_step(c + 1), 1)
                pe.wait_ge(sem("ffn_hidden"), c + 1)
                outs = [(PM[:, 2 * t + half, :], "rows", down(0, c)(t), slice(half * COL, (half + 1) * COL), True,
                         (sem("ffn_made"), t * half)) for t in range(TT) for half in range(2)]
                product(index["ffn_o"][c], outs, first=(c == 0), final=(c == FFN_GROUPS - 1))
                modulation(c + 2)
            pe.wait_ge(sem("x_2"), 4)
            turn("ctx", XN2)
            cols_ready("ctx")
            pe.wait_ge(cols_dve, 2 * TURN["ctx"] + 2)
            turn("x3", X3_ROWS)
            cols_ready("x3")
            for c in range(2):
                pair_free_wait(pe, step["q"] + c)
                product(index["q"][c], four_cols(step["q"] + c, 1))

            def rope_products(j):
                pe.wait_ge(sem("rope_raw"), j + 1)
                if j >= 2:
                    pe.wait_ge(sem("rope_done"), j - 1)
                mm(PM[:, j % 2, :], tab("turn"), RAW[:, j % 2, :, :], start=True, stop=True).then_inc(sem("rope_rot"), 1)

            def pieces_between(j):
                return [lambda: rope_products(j), lambda: rope_products(j + 1)]

            for j in range(2):
                rope_products(j)
            for c in range(2):
                p = step["k"] + 2 * c
                pair_free_wait(pe, p)
                pair_free_wait(pe, p + 1)
                product(index["k"][c], [(bank(p + m // 2, m % 2), "cols", lambda h, k: place[:, :, h, k, :],
                                         slice(m * P, (m + 1) * P), True, (made[(p + m // 2) % 2], 1)) for m in range(4)],
                        after_unit=pieces_between(2 + 2 * c))
            for c in range(2):
                p = step["v"] + 2 * c
                pair_free_wait(pe, p)
                pair_free_wait(pe, p + 1)
                product(index["v"][c], [(bank(p + t // 2, t % 2), "rows", tokens(t // 2, t % 2), slice(0, COL), True,
                                         (made[(p + t // 2) % 2], 1)) for t in range(4)],
                        after_unit=pieces_between(6) if c == 0 else ())
            pair_free_wait(pe, step["f"])
            product(index["f"][0], rows(step["f"], lambda t: tokens(1, t)))
            pe.wait_ge(sem("four_rows"), 2)
            pe.wait_ge(sem("rope_done"), 8)
            dft = tab("dft_tok", TT, 512)
            for g in range(4):
                if g >= 2:
                    pe.wait_ge(sem("four_A"), g - 1)
                for t in range(TT):
                    last = mm(PM[:, g % 2, :], FN[:, t, g * P:(g + 1) * P], dft[:, t, :], start=(t == 0), stop=(t == 1))
                last.then_inc(sem("four_1"), 1)
                pe.wait_ge(sem("four_A"), g + 1)
                if g >= 2:
                    pe.wait_ge(sem("four_B"), g - 1)
                mm(PM[:, 2 + g % 2, 0:SEQ], tab("dft_cos"), DT[:, g % 2, 0:SEQ], start=True, stop=False)
                mm(PM[:, 2 + g % 2, 0:SEQ], tab("dft_nsin"), DT[:, g % 2, SEQ:512], start=False, stop=True).then_inc(sem("four_2"), 1)

            def scores(n):
                hd, t = n // TT, n % TT
                if n >= 1:
                    pe.wait_ge(sem("probs"), 2 * n)
                for c in range(2):
                    last = mm(PM[:, c, :], QT[c * HD:(c + 1) * HD, hd, t * P:(t + 1) * P], KTT[c * HD:(c + 1) * HD, hd, :], start=True, stop=True)
                last.then_inc(sem("scores"), 1)

            def probs_turn(n):
                pe.wait_ge(sem("diff"), n + 1)
                if n >= 1:
                    pe.wait_ge(sem("diff_T"), n)
                for k in range(4):
                    last = nc.tensor.transpose(PM[:, 2, k * P:(k + 1) * P], PP[:, n % 2, 0, k * P:(k + 1) * P], ident)
                last.then_inc(sem("diff_turned"), 1)

            def heads_out(n):
                hd, t = n // TT, n % TT
                pe.wait_ge(sem("diff_T"), n + 1)
                if n >= 1:
                    pe.wait_ge(sem("heads_rows"), n)
                for k in range(4):
                    last = mm(PM[:, 3, 0:P], AA[:, n % 2, k * P:(k + 1) * P], V2[:, k, hd * P:(hd + 1) * P], start=(k == 0), stop=(k == 3))
                last.then_inc(sem("heads_made"), 1)

            pe.wait_ge(sem("four_B"), 4)
            pe.wait_ge(sem("kv_ready"), 8)
            N = HEADS2 * TT
            for n in range(N + 2):
                if n < N:
                    c, q = n // 4, n % 4
                    p = step["g2"] + c
                    if q == 0:
                        pair_free_wait(pe, p)
                    product_unit(units_of[index["g2"][c]][q], rows(p, lambda t: tokens(1, t)), True, True)
                    scores(n)
                if 1 <= n <= N:
                    probs_turn(n - 1)
                if n >= 2:
                    heads_out(n - 2)

            def mod_rows(name, which, c, k0=0, k1=KT):
                p = step["y"] + 2 + 3 * c if name == "mod_g1" else step[name] + c
                if k0 == 0:
                    pair_free_wait(pe, p)
                w = whole(index[name][c])
                for k in range(k0, k1):
                    mm(bank(p, 0), SB[:, k, :], w(k), start=(k == 0), stop=False)
                if k1 == KT:
                    pe.wait_ge(sem("late_in"), 96)
                    mm(bank(p, 0), ones[0:1, :], BM[0:1, which, c * COL:(c + 1) * COL], start=False, stop=True).then_inc(made[p % 2], 2)

            p = step["y"]
            pair_free_wait(pe, p)
            pair_free_wait(pe, p + 1)
            product(index["fo"][0], [(bank(p + half, t), "rows", tokens(None, t, src=four), slice(half * COL, (half + 1) * COL), True,
                                      (made[(p + half) % 2], 1)) for half in range(2) for t in range(TT)])
            pe.wait_ge(sem("sb_ready"), 1)
            mod_rows("mod_g1", 0, 0)
            turn("heads", O)
            cols_ready("heads")
            for half in range(2):
                pair_free_wait(pe, step["y"] + 3 + half)
                product(index["ao"][half], rows(step["y"] + 3 + half, lambda t: tokens(0, t)))
            mod_rows("mod_g1", 0, 1, 0, KT // 2)
            turn("y2", Y)
            mod_rows("mod_g1", 0, 1, KT // 2, KT)
            cols_ready("y2")
            for half in range(2):
                pair_free_wait(pe, step["out2"] + half)
                product(index["out2"][half], rows(step["out2"] + half, lambda t: tokens(1, t)))
            mod_rows("mod_g2", 1, 0)
            turn("x4", XN3)
            cols_ready("x4")
            pe.wait_ge(cols_act, TURN["x4"] + 1)
            for t in range(TT):
                for k in range(KT):
                    last = mm(PM[:, 0, t * 20:(t + 1) * 20], TF2[:, k, t * P:(t + 1) * P], wr[:, k, :], start=(k == 0), stop=(k == KT - 1))
            last.then_inc(sem("logits"), 1)
            mod_rows("mod_g2", 1, 1, 0, KT // 2)
            pe.wait_ge(sem("group_hot"), 1)
            before = tab("strict")[:, 0:P]
            hot0, hot1 = ms[:, 44:48], ms[:, 48:52]
            mm(PM[:, 1, 0:4], before, hot0, start=True, stop=True)
            mm(PM[:, 1, 4:8], ones, hot0, start=True, stop=False)
            mm(PM[:, 1, 4:8], before, hot1, start=False, stop=True)
            mm(PM[:, 1, 8:12], ones, hot0, start=True, stop=False)
            mm(PM[:, 1, 8:12], ones, hot1, start=False, stop=True).then_inc(sem("ranks"), 1)
            mod_rows("mod_g2", 1, 1, KT // 2, KT)

            def side(job):
                kind, g, part_ = job
                j = side_at[job]
                if j >= 1:
                    pe.wait_ge(side_read, j)
                if kind == "gather":
                    for i in range(4):
                        k = 4 * part_ + i
                        for t in range(TT):
                            last = mm(PM[:, 3, i * P:(i + 1) * P], XN3[:, t, k * P:(k + 1) * P], PICK[:, t, g * P:(g + 1) * P],
                                      start=(t == 0), stop=(t == TT - 1))
                else:
                    pe.wait_ge(sem("added"), 2 * PER_GROUP * (g + 1))
                    t, half = part_ // 2, part_ % 2
                    last = mm(PM[:, 3, :], PICK_T[:, g, t * P:(t + 1) * P], ACCG[:, g % 2, half * COL:(half + 1) * COL], start=True, stop=True)
                last.then_inc(side_made, 1)

            pe.wait_ge(sem("picked"), 1)
            side(("gather", 0, 0))
            side(("gather", 0, 1))
            def turned_window(w):
                return PM[:, w // 2, (w % 2) * SEQ:(w % 2 + 1) * SEQ]

            for w in range(WINDOWS):
                for t in range(TT):
                    nc.tensor.transpose(turned_window(w)[:, t * P:(t + 1) * P], PICK[:, t, w * P:(w + 1) * P], ident)
            def group_operand(g):
                return lambda h, k: win_T[:, g % 2, h, k, :]

            def gate_product(e, units_=None):
                p = step["exp"] + e
                outs = [(bank(p, 0), "rows", group_operand(e // PER_GROUP), slice(0, COL), True, (made[p % 2], 1))]
                for u in units_of[index["eg"][e]][units_ or slice(None)]:
                    product_unit(u, outs, True, True)

            def side_after(e, point):
                if (e, point) in SIDE:
                    side(SIDE[e, point])

            pe.wait_ge(sem("xs_ready"), 2)
            pair_free_wait(pe, step["exp"])
            gate_product(0)
            pe.wait_ge(sem("gates_ready"), 1)
            for w in range(WINDOWS):
                for t in range(TT):
                    last = mm(PM[:, 2, SEQ + w * NEXP:SEQ + (w + 1) * NEXP], PICK[:, t, w * P:(w + 1) * P],
                              ms[:, 176 + t * NEXP:176 + (t + 1) * NEXP], start=(t == 0), stop=(t == TT - 1))
            last.then_inc(sem("windows_turned"), 1)
            for e in range(NEXP):
                p = step["exp"] + e
                product(index["eu"][e], [(bank(p, 1), "rows", group_operand(e // PER_GROUP), slice(0, COL), True, (made[p % 2], 1))])
                side_after(e, "up")
                if e + 1 < NEXP:
                    if (e + 1) % PER_GROUP == 0:
                        pe.wait_ge(sem("xs_ready"), 2 * ((e + 1) // PER_GROUP + 1))
                    pair_free_wait(pe, p + 1)
                    gate_product(e + 1, slice(0, 2))
                if e == 0:
                    pe.wait_ge(sem("windows_read"), 1)
                else:
                    pe.wait_ge(sem("hidden"), e)
                pe.wait_ge(sem("hidden_rows"), e + 1)
                for k in range(4):
                    last = nc.tensor.transpose(PM[:, 2, k * P:(k + 1) * P], HROW[:, e % 2, k * P:(k + 1) * P], ident)
                last.then_inc(sem("hidden_turned"), 1)
                if e + 1 < NEXP:
                    gate_product(e + 1, slice(2, 4))
                side_after(e, "gate")
                pe.wait_ge(sem("hidden"), e + 1)
                if e >= 1:
                    pe.wait_ge(sem("added"), 2 * e)
                product(index["ed"][e], [(PM[:, half, :], "rows", lambda h, k: hs[:, e % 2, h, k, :], slice(half * COL, (half + 1) * COL), True,
                                          (sem("expert_made"), 1)) for half in range(2)])
                side_after(e, "down")
            pe.wait_ge(sem("added"), 2 * NEXP)
            pe.wait_ge(side_read, len(side_order))
            g = GROUPS - 1
            for q in range(4):
                t, half = q // 2, q % 2
                mm(PM[:, q, :], PICK_T[:, g, t * P:(t + 1) * P], ACCG[:, g % 2, half * COL:(half + 1) * COL], start=True, stop=True).then_inc(sem("last_sums"), 1)

            pe.wait_ge(sem("crowded_ready"), 1)
            again = pe.value_load(crowded[0:1, 0:1], min_val=0, max_val=1)
            with pe.If(again == 1):
                for p in (step["exp"] + NEXP - 2, step["exp"] + NEXP - 1):
                    pe.wait_ge(freed[p % 2], 2 * (p // 2 + 1))
                w = WINDOWS - 1
                for k in range(KT):
                    for t in range(TT):
                        last = mm(PG[:, k // 4, (k % 4) * P:(k % 4 + 1) * P], XN3[:, t, k * P:(k + 1) * P], PICK[:, t, w * P:(w + 1) * P],
                                  start=(t == 0), stop=(t == TT - 1))
                last.then_inc(sem("rest_made"), 1)
                pe.wait_ge(sem("rest_cols"), 1)
                for e in range(NEXP):
                    for b in range(2):
                        pe.wait_ge(sem("rest_in"), 48 * e + 32)
                        for k in range(KT):
                            last = mm(PG[:, b, :], XO[:, k, :], whole_chunk(b)[:, k, :], start=(k == 0), stop=(k == KT - 1))
                    last.then_inc(sem("rest_up"), 1)
                    pe.wait_ge(sem("rest_hidden"), e + 1)
                    for k in range(4):
                        last = nc.tensor.transpose(PM[:, 2, k * P:(k + 1) * P], HROW[:, 0, k * P:(k + 1) * P], ident)
                    last.then_inc(sem("rest_turned"), 1)
                    pe.wait_ge(sem("rest_hidden_T"), e + 1)
                    pe.wait_ge(sem("rest_in"), 48 * (e + 1))
                    if e >= 1:
                        pe.wait_ge(sem("rest_added"), e)
                    for half in range(2):
                        for k in range(4):
                            last = mm(PM[:, half, :], HO[:, k, :], whole_chunk(0, 4)[:, k, half * COL:(half + 1) * COL], start=(k == 0), stop=(k == 3))
                    last.then_inc(sem("rest_down"), 1)
                pe.wait_ge(sem("rest_added"), NEXP)
                for q in range(4):
                    t, half = q // 2, q % 2
                    last = mm(PG[:, q, :], PICK_T[:, w, t * P:(t + 1) * P], ACCG[:, 0, half * COL:(half + 1) * COL], start=True, stop=True)
                last.then_inc(sem("rest_sums"), 1)

        @block.scalar
        def _(act):
            A = nc.scalar.activation
            chain = [0]

            def link(ins):
                chain[0] += 1
                ins.then_inc(sem("act_chain"), 1)
                act.wait_ge(sem("act_chain"), chain[0])

            at_unit = [0]

            def hi_up_to(u):
                while at_unit[0] <= min(u, len(units) - 1):
                    if units[at_unit[0]]["maker"]:
                        make_hi(act, at_unit[0])
                    at_unit[0] += 1

            def hi_for(name, c=-1):
                hi_up_to(after(units_of[index[name][c]][-1]))

            def take(p, b, out, fn=ACT.Copy, src=None, **kw):
                pair_wait(act, p, b)
                A(out, bank(p, b) if src is None else src, fn, **kw).then_inc(freed[p % 2], 1)

            def norm_squares(name, src, junk):
                j = NORM[name]
                for t in range(TT):
                    A(junk, src[:, t, :], ACT.Square, accum_out=ss[:, 2 * j + t:2 * j + t + 1]).then_inc(squares, 1)
                    act.wait_ge(squares, 2 * j + t + 1)

            def cols(name, r, full, scale=None, shift=None):
                j = TURN[name]
                for k in range(4, KT):
                    if k % 2 == 0:
                        act.wait_ge(turned, 4 * j + k // 2 + 1)
                    src = PM[:, k // 2, (k % 2) * SEQ:(k % 2 + 1) * SEQ]
                    kw = {}
                    fn = ACT.Copy
                    if scale is not None:
                        kw["scale"] = scale(k)
                    if shift is not None:
                        kw["bias"] = shift(k)
                        fn = ACT.Identity
                    link(A(full[:, k, :], src, fn, **kw))
                if r is None:
                    act.nop().then_inc(cols_act, 1)
                else:
                    A(place[:, r, 0, 4:KT, :], full[:, 4:KT, :], ACT.Copy).then_inc(cols_act, 1)

            act.dma_start(x[:, :, :], a["x"][0].rearrange("(t p) d -> p t d", p=P)).then_inc(sem("x_in"), 16)
            act.dma_start(tables[:, :], a["tables"][:, 0:RESIDENT]).then_inc(sem("tables_in"), 16)
            act.wait_ge(sem("x_in"), 16)
            norm_squares("x1", x, JUNK)
            hi_up_to(1)
            act.wait_ge(sem("consts_read"), 2)
            cols("x1", 0, TF, scale=lambda k: feat("norm_mix_g", k))

            p = step["in"]
            hi_for("in", 0)
            take(p, 0, CB)
            take(p, 1, CC)
            hi_for("in", 1)
            pair_wait(act, p + 1, 1)
            A(U, bank(p + 1, 1), ACT.Gelu_apprx_tanh).then_inc(freed[(p + 1) % 2], 1)
            hi_for("in", 2)
            pair_wait(act, p + 2, 0)
            A(V, bank(p + 2, 0), ACT.Gelu_apprx_tanh).then_inc(sem("v_gelu"), 1)
            act.wait_ge(sem("v_gelu"), 1)
            act.nop().then_inc(freed[(p + 2) % 2], 1)
            pair_wait(act, p + 2, 1)
            A(SQ, bank(p + 2, 1), ACT.Copy).then_inc(sem("stick_qk"), 1)
            act.wait_ge(sem("stick_qk"), 1)
            act.nop().then_inc(freed[(p + 2) % 2], 1)
            hi_for("in", 3)
            pair_wait(act, p + 3, 0)
            A(SK, bank(p + 3, 0), ACT.Copy).then_inc(sem("stick_qk"), 1)
            act.wait_ge(sem("stick_qk"), 2)
            act.nop().then_inc(freed[(p + 3) % 2], 1)
            pair_wait(act, p + 3, 1)
            A(SV, bank(p + 3, 1), ACT.Copy).then_inc(sem("stick_v"), 1)
            act.wait_ge(sem("stick_v"), 1)
            act.nop().then_inc(freed[(p + 3) % 2], 1)
            hi_for("in", 4)
            for t in range(TT):
                take(p + 4, t, FQK[:, t, :])
            hi_for("in", 5)
            for t in range(TT):
                pair_wait(act, p + 5, t)
                link(A(FV[:, t, :], bank(p + 5, t)[:, 0:MIX], ACT.Copy))
                A(FR[:, t, :], bank(p + 5, t)[:, MIX:MIX + 4], ACT.Copy).then_inc(freed[(p + 5) % 2], 1)

            def stick_softplus():
                act.wait_ge(sem("stick_z_read"), 1)
                link(A(T2, T1, ACT.Abs))
                link(A(T2, T2, ACT.Exp, scale=-1.0))
                A(T2, T2, ACT.Ln, bias=1.0).then_inc(sem("stick_ln"), 1)

            def fox_T():
                act.wait_ge(sem("fox_turned"), 1)
                link(A(FT[:, 0:2, :], PM[:, 0, :], ACT.Copy))
                A(FT[:, 2:4, :], PM[:, 1, :], ACT.Copy).then_inc(sem("fox_T"), 1)

            def fox_log():
                act.wait_ge(sem("fox_abs"), 1)
                f = fs[:, 0:8]
                link(A(f, FR.rearrange("p t h -> p (t h)"), ACT.Abs))
                link(A(f, f, ACT.Exp, scale=-1.0))
                A(f, f, ACT.Ln, bias=1.0).then_inc(sem("fox_ln"), 1)

            def stick_exp():
                act.wait_ge(sem("stick_logw"), 1)
                A(T1, T1, ACT.Exp).then_inc(sem("stick_w"), 1)

            def fox_exp():
                act.wait_ge(sem("fox_max"), 1)
                for hd in range(HEADS1):
                    for t in range(TT):
                        s = PM[:, hd, 0:P] if t == 0 else PM[:, hd, P:384]
                        d = T2[:, hd, 0:P] if t == 0 else T2[:, hd, P:384]
                        last = A(d, s, ACT.Exp, bias=fs[:, 24 + 4 * t + hd:25 + 4 * t + hd], accum_out=fs[:, 32 + 4 * t + hd:33 + 4 * t + hd])
                        last.then_inc(sem("fox_e"), 1)

            between = {0: (stick_softplus, fox_log), 1: (fox_T,), 2: (stick_exp,), 4: (fox_exp,)}
            for c in range(8):
                hi_for("gate", c)
                for t in range(TT):
                    take(step["gate"] + c, t, sg(c, t), ACT.Sigmoid)
                for f in between.get(c, ()):
                    f()
            A(silu_c[:, :, 0], feats("c_2", 0, 8), ACT.Silu)
            A(silu_c[:, :, 1], feats("c_ctx_2", 0, 8), ACT.Silu).then_inc(sem("silu_c"), 1)
            hi_for("branch", 1)
            cols("merged", 0, TF)
            hi_for("out1", 1)
            act.wait_ge(sem("x_1"), 4)
            norm_squares("x2", x, JUNK)
            cols("x2", 1, TF, scale=lambda k: feat("norm_ffn_g", k))
            for c in range(6):
                p = gate_step(c)
                hi_for("ffn_g", c)
                if c == 2:
                    act.wait_ge(sem("ctx_in"), 16)
                    norm_squares("ctx", CTX, JUNK_CTX)
                if c >= 2:
                    act.wait_ge(sem("ffn_hidden"), c - 1)
                for b in range(2 if c < FFN_GROUPS - 1 else 1):
                    pair_wait(act, p, b)
                    A(SILU[:, c % 2, 2 * b:2 * b + 2, :], bank(p, b), ACT.Silu).then_inc(sem("silu_done"), 1)
                    act.wait_ge(sem("silu_done"), 2 * c + b + 1)
                    act.nop().then_inc(freed[p % 2], 1 if c < FFN_GROUPS - 1 else 2)
            hi_for("ffn_o")
            act.wait_ge(sem("lam_sums"), 2)
            A(ds[:, 2:4], ds[:, 0:2], ACT.Exp).then_inc(sem("lam_exp"), 1)
            hi_up_to(units_of[index["q"][0]][-1])
            act.wait_ge(sem("x_2"), 4)
            norm_squares("x3", x, JUNK2)
            act.wait_ge(sem("mod_cols"), 2)
            cols("ctx", 0, TF, scale=lambda k: modT[:, 1, k, 1:2], shift=lambda k: modT[:, 0, k, 1:2])
            cols("x3", 1, TF, scale=lambda k: modT[:, 1, k, 0:1], shift=lambda k: modT[:, 0, k, 0:1])

            for j in range(4):
                p = step["q"] + j // 2
                hi_for("q", j // 2)
                if j >= 2:
                    act.wait_ge(sem("rope_done"), j - 1)
                pair_wait(act, p, j % 2)
                A(RAW[:, j % 2, :, :], bank(p, j % 2), ACT.Copy).then_inc(sem("rope_raw"), 1)
                act.wait_ge(sem("rope_raw"), j + 1)
                act.nop().then_inc(freed[p % 2], 1)
            for j in range(4):
                p = step["k"] + j
                hi_for("k", j // 2)
                act.wait_ge(sem("rope_done"), 3 + j)
                for b in range(2):
                    pair_wait(act, p, b)
                    link(A(KTT[:, 2 * j + b, 0:SEQ], bank(p, b)[:, 0:SEQ], ACT.Copy))
                    ins = A(RAW[:, j % 2, b, :], bank(p, b)[:, SEQ:512], ACT.Copy)
                    if b == 0:
                        link(ins)
                    else:
                        ins.then_inc(sem("rope_raw"), 1)
                        act.wait_ge(sem("rope_raw"), 5 + j)
                    act.nop().then_inc(freed[p % 2], 1)
            for j in range(4):
                p = step["v"] + j
                hi_for("v", j // 2)
                for b in range(2):
                    pair_wait(act, p, b)
                    c = j // 2
                    A(V2[:, 2 * (j % 2) + b, c * COL:(c + 1) * COL], bank(p, b), ACT.Copy).then_inc(sem("v_copied"), 1)
                    act.wait_ge(sem("v_copied"), 2 * j + b + 1)
                    act.nop().then_inc(freed[p % 2], 1)
            act.nop().then_inc(sem("kv_ready"), 4)
            p = step["f"]
            hi_for("f")
            for t in range(TT):
                pair_wait(act, p, t)
                A(FN[:, t, :], bank(p, t), ACT.Copy).then_inc(sem("four_rows"), 1)
                act.wait_ge(sem("four_rows"), t + 1)
                act.nop().then_inc(freed[p % 2], 1)
            for g in range(4):
                act.wait_ge(sem("four_1"), g + 1)
                if g >= 2:
                    act.wait_ge(sem("four_2"), g - 1)
                A(DT[:, g % 2, :], PM[:, g % 2, :], ACT.Copy).then_inc(sem("four_A"), 1)

            N = HEADS2 * TT
            for n in range(N):
                hi_up_to(after(units_of[index["g2"][n // 4]][n % 4]))
                act.wait_ge(sem("nmax"), n + 1)
                if n >= 2:
                    act.wait_ge(sem("diff_turned"), n - 1)
                for c in range(2):
                    A(PP[:, n % 2, c, :], PM[:, c, :], ACT.Exp, scale=HD ** -0.5, bias=ds[:, 16 + 2 * (n % 2) + c:17 + 2 * (n % 2) + c],
                      accum_out=ds[:, 20 + 2 * (n % 2) + c:21 + 2 * (n % 2) + c]).then_inc(sem("probs"), 1)
                if n % 4 == 3:
                    c = n // 4
                    for t in range(TT):
                        take(step["g2"] + c, t, SG2[:, t, c * COL:(c + 1) * COL], ACT.Sigmoid)
                if n >= 1:
                    act.wait_ge(sem("heads_made"), n)
                    m = n - 1
                    A(O[:, m % TT, (m // TT) * P:(m // TT + 1) * P], PM[:, 3, 0:P], ACT.Copy).then_inc(sem("heads_rows"), 1)
            act.wait_ge(sem("heads_made"), N)
            m = N - 1
            A(O[:, m % TT, (m // TT) * P:(m // TT + 1) * P], PM[:, 3, 0:P], ACT.Copy).then_inc(sem("heads_rows"), 1)
            hi_for("fo")
            act.wait_ge(sem("heads_rows"), N)

            def first_gate(c):
                p = step["y"] + 2 + 3 * c
                pair_wait(act, p, 1)
                A(G1[:, c * COL:(c + 1) * COL], bank(p, 0), ACT.Copy).then_inc(sem("g1_rows"), 1)
                act.wait_ge(sem("g1_rows"), c + 1)
                act.nop().then_inc(freed[p % 2], 2)

            first_gate(0)
            cols("heads", 0, TF2)
            hi_for("ao", 1)
            cols("y2", 1, TF2)
            first_gate(1)
            hi_for("out2", 1)

            def second_gate(c):
                p = step["mod_g2"] + c
                pair_wait(act, p, 1)
                A(G2[:, c * COL:(c + 1) * COL], bank(p, 0), ACT.Copy).then_inc(sem("g2_rows"), 1)
                act.wait_ge(sem("g2_rows"), c + 1)
                act.nop().then_inc(freed[p % 2], 2)

            act.wait_ge(sem("x_3"), 4)
            norm_squares("x4", x, JUNK4)
            second_gate(0)
            cols("x4", None, TF2, scale=lambda k: modT[:, 3, k, 0:1], shift=lambda k: modT[:, 2, k, 0:1])
            hi_up_to(units_of[index["eg"][0]][-1])

            def side(job):
                kind, g, half = job
                if kind == "scatter":
                    return
                n = gathers_before(g, half)
                if n >= 2:
                    act.wait_ge(sem("xs_ready"), n - 1)
                if g >= 2:
                    p = step["exp"] + PER_GROUP * (g - 1) - 1
                    pair_wait(act, p, 1)
                act.wait_ge(side_made, side_at[job] + 1)
                for i in range(4):
                    k = 4 * half + i
                    ins = A(XF[:, k, :], PM[:, 3, i * P:(i + 1) * P], ACT.Identity, scale=modT[:, 3, k, 0:1], bias=modT[:, 2, k, 0:1])
                    if i < 3:
                        link(ins)
                ins.then_inc(side_read, 1)
                act.wait_ge(side_read, side_at[job] + 1)
                A(win_T[:, g % 2, 0, 4 * half:4 * half + 4, :], XF[:, 4 * half:4 * half + 4, :], ACT.Copy).then_inc(sem("xs_hi"), 1)

            def side_after(e, point):
                if (e, point) in SIDE:
                    side(SIDE[e, point])

            act.wait_ge(sem("route_d"), 1)
            A(ms[:, 80:88], ms[:, 72:80], ACT.Exp).then_inc(sem("route_e"), 1)
            second_gate(1)
            side(("gather", 0, 0))
            side(("gather", 0, 1))
            hi_for("eg", 0)
            act.wait_ge(sem("route_r"), 1)
            A(ms[:, 130:132], ms[:, 128:130], ACT.Exp).then_inc(sem("route_e"), 1)
            for e in range(NEXP):
                p = step["exp"] + e
                pair_wait(act, p, 0)
                if e >= 2:
                    act.wait_ge(sem("hidden_rows"), e - 1)
                A(SL[:, e % 2, :], bank(p, 0), ACT.Silu).then_inc(sem("exp_silu"), 1)
                act.wait_ge(sem("exp_silu"), e + 1)
                act.nop().then_inc(freed[p % 2], 1)
                hi_for("eu", e)
                side_after(e, "up")
                if e + 1 < NEXP:
                    hi_up_to(after(units_of[index["eg"][e + 1]][1], 4))
                act.wait_ge(sem("hidden_turned"), e + 1)
                if e >= 2:
                    act.wait_ge(sem("expert_made"), 2 * (e - 1))
                A(hs[:, e % 2, 0, :, :], PM[:, 2, :].rearrange("p (k q) -> p k q", k=4), ACT.Copy).then_inc(sem("hidden_hi"), 1)
                if e + 1 < NEXP:
                    hi_for("eg", e + 1)
                side_after(e, "gate")
                hi_for("ed", e)
                side_after(e, "down")
            act.wait_ge(sem("crowded_ready"), 1)
            again = act.value_load(crowded[0:1, 0:1], min_val=0, max_val=1)
            with act.If(again == 1):
                for e in range(NEXP):
                    act.wait_ge(sem("rest_up"), e + 1)
                    A(SL[:, 0, :], PG[:, 0, :], ACT.Silu).then_inc(sem("rest_silu"), 1)
            act.wait_ge(sem("x_4"), 2)
            norm_squares("last", x, JUNK3)

        @block.vector
        def _(dve):
            V_ = nc.vector
            chain = [0]

            def link(ins):
                chain[0] += 1
                ins.then_inc(sem("vec_chain"), 1)
                dve.wait_ge(sem("vec_chain"), chain[0])

            roots = [0]

            def inv_sqrt(ins):
                roots[0] += 1
                ins.then_inc(sem("var_ready"), 1)
                dve.wait_ge(sem("root_ready"), roots[0])

            def norm_rows(name, src, dst, g_turn):
                j = NORM[name]
                for t in range(TT):
                    s, r = ss[:, 2 * j + t:2 * j + t + 1], rs[:, 2 * j + t:2 * j + t + 1]
                    dve.wait_ge(squares, 2 * j + t + 1)
                    inv_sqrt(V_.tensor_scalar(r, s, 1.0 / D, EPS, ALU.mult, ALU.add))
                    ins = V_.tensor_scalar(dst[:, t, :], src[:, t, :], r, None, ALU.mult)
                    if g_turn:
                        ins.then_inc(rows_ready, 1)
                    else:
                        link(ins)

            at_unit = [0]

            def lo_up_to(u):
                while at_unit[0] <= min(u, len(units) - 1):
                    if units[at_unit[0]]["maker"] == "dve":
                        make_lo(dve, at_unit[0])
                    at_unit[0] += 1

            def lo_for(name, c=-1):
                lo_up_to(after(units_of[index[name][c]][-1]))

            def split(dst_hi, dst_lo, src, last_sem):
                link(V_.tensor_copy(dst_hi, src))
                V_.tensor_tensor(dst_lo, src, dst_hi, ALU.subtract).then_inc(sem(last_sem), 1)

            def cols(name, r, full, scale=None, shift=None):
                j = TURN[name]
                for k in range(4):
                    if k % 2 == 0:
                        dve.wait_ge(turned, 4 * j + k // 2 + 1)
                    src = PM[:, k // 2, (k % 2) * SEQ:(k % 2 + 1) * SEQ]
                    if scale is None:
                        ins = V_.tensor_copy(full[:, k, :], src)
                    elif shift is None:
                        ins = V_.tensor_scalar(full[:, k, :], src, scale(k), None, ALU.mult)
                    else:
                        ins = V_.tensor_scalar(full[:, k, :], src, scale(k), shift(k), ALU.mult, ALU.add)
                if r is None:
                    ins.then_inc(cols_dve, 2)
                    return
                link(ins)
                link(V_.tensor_copy(place[:, r, 0, 0:4, :], full[:, 0:4, :]))
                V_.tensor_tensor(place[:, r, 1, 0:4, :], full[:, 0:4, :], place[:, r, 0, 0:4, :], ALU.subtract).then_inc(cols_dve, 1)
                dve.wait_ge(cols_act, j + 1)
                V_.tensor_tensor(place[:, r, 1, 4:KT, :], full[:, 4:KT, :], place[:, r, 0, 4:KT, :], ALU.subtract).then_inc(cols_dve, 1)

            def modulation(c):
                p = mod_step(c)
                part, half = c // 2, c % 2
                pair_wait(dve, p, 1)
                b0 = (0, 1, 3, 4)[part] * 8 + 4 * half
                dst = modT[:, part, 4 * half:4 * half + 4, :]
                V_.tensor_tensor(dst, bank(p, 0)[:, 0:8].rearrange("p (m c) -> p m c", c=2),
                                 feats("b_mod_2", b0, 4).unsqueeze(2).to_broadcast([P, 4, 2]), ALU.add).then_inc(freed[p % 2], 2)
                dve.wait_ge(freed[p % 2], 2 * (p // 2 + 1))
                if c in (3, 7):
                    g = "norm1_g_2" if c == 3 else "norm2_g_2"
                    V_.scalar_tensor_tensor(modT[:, part, :, :], modT[:, part, :, :], 1.0,
                                            feats(g, 0, 8).unsqueeze(2).to_broadcast([P, KT, 2]), ALU.add, ALU.mult).then_inc(sem("mod_cols"), 1)

            dve.wait_ge(sem("consts_turned"), 1)
            V_.tensor_copy(feat_cols[:, :], PM[:, 0, 0:N_ROWS]).then_inc(sem("consts_read"), 1)
            dve.wait_ge(sem("consts_turned"), 2)
            dve.wait_ge(sem("tables_in"), 16)
            V_.tensor_tensor(WST, PM[:, 1, :].rearrange("p (g t) -> p g t", g=4), tab("upto").unsqueeze(1).to_broadcast([P, 4, P]),
                             ALU.mult).then_inc(sem("consts_read"), 1)
            dve.wait_ge(sem("x_in"), 16)
            norm_rows("x1", x, XN, True)
            lo_up_to(1)
            dve.wait_ge(sem("consts_read"), 2)
            cols("x1", 0, TF, scale=lambda k: feat("norm_mix_g", k))
            lo_up_to(units_of[1][-1])

            p = step["in"]
            pair_wait(dve, p + 1, 0)
            dve.wait_ge(sem("pad_ready"), 1)
            dve.wait_ge(freed[p % 2], 2)
            V_.tensor_tensor(XC[:, :, 2:SEQ + 2], CC, bank(p + 1, 0).rearrange("p (j q) -> p j q", j=2), ALU.mult).then_inc(freed[(p + 1) % 2], 1)
            dve.wait_ge(freed[(p + 1) % 2], 2)
            for j in range(2):
                y = CC[:, j, :]
                link(V_.tensor_scalar(y, XC[:, j, 0:SEQ], feat("w_conv", j), None, ALU.mult))
                link(V_.scalar_tensor_tensor(y, XC[:, j, 1:SEQ + 1], feat("w_conv", 2 + j), y, ALU.mult, ALU.add))
                link(V_.scalar_tensor_tensor(y, XC[:, j, 2:SEQ + 2], feat("w_conv", 4 + j), y, ALU.mult, ALU.add))
            link(V_.tensor_tensor(CC, CC, CB, ALU.mult))
            split(place[:, 1, 0, 0:2, :], place[:, 1, 1, 0:2, :], CC, "branch_T")

            dve.wait_ge(sem("v_gelu"), 1)
            dve.wait_ge(sem("small"), 16 * 9)
            mean, var = gm[:, 0:2], gm[:, 2:4]
            link(V_.tensor_reduce(mean, V, AX.X, ALU.add))
            link(V_.tensor_scalar(mean, mean, 1.0 / MIX, None, ALU.mult))
            for t in range(TT):
                link(V_.tensor_scalar(V[:, t, :], V[:, t, :], mean[:, t:t + 1], None, ALU.subtract))
            sq = TMP[:, :, 0:MIX]
            link(V_.tensor_tensor(sq, V, V, ALU.mult))
            link(V_.tensor_reduce(var, sq, AX.X, ALU.add))
            inv_sqrt(V_.tensor_scalar(var, var, 1.0 / MIX, EPS, ALU.mult, ALU.add))
            for t in range(TT):
                link(V_.scalar_tensor_tensor(V[:, t, :], V[:, t, :], var[:, t:t + 1], lnw[:, 0, :], ALU.mult, ALU.mult))
            V_.tensor_tensor(V, V, lnw[:, 1, :].unsqueeze(1).to_broadcast([P, TT, MIX]), ALU.add).then_inc(sem("spatial_v"), 1)

            dve.wait_ge(freed[(p + 4) % 2], 2 * ((p + 4) // 2 + 1))
            nh = 2 * HEADS1
            heads = FQK.rearrange("p t (h d) -> p t h d", d=HD)
            sq4 = TMP
            r = fs[:, 40:40 + 2 * nh].rearrange("p (t h) -> p t h", t=TT)
            link(V_.tensor_tensor(sq4, FQK, FQK, ALU.mult))
            link(V_.tensor_reduce(r, sq4.rearrange("p t (h d) -> p t h d", d=HD), AX.X, ALU.add))
            inv_sqrt(V_.tensor_scalar(r, r, 1.0 / HD, EPS, ALU.mult, ALU.add))
            link(V_.tensor_scalar(r[:, :, 0:HEADS1], r[:, :, 0:HEADS1], HD ** -0.5, None, ALU.mult))
            link(V_.tensor_tensor(heads, heads, r.unsqueeze(3).to_broadcast([P, TT, nh, HD]), ALU.mult))
            for n in range(2):
                hv = heads[:, :, n * HEADS1:(n + 1) * HEADS1, :]
                for t in range(TT):
                    ins = V_.tensor_tensor(hv[:, t], hv[:, t], qk_g[:, n, :].unsqueeze(1).to_broadcast([P, HEADS1, HD]), ALU.mult)
                    if (n, t) == (1, TT - 1):
                        ins.then_inc(sem("fox_qk"), 1)
                    else:
                        link(ins)
            dve.wait_ge(freed[(p + 5) % 2], 2 * ((p + 5) // 2 + 1))
            V_.tensor_tensor(FR, FR, bf[:, :].unsqueeze(1).to_broadcast([P, TT, HEADS1]), ALU.add).then_inc(sem("fox_abs"), 1)
            dve.wait_ge(sem("fox_abs"), 1)
            fflat = FR.rearrange("p t h -> p (t h)")
            link(V_.tensor_scalar(fs[:, 8:16], fflat, 0.0, None, ALU.min))

            dve.wait_ge(sem("stick_z"), 1)
            V_.tensor_scalar(T1, PM[:, :, 0:384], HD ** -0.5, None, ALU.mult).then_inc(sem("stick_z_read"), 1)
            dve.wait_ge(sem("stick_z_read"), 1)
            link(V_.tensor_scalar(T3, T1, 0.0, None, ALU.max))
            dve.wait_ge(sem("stick_ln"), 1)
            link(V_.tensor_tensor(T3, T3, T2, ALU.add))
            V_.tensor_tensor(T3, T3, tab("strict").unsqueeze(1).to_broadcast([P, 4, 384]), ALU.mult).then_inc(sem("stick_l"), 1)
            link(V_.tensor_tensor(T1, T1, tab("strict_neg").unsqueeze(1).to_broadcast([P, 4, 384]), ALU.add))
            dve.wait_ge(sem("fox_ln"), 1)
            link(V_.tensor_tensor(fs[:, 0:8], fs[:, 0:8], fs[:, 8:16], ALU.subtract))
            V_.tensor_copy(NLF.rearrange("p t h n -> p (t h) n"), fs[:, 0:8].unsqueeze(2).to_broadcast([P, 8, P])).then_inc(sem("fox_f"), 1)
            dve.wait_ge(sem("stick_c"), 1)
            V_.tensor_tensor(T1, T1, PM[:, :, 0:384], ALU.subtract).then_inc(sem("stick_logw"), 1)

            dve.wait_ge(sem("spatial_mix"), 1)
            dve.wait_ge(freed[(p + 1) % 2], 2)
            m4 = PM[:, 1, :].rearrange("p (j t n) -> p j t n", j=2, t=TT)
            mixed = XC[:, :, 0:SEQ]
            y4 = mixed.rearrange("p j (t n) -> p j t n", t=TT)
            for j in range(2):
                ins = V_.tensor_tensor(y4[:, j], m4[:, j], bs[:, j, :].unsqueeze(1).to_broadcast([P, TT, P]), ALU.add)
                if j == 0:
                    link(ins)
                else:
                    ins.then_inc(sem("spatial_read"), 1)
            dve.wait_ge(sem("spatial_read"), 1)
            link(V_.tensor_tensor(U, mixed, U, ALU.mult))
            split(place[:, 1, 0, 2:4, :], place[:, 1, 1, 2:4, :], U, "branch_T")
            dve.wait_ge(sem("stick_o"), 1)
            o = PM[:, 0, :].rearrange("p (j q) -> p j q", j=2)
            split(place[:, 1, 0, 4:6, :], place[:, 1, 1, 4:6, :], o, "branch_T")
            dve.wait_ge(sem("branch_T"), 3)
            V_.nop().then_inc(sem("stick_o_read"), 1)

            dve.wait_ge(sem("fox_s"), 1)
            mx = fs[:, 16:24]
            link(V_.tensor_reduce(mx[:, 0:4], PM[:, :, 0:P], AX.X, ALU.max))
            link(V_.tensor_reduce(mx[:, 4:8], PM[:, :, P:384], AX.X, ALU.max))
            nF = fs[:, 60:68]
            link(V_.tensor_copy(nF, PM[:, 0, 384:392]))
            link(V_.tensor_tensor(mx, mx, nF, ALU.subtract))
            link(V_.tensor_tensor(fs[:, 24:32], mx, nF, ALU.add))
            V_.tensor_scalar(fs[:, 24:32], fs[:, 24:32], -1.0, None, ALU.mult).then_inc(sem("fox_max"), 1)
            dve.wait_ge(sem("fox_e"), 8)
            link(V_.reciprocal(fs[:, 32:40], fs[:, 32:40]))
            link(V_.tensor_tensor(T2[:, :, 0:P], T2[:, :, 0:P], fs[:, 32:36].unsqueeze(2).to_broadcast([P, 4, P]), ALU.mult))
            V_.tensor_tensor(T2[:, :, P:384], T2[:, :, P:384], fs[:, 36:40].unsqueeze(2).to_broadcast([P, 4, 2 * P]), ALU.mult).then_inc(sem("fox_p"), 1)
            dve.wait_ge(sem("fox_p_turned"), 1)
            V_.tensor_copy(T3, PM[:, :, 0:384]).then_inc(sem("fox_pT"), 1)
            dve.wait_ge(sem("fox_o"), 1)
            split(place[:, 1, 0, 6:8, :], place[:, 1, 1, 6:8, :], o, "branch_T")

            for half in range(2):
                for n in range(4):
                    p = step["branch"] + 4 * half + n
                    for t in range(TT):
                        pair_wait(dve, p, t)
                        if (half, n, t) == (0, 0, 0):
                            dve.wait_ge(freed[(step["gate"] + 7) % 2], 2 * ((step["gate"] + 7) // 2 + 1))
                            dve.wait_ge(freed[(step["gate"] + 6) % 2], 2 * ((step["gate"] + 6) // 2 + 1))
                        g = sg(2 * n + half, t)
                        m = XN[:, t, half * COL:(half + 1) * COL]
                        if n == 0:
                            V_.tensor_tensor(m, g, bank(p, t), ALU.mult).then_inc(freed[p % 2], 1)
                        else:
                            tmp = TMP[:, t, :]
                            V_.tensor_tensor(tmp, g, bank(p, t), ALU.mult).then_inc(freed[p % 2], 1)
                            dve.wait_ge(freed[p % 2], 2 * (p // 2) + t + 1)
                            ins = V_.tensor_tensor(m, m, tmp, ALU.add)
                            if half == 1 and n == 3:
                                ins.then_inc(rows_ready, 1)
                            else:
                                link(ins)
            cols("merged", 0, TF)
            for half in range(2):
                p = step["out1"] + half
                for t in range(TT):
                    pair_wait(dve, p, t)
                    xs = x[:, t, half * COL:(half + 1) * COL]
                    V_.tensor_tensor(xs, xs, bank(p, t), ALU.add).then_inc(sem("x_1"), 1)
                    dve.wait_ge(sem("x_1"), 2 * half + t + 1)
                    V_.nop().then_inc(freed[p % 2], 1)
            lo_for("out1")
            norm_rows("x2", x, XN, True)
            for c in range(2):
                modulation(c)
            cols("x2", 1, TF, scale=lambda k: feat("norm_ffn_g", k))
            def first_gather():
                lo_up_to(units_of[index["eg"][0]][-1])
                for half in range(2):
                    dve.wait_ge(sem("xs_hi"), half + 1)
                    V_.tensor_tensor(win_T[:, 0, 1, 4 * half:4 * half + 4, :], XF[:, 4 * half:4 * half + 4, :], win_T[:, 0, 0, 4 * half:4 * half + 4, :],
                                     ALU.subtract).then_inc(sem("xs_ready"), 1)

            def hidden(p, buf, dst, tiles, done):
                for b in range(tiles // 2):
                    pair_wait(dve, p, b)
                    V_.tensor_tensor(buf[:, 2 * b:2 * b + 2, :], buf[:, 2 * b:2 * b + 2, :],
                                     bank(p, b).rearrange("p (j q) -> p j q", j=2), ALU.mult).then_inc(freed[p % 2], 1 if tiles == 4 else 2)
                dve.wait_ge(freed[p % 2], 2 * (p // 2 + 1))
                split(dst[:, 0, 0:tiles, :], dst[:, 1, 0:tiles, :], buf[:, 0:tiles, :], done)

            for c in range(FFN_GROUPS):
                lo_for("ffn_u", c)
                dve.wait_ge(sem("silu_done"), 2 * c + (2 if c < FFN_GROUPS - 1 else 1))
                if c >= 2:
                    dve.wait_ge(sem("ffn_made"), c - 1)
                if c >= 1:
                    modulation(c + 1)
                hidden(up_step(c), SILU[:, c % 2], hidden_at(0)[:, c % 2],
                       4 if c < FFN_GROUPS - 1 else 2, "ffn_hidden")
                if c == 3:
                    dve.wait_ge(sem("ctx_in"), 16)
                    norm_rows("ctx", CTX, XN2, True)
            lo_for("ffn_o")
            dve.wait_ge(sem("small2"), 16 * 7)
            for j in range(2):
                link(V_.tensor_tensor(lamv[:, 2 * j, :], lamv[:, 2 * j, :], lamv[:, 2 * j + 1, :], ALU.mult))
                V_.tensor_reduce(ds[:, j:j + 1], lamv[:, 2 * j, :], AX.X, ALU.add).then_inc(sem("lam_sums"), 1)
            dve.wait_ge(sem("lam_exp"), 1)
            link(V_.tensor_tensor(ds[:, 4:5], ds[:, 2:3], ds[:, 3:4], ALU.subtract))
            lam = ds[:, 5:6]
            link(V_.tensor_scalar(lam, ds[:, 4:5], 0.2, None, ALU.add))
            link(V_.tensor_scalar(subln[:, :], subln[:, :], 0.8, None, ALU.mult))
            dve.wait_ge(sem("ffn_made"), FFN_GROUPS)
            for t in range(TT):
                for half in range(2):
                    xs = x[:, t, half * COL:(half + 1) * COL]
                    V_.tensor_tensor(xs, xs, PM[:, 2 * t + half, :], ALU.add).then_inc(sem("x_2"), 1)
            modulation(7)
            dve.wait_ge(sem("x_2"), 4)
            norm_rows("x3", x, X3_ROWS, True)
            dve.wait_ge(sem("mod_cols"), 2)
            cols("ctx", 0, TF, scale=lambda k: modT[:, 1, k, 1:2], shift=lambda k: modT[:, 0, k, 1:2])
            cols("x3", 1, TF, scale=lambda k: modT[:, 1, k, 0:1], shift=lambda k: modT[:, 0, k, 0:1])

            for j in range(8):
                dst = QT[:, 2 * j:2 * j + 2, :] if j < 4 else KTT[:, 2 * (j - 4):2 * (j - 4) + 2, SEQ:2 * SEQ]
                raw, rot = RAW[:, j % 2, :, :], ROT[:, j % 2, :, :]
                dve.wait_ge(sem("rope_raw"), j + 1)
                dve.wait_ge(sem("rope_rot"), j + 1)
                link(V_.tensor_tensor(rot, PM[:, j % 2, :].rearrange("p (a q) -> p a q", a=2),
                                      tab("sin").unsqueeze(1).to_broadcast([P, 2, SEQ]), ALU.mult))
                link(V_.tensor_tensor(dst, raw, tab("cos").unsqueeze(1).to_broadcast([P, 2, SEQ]), ALU.mult))
                V_.tensor_tensor(dst, dst, rot, ALU.add).then_inc(sem("rope_done"), 1)
                dve.wait_ge(sem("rope_done"), j + 1)
            V_.nop().then_inc(sem("kv_ready"), 4)
            for g in range(4):
                dve.wait_ge(sem("four_2"), g + 1)
                split(four[:, 0, g, :], four[:, 1, g, :], PM[:, 2 + g % 2, 0:SEQ], "four_B")

            N = HEADS2 * TT
            for n in range(N):
                nm = ds[:, 16 + 2 * (n % 2):18 + 2 * (n % 2)]
                sums = ds[:, 20 + 2 * (n % 2):22 + 2 * (n % 2)]
                dve.wait_ge(sem("scores"), n + 1)
                link(V_.tensor_reduce(ds[:, 8:10], PM[:, 0:2, :], AX.X, ALU.max))
                V_.tensor_scalar(nm, ds[:, 8:10], -HD ** -0.5, None, ALU.mult).then_inc(sem("nmax"), 1)
                if n >= 1:
                    dve.wait_ge(sem("diff_turned"), n)
                    if n >= 3:
                        dve.wait_ge(sem("heads_made"), n - 2)
                    V_.tensor_copy(AA[:, (n - 1) % 2, :], PM[:, 2, :]).then_inc(sem("diff_T"), 1)
                dve.wait_ge(sem("probs"), 2 * n + 2)
                link(V_.reciprocal(ds[:, 12:14], sums))
                link(V_.tensor_tensor(ds[:, 14:15], ds[:, 13:14], lam, ALU.mult))
                link(V_.tensor_scalar(PP[:, n % 2, 1, :], PP[:, n % 2, 1, :], ds[:, 14:15], None, ALU.mult))
                V_.scalar_tensor_tensor(PP[:, n % 2, 0, :], PP[:, n % 2, 0, :], ds[:, 12:13], PP[:, n % 2, 1, :],
                                        ALU.mult, ALU.subtract).then_inc(sem("diff"), 1)
            dve.wait_ge(sem("diff_turned"), N)
            V_.tensor_copy(AA[:, (N - 1) % 2, :], PM[:, 2, :]).then_inc(sem("diff_T"), 1)
            V_.tensor_copy(SB, silu_c[:, :, 0:1].to_broadcast([P, KT, P])).then_inc(sem("sb_ready"), 1)
            dve.wait_ge(sem("heads_rows"), N)
            hv = O.rearrange("p t (h d) -> p (t h) d", d=P)
            sq = XN3.rearrange("p t (h d) -> p (t h) d", d=P)
            r = ds[:, 32:48]
            link(V_.tensor_tensor(sq, hv, hv, ALU.mult))
            link(V_.tensor_reduce(r, sq, AX.X, ALU.add))
            inv_sqrt(V_.tensor_scalar(r, r, 1.0 / P, EPS, ALU.mult, ALU.add))
            link(V_.tensor_tensor(hv, hv, r.unsqueeze(2).to_broadcast([P, 16, P]), ALU.mult))
            for t in range(TT):
                ht = O[:, t, :].rearrange("p (h d) -> p h d", d=P)
                V_.tensor_tensor(ht, ht, subln[:, :].unsqueeze(1).to_broadcast([P, HEADS2, P]), ALU.mult).then_inc(rows_ready, 1)
            for half in range(2):
                p = step["y"] + half
                for t in range(TT):
                    pair_wait(dve, p, t)
                    g = SG2[:, t, D + half * COL:D + (half + 1) * COL]
                    V_.tensor_tensor(Y[:, t, half * COL:(half + 1) * COL], g, bank(p, t), ALU.mult).then_inc(freed[p % 2], 1)
            cols("heads", 0, TF2)
            for half in range(2):
                p = step["y"] + 3 + half
                for t in range(TT):
                    pair_wait(dve, p, t)
                    g = SG2[:, t, half * COL:(half + 1) * COL]
                    tmp = XN3[:, t, 0:COL]
                    ys = Y[:, t, half * COL:(half + 1) * COL]
                    V_.tensor_tensor(tmp, g, bank(p, t), ALU.mult).then_inc(freed[p % 2], 1)
                    dve.wait_ge(freed[p % 2], 2 * (p // 2) + t + 1)
                    ins = V_.tensor_tensor(ys, ys, tmp, ALU.add)
                    if half == 1:
                        ins.then_inc(rows_ready, 1)
                    else:
                        link(ins)
            cols("y2", 1, TF2)
            dve.wait_ge(sem("g1_rows"), 2)
            for half in range(2):
                p = step["out2"] + half
                for t in range(TT):
                    pair_wait(dve, p, t)
                    xs = x[:, t, half * COL:(half + 1) * COL]
                    tmp = XN3[:, t, half * COL:(half + 1) * COL]
                    V_.tensor_tensor(tmp, G1[:, half * COL:(half + 1) * COL], bank(p, t), ALU.mult).then_inc(freed[p % 2], 1)
                    dve.wait_ge(freed[p % 2], 2 * (p // 2) + t + 1)
                    V_.tensor_tensor(xs, xs, tmp, ALU.add).then_inc(sem("x_3"), 1)
                    dve.wait_ge(sem("x_3"), 2 * half + t + 1)
            norm_rows("x4", x, XN3, True)
            cols("x4", None, TF2, scale=lambda k: modT[:, 3, k, 0:1], shift=lambda k: modT[:, 2, k, 0:1])

            dve.wait_ge(sem("logits"), 1)
            L = ms[:, 0:40].rearrange("p (t n) -> p t n", t=TT)
            V_.tensor_tensor(L, PM[:, 0, 0:40].rearrange("p (t n) -> p t n", t=TT), rb[:, :].unsqueeze(1).to_broadcast([P, TT, 20]),
                             ALU.add).then_inc(sem("logits_read"), 1)
            dve.wait_ge(sem("logits_read"), 1)
            lg, le = L[:, :, 0:4], L[:, :, 4:20]
            rev = tab("rev").unsqueeze(1).to_broadcast([P, TT, 4])

            def small(s, n):
                return ms[:, s:s + TT * n].rearrange("p (t n) -> p t n", t=TT) if n > 1 else ms[:, s:s + TT]

            def spread(v, n=4):
                return v.unsqueeze(2).to_broadcast([P, TT, n])

            def first_max(src, top, hot, tmp):
                link(V_.tensor_reduce(top, src, AX.X, ALU.max))
                link(V_.tensor_tensor(hot, src, spread(top), ALU.is_equal))
                link(V_.tensor_tensor(hot, hot, rev, ALU.mult))
                link(V_.tensor_reduce(tmp, hot, AX.X, ALU.max))
                link(V_.tensor_tensor(hot, hot, spread(tmp), ALU.is_equal))

            gmax, ghot, t1 = small(40, 1), small(44, 4), small(42, 1)
            first_max(lg, gmax, ghot, t1)
            V_.nop().then_inc(sem("group_hot"), 1)
            V_.tensor_tensor(small(72, 4), lg, spread(gmax), ALU.subtract).then_inc(sem("route_d"), 1)
            first, late, flag = place_of[:, 0:2], place_of[:, 2:4], place_of[:, 4:5]
            order, slot = place_of[:, 5:7], st[:, 48:50]
            link(V_.tensor_tensor(rank, ghot, rev, ALU.mult))
            link(V_.tensor_reduce(first, rank, AX.X, ALU.add))
            link(V_.tensor_scalar(first, first, -P, GROUPS * P, ALU.mult, ALU.add))
            dve.wait_ge(sem("ranks"), 1)
            link(V_.tensor_tensor(rank, PM[:, 1, 0:8].rearrange("p (t g) -> p t g", t=TT), ghot, ALU.mult))
            link(V_.tensor_reduce(flag, PM[:, 1, 8:12], AX.X, ALU.max))
            link(V_.tensor_reduce(order, rank, AX.X, ALU.add))
            link(V_.tensor_scalar(late, order, P, None, ALU.is_ge))
            link(V_.tensor_tensor(slot, first, order, ALU.add))
            link(V_.tensor_scalar(first, first, -1.0, (GROUPS - 1) * P, ALU.mult, ALU.add))
            link(V_.tensor_tensor(first, first, late, ALU.mult))
            link(V_.tensor_tensor(slot, slot, first, ALU.add))
            dve.wait_ge(sem("late_in"), 96)
            for t in range(TT):
                ins = V_.tensor_scalar(PICK[:, t, :], IOTA, slot[:, t:t + 1], None, ALU.is_equal)
                if t < TT - 1:
                    link(ins)
            ins.then_inc(sem("picked"), 1)
            link(V_.tensor_scalar(flag, flag, P, None, ALU.is_gt))
            V_.tensor_copy(crowded[0:1, 0:1], flag[0:1, :]).then_inc(sem("crowded_ready"), 1)
            first_gather()
            prod = ms[:, 144:176].rearrange("p (t g e) -> p t g e", t=TT, g=4)
            for t in range(TT):
                link(V_.tensor_tensor(prod[:, t], le[:, t, :].rearrange("p (g e) -> p g e", g=4),
                                      ghot[:, t, :].unsqueeze(2).to_broadcast([P, 4, 4]), ALU.mult))
            leg = small(52, 4)
            for t in range(TT):
                link(V_.tensor_reduce(leg[:, t, :], prod[:, t].rearrange("p g e -> p e g"), AX.X, ALU.add))
            v1, h1, v2, h2 = small(60, 1), small(92, 4), small(62, 1), small(100, 4)
            first_max(leg, v1, h1, t1)
            rest = small(108, 4)
            link(V_.scalar_tensor_tensor(rest, h1, NEG, leg, ALU.mult, ALU.add))
            first_max(rest, v2, h2, t1)
            V_.tensor_tensor(small(128, 1), v2, v1, ALU.subtract).then_inc(sem("route_r"), 1)
            dve.wait_ge(sem("route_e"), 1)
            wg = small(64, 1)
            link(V_.tensor_reduce(wg, small(80, 4), AX.X, ALU.add))
            dve.wait_ge(sem("route_e"), 2)
            r = small(130, 1)
            den, w1, w2 = small(66, 1), small(68, 1), small(70, 1)
            link(V_.tensor_scalar(den, r, 1.0, None, ALU.add))
            link(V_.tensor_tensor(den, den, wg, ALU.mult))
            link(V_.reciprocal(w1, den))
            link(V_.tensor_tensor(w2, w1, r, ALU.mult))
            link(V_.tensor_tensor(h1, h1, spread(w1), ALU.mult))
            link(V_.tensor_tensor(h2, h2, spread(w2), ALU.mult))
            link(V_.tensor_tensor(h1, h1, h2, ALU.add))
            gates = ms[:, 176:208].rearrange("p (t g e) -> p t g e", t=TT, g=4)
            for t in range(TT):
                link(V_.tensor_tensor(gates[:, t], ghot[:, t, :].unsqueeze(2).to_broadcast([P, 4, 4]),
                                      h1[:, t, :].unsqueeze(1).to_broadcast([P, 4, 4]), ALU.mult))

            V_.nop().then_inc(sem("gates_ready"), 1)

            def side(job):
                kind, g, q = job
                j = side_at[job]
                if kind == "gather":
                    n = gathers_before(g, q)
                    dve.wait_ge(sem("xs_hi"), n + 1)
                    V_.tensor_tensor(win_T[:, g % 2, 1, 4 * q:4 * q + 4, :], XF[:, 4 * q:4 * q + 4, :], win_T[:, g % 2, 0, 4 * q:4 * q + 4, :],
                                     ALU.subtract).then_inc(sem("xs_ready"), 1)
                    return
                dve.wait_ge(side_made, j + 1)
                to_tokens(g, q, PM[:, 3, :]).then_inc(side_read, 1)

            def to_tokens(g, q, src):
                t, half = q // 2, q % 2
                acc = ACC[:, t, half * COL:(half + 1) * COL]
                if g == 0:
                    return V_.tensor_copy(acc, src)
                if g < GROUPS:
                    dve.wait_ge(side_read, side_at["scatter", g - 1, q] + 1)
                return V_.tensor_tensor(acc, acc, src, ALU.add)

            def side_after(e, point):
                if (e, point) in SIDE:
                    side(SIDE[e, point])

            def add_expert(acc_rows, e, window, waits, done):
                gate = SLOT_GATES[:, window, e:e + 1]
                for half in range(2):
                    waits(half)
                    acc = acc_rows[:, half * COL:(half + 1) * COL]
                    if e % PER_GROUP == 0 and window < GROUPS or e == 0:
                        ins = V_.tensor_scalar(acc, PM[:, half, :], gate, None, ALU.mult)
                    else:
                        ins = V_.scalar_tensor_tensor(acc, PM[:, half, :], gate, acc, ALU.mult, ALU.add)
                    done(ins, half)

            dve.wait_ge(sem("windows_turned"), 1)
            link(V_.tensor_copy(PICK_T[:, 0:4, :].rearrange("p (b w) q -> p b (w q)", b=2), PM[:, 0:2, :]))
            link(V_.tensor_copy(PICK_T[:, 4, :], PM[:, 2, 0:SEQ]))
            link(V_.tensor_copy(SLOT_GATES.rearrange("p w e -> p (w e)"), PM[:, 2, SEQ:SEQ + WINDOWS * NEXP]))
            V_.nop().then_inc(sem("windows_read"), 1)
            for e in range(NEXP):
                p = step["exp"] + e
                lo_for("eu", e)
                dve.wait_ge(sem("exp_silu"), e + 1)
                pair_wait(dve, p, 1)
                if e >= 2:
                    dve.wait_ge(sem("hidden_turned"), e - 1)
                V_.tensor_tensor(HROW[:, e % 2, :], SL[:, e % 2, :], bank(p, 1), ALU.mult).then_inc(sem("hidden_rows"), 1)
                dve.wait_ge(sem("hidden_rows"), e + 1)
                V_.nop().then_inc(freed[p % 2], 1)
                side_after(e, "up")
                if e + 1 < NEXP:
                    lo_up_to(after(units_of[index["eg"][e + 1]][1], 4))
                dve.wait_ge(sem("hidden_hi"), e + 1)
                V_.tensor_tensor(hs[:, e % 2, 1, :, :], PM[:, 2, :].rearrange("p (k q) -> p k q", k=4), hs[:, e % 2, 0, :, :],
                                 ALU.subtract).then_inc(sem("hidden"), 1)
                if e + 1 < NEXP:
                    lo_for("eg", e + 1)
                side_after(e, "gate")
                lo_for("ed", e)

                def waits(half):
                    dve.wait_ge(sem("expert_made"), 2 * e + half + 1)
                    if e >= 1:
                        dve.wait_ge(sem("added"), 2 * e + half - 1)

                add_expert(ACCG[:, e // PER_GROUP % 2, :], e, e // PER_GROUP, waits, lambda ins, half: ins.then_inc(sem("added"), 1))
                side_after(e, "down")
            for q in range(4):
                dve.wait_ge(sem("last_sums"), q + 1)
                link(to_tokens(GROUPS - 1, q, PM[:, q, :]))
            dve.wait_ge(sem("crowded_ready"), 1)
            again = dve.value_load(crowded[0:1, 0:1], min_val=0, max_val=1)
            with dve.If(again == 1):
                rest_links = [0]

                def rest_link(ins):
                    rest_links[0] += 1
                    ins.then_inc(sem("rest_chain"), 1)
                    dve.wait_ge(sem("rest_chain"), rest_links[0])

                dve.wait_ge(sem("rest_made"), 1)
                for k in range(KT):
                    ins = V_.tensor_scalar(XO[:, k, :], PG[:, k // 4, (k % 4) * P:(k % 4 + 1) * P],
                                           modT[:, 3, k, 0:1], modT[:, 2, k, 0:1], ALU.mult, ALU.add)
                    if k < KT - 1:
                        rest_link(ins)
                ins.then_inc(sem("rest_cols"), 1)
                for e in range(NEXP):
                    dve.wait_ge(sem("rest_silu"), e + 1)
                    V_.tensor_tensor(HROW[:, 0, :], SL[:, 0, :], PG[:, 1, :], ALU.mult).then_inc(sem("rest_hidden"), 1)
                    dve.wait_ge(sem("rest_turned"), e + 1)
                    V_.tensor_copy(HO, PM[:, 2, :].rearrange("p (k q) -> p k q", k=4)).then_inc(sem("rest_hidden_T"), 1)
                    dve.wait_ge(sem("rest_down"), e + 1)

                    def rest_done(ins, half):
                        if half == 0:
                            rest_link(ins)
                        else:
                            ins.then_inc(sem("rest_added"), 1)
                            dve.wait_ge(sem("rest_added"), e + 1)

                    add_expert(ACCG[:, 0, :], e, WINDOWS - 1, lambda half: None, rest_done)
                dve.wait_ge(sem("rest_sums"), 1)
                for q in range(4):
                    V_.tensor_tensor(ACC[:, q // 2, (q % 2) * COL:(q % 2 + 1) * COL], ACC[:, q // 2, (q % 2) * COL:(q % 2 + 1) * COL],
                                     PG[:, q, :], ALU.add).then_inc(sem("rest_out"), 1)
                dve.wait_ge(sem("rest_out"), 4)
            dve.wait_ge(sem("g2_rows"), 2)
            for t in range(TT):
                link(V_.tensor_tensor(ACC[:, t, :], ACC[:, t, :], G2, ALU.mult))
                V_.tensor_tensor(x[:, t, :], x[:, t, :], ACC[:, t, :], ALU.add).then_inc(sem("x_4"), 1)
            norm_rows("last", x, XN3, False)
            dve.wait_ge(sem("late_in"), 96)
            for t in range(TT):
                V_.tensor_tensor(XN3[:, t, :], XN3[:, t, :], FINAL, ALU.mult).then_inc(sem("out_ready"), 1)


_INS = ["x", "norm_mix_g", "w_in", "w_conv", "w_spatial", "b_spatial", "gmlp_ln_g", "gmlp_ln_b", "fox_q_norm_g",
        "fox_k_norm_g", "fox_forget_b", "w_branch", "w_out", "norm_ffn_g", "w_ffn_in", "w_ffn_out", "c_2", "ctx_2",
        "c_ctx_2", "w_mod_2", "b_mod_2", "norm1_g_2", "norm2_g_2", "w_in_2", "lam_q1_2", "lam_k1_2", "lam_q2_2",
        "lam_k2_2", "subln_g_2", "w_attn_out_2", "w_four_out_2", "w_out_2", "w_router_group_2", "b_router_group_2",
        "w_router_expert_2", "b_router_expert_2", "w_exp_gate_2", "w_exp_up_2", "w_exp_down_2", "final_g_2"]


def kernel(**inputs):
    import numpy as _np
    import concourse.bacc as _bacc
    from concourse.bass_utils import run_bass_kernel_spmd as _run

    nc = _bacc.Bacc("TRN2", target_bir_lowering=False, num_devices=1)
    arrays = {f"in_{n}_dram": _np.ascontiguousarray(inputs[n]) for n in _INS}
    arrays["in_tables_dram"] = TABLES
    a = {n: nc.dram_tensor(f"in_{n}_dram", arrays[f"in_{n}_dram"].shape, F32, kind="ExternalInput").ap()
         for n in [*_INS, "tables"]}
    out = nc.dram_tensor("out_0_dram", (1, SEQ, D), F32, kind="ExternalOutput").ap()
    block_pair_kernel(nc, a, out)
    r = _run(nc, [arrays], core_ids=[0])
    return r.results[0]["out_0_dram"]
```
